# Optimizing a Trainium2 kernel written in Bass

```python
import math
import jax
import jax.numpy as jnp
from jax import lax
import numpy as np

D_MODEL = 1024
BATCH = 1
SEQ = 256
DEPTH = 2

HEAD_DIM = 64
N_HEADS_GDN = 6
N_HEADS_DSW = 6
N_HEADS_SB = 4
D_GDN = N_HEADS_GDN * HEAD_DIM
D_DSW = N_HEADS_DSW * HEAD_DIM
D_SB = N_HEADS_SB * HEAD_DIM
D_MIX = D_GDN + D_DSW + D_SB
CONV_WIDTH = 4
GDN_CHUNK = 64
DSW_CONFIGS = ((128, 1), (512, 4), (2048, 16))
SB_BLOCK = 128
D_FF = 2816
N_EXPERTS = 8
TOP_K = 2
MOE_D_FF = 3584
PLE_DIM = 256
N_DENSE = (DEPTH + 1) // 2
N_MOE = DEPTH // 2
RMS_EPS = 1e-6
IN_SPLITS = (D_GDN,) * 4 + (N_HEADS_GDN,) * 2 + (D_DSW,) * 3 + (D_SB,) * 3
D_IN = 4 * D_GDN + 2 * N_HEADS_GDN + 3 * D_DSW + 3 * D_SB

kernel_name = 'hybrid_gdn_dilated_stickbreaking_moe'

F32 = jnp.float32

def rms_norm(x, w):
    xf = x.astype(F32)
    y = xf * lax.rsqrt(jnp.mean(xf * xf, axis=-1, keepdims=True) + RMS_EPS)
    return (y * w.astype(F32)).astype(x.dtype)

def l2_normalize(x):
    xf = x.astype(F32)
    return xf * lax.rsqrt(jnp.sum(xf * xf, axis=-1, keepdims=True) + RMS_EPS)

def to_heads(t, n_heads):
    b, s, _ = t.shape
    return t.reshape(b, s, n_heads, -1).transpose(0, 2, 1, 3)

def from_heads(t):
    b, h, s, d = t.shape
    return t.transpose(0, 2, 1, 3).reshape(b, s, h * d)

def causal_depthwise_conv(x, w):
    c = x.shape[-1]
    y = lax.conv_general_dilated(
        x, w.astype(x.dtype)[:, None, :], window_strides=(1,),
        padding=[(CONV_WIDTH - 1, 0)], dimension_numbers=('NWC', 'WIO', 'NWC'),
        feature_group_count=c)
    return jax.nn.silu(y)

def gated_delta_rule(q, k, v, g, beta):
    b, h, s, dk = q.shape
    dv = v.shape[-1]
    c = GDN_CHUNK
    n = s // c

    def chunks(t):
        t = t.astype(F32).reshape(b, h, n, c, *t.shape[3:])
        return jnp.moveaxis(t, 2, 0)

    q = chunks(q) * (dk ** -0.5)
    k, v, g, beta = chunks(k), chunks(v), chunks(g), chunks(beta)
    G = jnp.cumsum(g, axis=-1)
    idx = jnp.arange(c)
    causal = idx[:, None] >= idx[None, :]
    strict = idx[:, None] > idx[None, :]
    decay = jnp.exp(jnp.where(causal, G[..., :, None] - G[..., None, :], -jnp.inf))
    kk = jnp.einsum('nbhid,nbhjd->nbhij', k, k)
    tri = jnp.where(strict, beta[..., :, None] * kk * decay, 0.0) + jnp.eye(c, dtype=F32)
    rhs = jnp.concatenate([v * beta[..., None], k * (beta * jnp.exp(G))[..., None]], axis=-1)
    sol = lax.linalg.triangular_solve(tri, rhs, left_side=True, lower=True, unit_diagonal=True)
    u, w = sol[..., :dv], sol[..., dv:]
    qk = jnp.einsum('nbhid,nbhjd->nbhij', q, k) * decay
    q_dec = q * jnp.exp(G)[..., None]
    k_dec = k * jnp.exp(G[..., -1:] - G)[..., None]
    g_tot = jnp.exp(G[..., -1])[..., None, None]

    def step(state, xs):
        u_n, w_n, qk_n, q_n, k_n, gt_n = xs
        v_new = u_n - jnp.einsum('bhcd,bhde->bhce', w_n, state)
        o_n = jnp.einsum('bhcd,bhde->bhce', q_n, state) + jnp.einsum('bhij,bhje->bhie', qk_n, v_new)
        state = state * gt_n + jnp.einsum('bhcd,bhce->bhde', k_n, v_new)
        return state, o_n

    s0 = jnp.zeros((b, h, dk, dv), F32)
    _, o = lax.scan(step, s0, (u, w, qk, q_dec, k_dec, g_tot))
    return jnp.moveaxis(o, 0, 2).reshape(b, h, s, dv)

def gdn_mixer(q, k, v, z, a, bl, conv_w, a_log, dt_bias, norm_w):
    qkv = causal_depthwise_conv(jnp.concatenate([q, k, v], axis=-1), conv_w)
    q, k, v = jnp.split(qkv, 3, axis=-1)
    q = l2_normalize(to_heads(q, N_HEADS_GDN))
    k = l2_normalize(to_heads(k, N_HEADS_GDN))
    v = to_heads(v, N_HEADS_GDN)
    g = -jnp.exp(a_log.astype(F32)) * jax.nn.softplus(a.astype(F32) + dt_bias.astype(F32))
    beta = jax.nn.sigmoid(bl.astype(F32))
    o = gated_delta_rule(q, k, v, g.transpose(0, 2, 1), beta.transpose(0, 2, 1))
    o = from_heads(rms_norm(o, norm_w))
    return (o * jax.nn.silu(z.astype(F32))).astype(z.dtype)

def alibi_slopes(n):
    return 2.0 ** (-8.0 * (jnp.arange(n, dtype=F32) + 1.0) / n)

def dilated_window_attention(q, k, v, slopes, window, dilation):
    b, h, s, d = q.shape
    r = dilation
    span = window // dilation
    blk = span
    L = s // r
    nb = -(-L // blk)
    lp = nb * blk

    def sub(t):
        t = t.reshape(b, h, L, r, d).transpose(0, 1, 3, 2, 4)
        t = jnp.pad(t, ((0, 0), (0, 0), (0, 0), (0, lp - L), (0, 0)))
        return t.reshape(b, h, r, nb, blk, d)

    def with_prev(t):
        prev = jnp.pad(t[:, :, :, :-1], ((0, 0), (0, 0), (0, 0), (1, 0), (0, 0), (0, 0)))
        return jnp.concatenate([prev, t], axis=4)

    qb = sub(q)
    kc, vc = with_prev(sub(k)), with_prev(sub(v))
    scores = jnp.einsum('bhrnqd,bhrnkd->bhrnqk', qb, kc).astype(F32) * (d ** -0.5)
    qi = jnp.arange(blk)[:, None]
    ki = jnp.arange(2 * blk)[None, :]
    dist = qi - ki + blk
    n_idx = jnp.arange(nb)[:, None, None]
    valid = (dist >= 0) & (dist <= span) & (n_idx * blk + ki - blk >= 0)
    bias = -slopes[:, None, None, None, None] * (dist * r).astype(F32)
    scores = jnp.where(valid, scores + bias, -jnp.inf)
    m = jnp.max(scores, axis=-1, keepdims=True)
    e = jnp.exp(scores - m)
    den = jnp.sum(e, axis=-1, keepdims=True)
    o = jnp.einsum('bhrnqk,bhrnkd->bhrnqd', e, vc.astype(F32)) / den
    lse = (m + jnp.log(den))[..., 0]

    def unsub(t):
        t = t.reshape(b, h, r, lp, *t.shape[5:])[:, :, :, :L]
        t = jnp.moveaxis(t, 2, 3)
        return t.reshape(b, h, s, *t.shape[4:])

    return unsub(o), unsub(lse)

def dsw_mixer(q, k, v):
    slopes = alibi_slopes(N_HEADS_DSW)
    outs = []
    lses = []
    for window, dilation in DSW_CONFIGS:
        o_c, lse_c = dilated_window_attention(q, k, v, slopes, window, dilation)
        outs.append(o_c)
        lses.append(lse_c)
    wts = jax.nn.softmax(jnp.stack(lses, axis=0), axis=0)
    return jnp.sum(wts[..., None] * jnp.stack(outs, axis=0), axis=0)

def stick_breaking_attention(q, k, v):
    b, h, s, d = q.shape
    nb = s // SB_BLOCK
    kf = k.astype(F32)
    vf = v.astype(F32)
    qb = jnp.moveaxis(q.astype(F32).reshape(b, h, nb, SB_BLOCK, d), 2, 0) * (d ** -0.5)
    key_pos = jnp.arange(s)

    def block(args):
        q_blk, start = args
        z = jnp.einsum('bhqd,bhkd->bhqk', q_blk, kf)
        t = start + jnp.arange(SB_BLOCK)
        before = key_pos[None, :] < t[:, None]
        log_keep = jnp.where(before, jax.nn.log_sigmoid(-z), 0.0)
        suffix = lax.cumsum(log_keep, axis=3, reverse=True) - log_keep
        a = jnp.where(before, jnp.exp(jax.nn.log_sigmoid(z) + suffix), 0.0)
        return jnp.einsum('bhqk,bhkd->bhqd', a, vf)

    o = lax.map(block, (qb, jnp.arange(nb) * SB_BLOCK))
    return jnp.moveaxis(o, 0, 2).reshape(b, h, s, d)

def token_mixers(hn, w_in, conv_w, a_log, dt_bias, gdn_norm_w, dsw_norm_w, sb_norm_w, w_out):
    proj = hn @ w_in
    cuts = [int(c) for c in np.cumsum(IN_SPLITS)[:-1]]
    (gq, gk, gv, gz, ga, gb, dq, dk, dv, sq, sk, sv) = jnp.split(proj, cuts, axis=-1)
    o_gdn = gdn_mixer(gq, gk, gv, gz, ga, gb, conv_w, a_log, dt_bias, gdn_norm_w)
    o_dsw = dsw_mixer(to_heads(dq, N_HEADS_DSW), to_heads(dk, N_HEADS_DSW), to_heads(dv, N_HEADS_DSW))
    o_dsw = from_heads(rms_norm(o_dsw, dsw_norm_w))
    o_sb = stick_breaking_attention(to_heads(sq, N_HEADS_SB), to_heads(sk, N_HEADS_SB), to_heads(sv, N_HEADS_SB))
    o_sb = from_heads(rms_norm(o_sb, sb_norm_w))
    o = jnp.concatenate([o_gdn.astype(hn.dtype), o_dsw.astype(hn.dtype), o_sb.astype(hn.dtype)], axis=-1)
    return o @ w_out

def swiglu(x, w1, w3, w2):
    return (jax.nn.silu(x @ w1) * (x @ w3)) @ w2

def moe_swiglu(x, router_w, w1, w3, w2):
    logits = (x @ router_w).astype(F32)
    top_val, top_idx = lax.top_k(logits, TOP_K)
    top_w = jax.nn.softmax(top_val, axis=-1)
    gates = jnp.sum(jax.nn.one_hot(top_idx, N_EXPERTS, dtype=F32) * top_w[..., None], axis=-2)
    y = jnp.zeros(x.shape, F32)
    for e in range(N_EXPERTS):
        y = y + gates[..., e:e + 1] * swiglu(x, w1[e], w3[e], w2[e]).astype(F32)
    return y.astype(x.dtype)

def setup_inputs(seed: int = 0) -> dict:
    key = jax.random.key(seed)
    ks = jax.random.split(key, 24)

    def nrm(k, shape, scale):
        return scale * jax.random.normal(k, shape, F32)

    dt = jnp.exp(jax.random.uniform(ks[6], (DEPTH, N_HEADS_GDN), F32, math.log(1e-3), math.log(1e-1)))
    return {
        'x': nrm(ks[0], (BATCH, SEQ, D_MODEL), 1.0),
        'p': nrm(ks[1], (DEPTH, BATCH, SEQ, PLE_DIM), 1.0),
        'attn_norm_w': 1.0 + nrm(ks[2], (DEPTH, D_MODEL), 0.02),
        'w_in': nrm(ks[3], (DEPTH, D_MODEL, D_IN), D_MODEL ** -0.5),
        'conv_w': nrm(ks[4], (DEPTH, CONV_WIDTH, 3 * D_GDN), CONV_WIDTH ** -0.5),
        'a_log': jnp.log(jax.random.uniform(ks[5], (DEPTH, N_HEADS_GDN), F32, 1.0, 16.0)),
        'dt_bias': dt + jnp.log(-jnp.expm1(-dt)),
        'gdn_norm_w': 1.0 + nrm(ks[7], (DEPTH, HEAD_DIM), 0.02),
        'dsw_norm_w': 1.0 + nrm(ks[8], (DEPTH, HEAD_DIM), 0.02),
        'sb_norm_w': 1.0 + nrm(ks[9], (DEPTH, HEAD_DIM), 0.02),
        'w_out': nrm(ks[10], (DEPTH, D_MIX, D_MODEL), D_MIX ** -0.5),
        'ffn_norm_w': 1.0 + nrm(ks[11], (DEPTH, D_MODEL), 0.02),
        'ffn_w1': nrm(ks[12], (N_DENSE, D_MODEL, D_FF), D_MODEL ** -0.5),
        'ffn_w3': nrm(ks[13], (N_DENSE, D_MODEL, D_FF), D_MODEL ** -0.5),
        'ffn_w2': nrm(ks[14], (N_DENSE, D_FF, D_MODEL), D_FF ** -0.5),
        'router_w': nrm(ks[15], (N_MOE, D_MODEL, N_EXPERTS), D_MODEL ** -0.5),
        'moe_w1': nrm(ks[16], (N_MOE, N_EXPERTS, D_MODEL, MOE_D_FF), D_MODEL ** -0.5),
        'moe_w3': nrm(ks[17], (N_MOE, N_EXPERTS, D_MODEL, MOE_D_FF), D_MODEL ** -0.5),
        'moe_w2': nrm(ks[18], (N_MOE, N_EXPERTS, MOE_D_FF, D_MODEL), MOE_D_FF ** -0.5),
        'ple_proj': nrm(ks[19], (DEPTH, PLE_DIM, D_MODEL), PLE_DIM ** -0.5),
        'ple_norm_w': 1.0 + nrm(ks[20], (DEPTH, D_MODEL), 0.02),
        'ple_gate': nrm(ks[21], (DEPTH, D_MODEL, D_MODEL), D_MODEL ** -0.5),
        'final_norm_w': 1.0 + nrm(ks[22], (D_MODEL,), 0.02),
    }

def reference(x, p, attn_norm_w, w_in, conv_w, a_log, dt_bias, gdn_norm_w, dsw_norm_w,
              sb_norm_w, w_out, ffn_norm_w, ffn_w1, ffn_w3, ffn_w2, router_w, moe_w1,
              moe_w3, moe_w2, ple_proj, ple_norm_w, ple_gate, final_norm_w):
    h = x
    for i in range(DEPTH):
        hn = rms_norm(h, attn_norm_w[i])
        h = h + token_mixers(hn, w_in[i], conv_w[i], a_log[i], dt_bias[i], gdn_norm_w[i],
                             dsw_norm_w[i], sb_norm_w[i], w_out[i])
        hn = rms_norm(h, ffn_norm_w[i])
        j = i // 2
        if i % 2 == 0:
            h = h + swiglu(hn, ffn_w1[j], ffn_w3[j], ffn_w2[j])
        else:
            h = h + moe_swiglu(hn, router_w[j], moe_w1[j], moe_w3[j], moe_w2[j])
        gate = jax.nn.sigmoid(rms_norm(h, ple_norm_w[i]) @ ple_gate[i])
        h = h + (p[i] @ ple_proj[i]) * gate
    return rms_norm(h, final_norm_w)


_drawn_inputs = setup_inputs


def setup_inputs(seed=0):
    import zlib

    import numpy as np

    out = dict(_drawn_inputs(seed))
    spreads = {}
    factors = {'gdn_norm_w': 18.714,
     'dsw_norm_w': 8.245,
     'sb_norm_w': 9.881,
     'ple_norm_w': 200.0,
     'final_norm_w': 22.621,
     'ffn_norm_w': 4.719}
    for name, (base, spread) in spreads.items():
        noise = np.random.default_rng([zlib.crc32(name.encode()), seed]).standard_normal(out[name].shape)
        drawn = base * np.exp(spread * noise) if base else spread * noise
        out[name] = jnp.asarray(drawn.astype(out[name].dtype))
    for name, factor in factors.items():
        out[name] = (out[name] * factor).astype(out[name].dtype)
    return out
```

```python
from contextlib import ExitStack

import numpy as np

import concourse.bass as bass
from concourse import mybir

ALU = mybir.AluOpType
ACT = mybir.ActivationFunctionType
F32 = mybir.dt.float32
I32 = mybir.dt.int32
AX_X = mybir.AxisListType.X

P = 128
T, D = 256, 1024
NB = T // P
KC = D // P
DEPTH = 2
HD = 64
HG, HW, HS = 6, 6, 4
DG, DW, DS = HG * HD, HW * HD, HS * HD
CONV = 4
FF = 2816
NF = FF // P
NE, TOPK, MFF = 8, 2, 3584
NJ = MFF // 512
PLE = 256
EPS = 1e-6
SCALE = HD ** -0.5
SLOPES = [2.0 ** (-8.0 * (i + 1.0) / HW) for i in range(HW)]
WINDOWS = ((128, 1), (512, 4), (2048, 16))
FAR = -1e30
MORE = T * TOPK // (P + 1)
NI = NE + MORE + 1
NSLOT = 7
SLOT = 4096
NG = -(-NF // 4)
GS, GW = 4, 384
NLEV = 7
CQ = 9
CA = 10


class Count:

    def __init__(self, sem):
        self.sem, self.k, self.items = sem, 0, None

    def up(self):
        self.k += 1
        return 1

    @property
    def n(self):
        return self.k if self.items is None else self.items + self.k


class Tiles:

    def __init__(self):
        self.at, self.filled, self.drained, self.last = {}, 0, {"v": 0, "a": 0}, {}

    def add(self, key, bank, who):
        self.filled += 1
        for w in who:
            self.drained[w] += 1
        self.at[key] = dict(bank=bank, filled=self.filled, before=self.last.get(bank),
                            drained={w: self.drained[w] for w in who}, item=False, back=0)
        self.last[bank] = self.at[key]


def system_at(k, b):
    n = GW * (2 * (k % 2) + b) + P * (k // 2)
    return slice(n, n + P)


def group_heads(g):
    return [(2 * q + g // 2, g % 2, P * q) for q in range(3)]


def norm_tiles(t, occ):
    for c in range(4):
        t.add(("T", occ, c), c, "va"[c % 2])


def mixer_tiles(t, L):
    n = [0]

    def add(key, who):
        t.add(key, n[0] % 8, who)
        n[0] += 1

    norm_tiles(t, 3 * L)
    for b in range(NB):
        add(("J", L, b, 0), "a")
    for c in range(10):
        add(("I", L, c), "va"[c % 2])
    for g in (1, 2):
        for b in range(NB):
            add(("J", L, b, g), "a")
    add(("G", L), "v")
    for g in range(GS):
        add(("R", L, g), "v")
    for c in range(3):
        add(("N2", L, c), "a")
    for c in range(3):
        add(("V", L, c), "aav"[c])
    for kind in ("KK", "QK", "C0"):
        for g in range(GS):
            add((kind, L, g), "v")
    for lev in range(1, NLEV):
        for g in range(GS):
            add(("P", L, lev, g), "a")
        for g in range(GS):
            if lev < NLEV - 1:
                add(("X", L, lev, g), "v")
            add(("Y", L, lev, g), "v")
    for key, who in (("W0", "v"), ("S", "a"), ("KS0", "v"), ("KS1", "v"), ("QS0", "a"), ("QS1", "a"), ("W1", "v"), ("O0", "a"),
                     ("O1", "v")):
        add((key, L), who)
    for kind, who, heads in (("D", "v", HW), ("E", "a", HW), ("F", "v", HW), ("Z", "a", HS), ("CS", "v", HS)):
        for k in range(heads):
            add((kind, L, k), who)
    add(("U", L), "a")
    for c in range(4):
        add(("OT", L, c), "va"[c % 2])
    for b in range(NB):
        for m in range(2):
            add(("WO", L, b, m), "v")


def ple_tiles(t, L):
    for b in range(NB):
        for m in range(2):
            t.add(("PG", L, b, m), 4 + m, "a")
            t.add(("PP", L, b, m), 6 + m, "v")


def gather_tiles(t, when):
    t.add(("GA", when, 0), 6, "v")
    t.add(("GA", when, 1), 7, "a")


def item_tiles(t):
    for j in range(NJ):
        t.add(("A", j), 2 * (j % 2), "a")
        if j:
            t.add(("TT", j - 1), 6 + (j - 1) % 2, "a")
        t.add(("B", j), 2 * (j % 2) + 1, "v")
    gather_tiles(t, "next")
    t.add(("TT", NJ - 1), 6 + (NJ - 1) % 2, "a")
    for m in range(2):
        t.add(("YY", m), 4 + m, "a")
    for m in range(2):
        for b in range(NB):
            t.add(("SC", b, m), 2 * b + m, "v")
    t.add(("GT", "next"), 6, "a")


def plan_tiles():
    t = Tiles()
    mixer_tiles(t, 0)
    norm_tiles(t, 1)
    for f in range(NF):
        t.add(("H", f), f % 4, "av")
    for b in range(NB):
        for m in range(2):
            t.add(("Y2", b, m), 4 + 2 * b + m, "v")
    norm_tiles(t, 2)
    ple_tiles(t, 0)
    mixer_tiles(t, 1)
    norm_tiles(t, 4)
    t.add(("LG",), 4, "v")
    t.add(("POS",), 5, "v")
    gather_tiles(t, "first")
    t.add(("GT", "first"), 6, "a")
    filled, drained, known = t.filled, dict(t.drained), set(t.at)
    item_tiles(t)
    per_fill = t.filled - filled
    per_drain = {w: t.drained[w] - drained[w] for w in "va"}
    ahead = [t.at[k] for k in known]
    for key in t.at:
        if key not in known:
            t.at[key]["item"] = True
            if any(t.at[key]["before"] is a for a in ahead):
                t.at[key]["before"], t.at[key]["back"] = t.last[t.at[key]["bank"]], 1
    t.filled, t.drained, t.last = filled, dict(drained), {}
    t.base = drained
    norm_tiles(t, 5)
    ple_tiles(t, 1)
    return t, per_fill, per_drain


def plan_loads():
    order, release = [], {}

    def add(key, *until):
        order.append(key)
        release[key] = until

    for L in range(DEPTH):
        add(("J", L, 0), "tile", ("J", L, 1, 0))
        for c in range(5):
            add(("I", L, c), "tile", ("I", L, 2 * c + 1))
        for g in (1, 2):
            add(("J", L, g), "tile", ("J", L, 1, g))
        for m in range(2):
            add(("WO", L, m), "tile", ("WO", L, 1, m))
        if L == 0:
            for j in range(NG):
                last = min(4 * j + 4, NF) - 1
                add(("w1", j), "tile", ("H", last))
                add(("w3", j), "tile", ("H", last))
                if j < NG - 1:
                    add(("w2", j), "down", j + 1)
                else:
                    add(("w2", j), "tile", ("Y2", 1, 1))
            add(("PP", 0), "tile", ("PP", 0, 1, 1))
            for m in range(2):
                add(("PG", 0, m), "tile", ("PG", 0, 1, m))
    static = len(order)
    for j in range(NJ):
        add(("A", j), "tile", ("A", j))
        add(("B", j), "tile", ("B", j))
        if j:
            add(("C", j - 1), "down", NG - 1 + j)
    add(("C", NJ - 1), "tile", ("YY", 1))
    per = len(order) - static
    tail = [("PP", 1), ("PG", 1, 0), ("PG", 1, 1)]
    return order, release, static, per, tail


CONSTS = {}
_at = 0
for _name, _w in (("ident", P), ("ones", P), ("upto", P), ("before", P), ("from", P), ("headsum", P), ("slots", P),
                  ("levels", NLEV * P), ("dist", 384), ("mult", 384), ("earlier", 384), ("lower8", NE * NE),
                  ("expert", NE), ("item", MORE + 1), ("eps", 1)):
    CONSTS[_name] = (_at, _w)
    _at += _w
NCONST = _at


def shape_constants():
    c = np.zeros((P, NCONST), np.float32)
    i = np.arange(P)

    def put(name, value):
        a, w = CONSTS[name]
        c[:, a:a + w] = np.asarray(value, np.float32).reshape(-1, w)

    put("ident", np.eye(P))
    put("ones", np.ones((P, P)))
    put("upto", i[:, None] <= i[None, :])
    put("before", i[:, None] < i[None, :])
    put("from", i[:, None] >= i[None, :])
    put("headsum", i[:, None] // HD == i[None, :] // HD)
    put("slots", np.tile(i, (P, 1)))
    lev = []
    for s in range(NLEV):
        w = 1 << s
        same = i[:, None] // (2 * w) == i[None, :] // (2 * w)
        lev.append(same & (i[:, None] // w % 2 == 0) & (i[None, :] // w % 2 == 1))
    put("levels", np.concatenate(lev, 1))
    q = np.concatenate([i[:, None] - i[None, :], P + i[:, None] - np.arange(T)[None, :]], 1)
    m = sum((q >= 0) & (q <= window) & (q % r == 0) for window, r in WINDOWS)
    put("dist", np.where(m > 0, -q, FAR))
    put("mult", m)
    b = i[:, None] < i[None, :]
    put("earlier", np.concatenate([b, np.ones((P, P)), b], 1))
    put("lower8", np.tile((np.arange(NE)[None, :] < np.arange(NE)[:, None]).reshape(1, -1), (P, 1)))
    put("expert", np.tile(np.arange(NE), (P, 1)))
    put("item", np.tile(np.arange(MORE + 1), (P, 1)))
    put("eps", np.full((P, 1), EPS))
    return c


COL_NORM = lambda occ: occ * KC
COL_CONV = 3 * DEPTH * KC
COL_ROUTER = COL_CONV + DEPTH * CQ * CONV
NCOL = COL_ROUTER + KC * NE
ROW_ALOG, ROW_DT = 0, DEPTH * HG
ROW_HN = lambda L, i: 2 * DEPTH * HG + (L * 3 + i) * HD
NROW = 2 * DEPTH * HG + DEPTH * 3 * HD


def build(nc, x, stream, experts, columns, rows, final_w, consts, out):
    tiles, per_fill, per_drain = plan_tiles()
    load_order, release, n_static, per_load, tail_loads = plan_loads()
    load_at = {key: n for n, key in enumerate(load_order)}
    load_at.update({key: n_static + k for k, key in enumerate(tail_loads)})
    assert per_load % NSLOT == 0
    laps = per_load // NSLOT

    with ExitStack() as ctx:
        def sb(name, shape, dt=F32):
            return ctx.enter_context(nc.sbuf_tensor(name, shape, dt))

        def sem(name):
            return ctx.enter_context(nc.semaphore(name))

        ps = ctx.enter_context(nc.psum_tensor("ps", [P, 8, 512], F32))
        ring = sb("ring", [P, NSLOT, SLOT])
        cst = sb("cst", [P, NCONST])
        cols = sb("cols", [P, NCOL])
        rws = sb("rws", [P, NROW])
        h = sb("h", [P, NB, D])
        hn = sb("hn", [P, NB, D])
        hnT = sb("hnT", [P, KC, T])
        table = sb("table", [1, 8], I32)

        sizes = dict(xc=CQ * (T + 3) + 1, qkv=CQ * T, att=CA * T, z=NB * DG, dva=NB * HW * (HD + 1), sva=NB * DS,
                     kd=DG, dec=1536, mt=1536, xt=1536, ab=24, em=30, lnp=12, beta=12, g=12, gc=18, xa=12,
                     e1=24, gx=12, eg=12, ss=64, rs=68, mx=12, nm=12, rden=12)
        off, place = 0, {}
        for k, w in sizes.items():
            place[k] = (off, w)
            off += w
        work = sb("work", [P, off])

        def area(name, start=0, width=None):
            a, w = place[name]
            return work[:, a + start:a + start + (w - start if width is None else width)]

        def cc(name, start=0, width=None):
            a, w = CONSTS[name]
            return cst[:, a + start:a + start + (w - start if width is None else width)]

        def col(n):
            return cols[:, n:n + 1]

        ident, ones = cc("ident"), cc("ones")

        xc = area("xc", 0, CQ * (T + 3)).rearrange("p (c t) -> p c t", c=CQ)
        qkv = area("qkv").rearrange("p (c t) -> p c t", c=CQ)
        att = area("att").rearrange("p (c t) -> p c t", c=CA)
        zt = area("z").rearrange("p (b c) -> p b c", b=NB)
        dva = area("dva").rearrange("p (b h e) -> p b h e", b=NB, h=HW)
        sva = area("sva").rearrange("p (b c) -> p b c", b=NB)
        ab = area("ab").rearrange("p (b c) -> p b c", b=NB)
        squares = area("xc", 0, 1536)
        pbuf = area("xc", 0, 1536)
        vt = area("xc", 1536, NB * DG).rearrange("p (b c) -> p b c", b=NB)
        kd, dec, mt, xt = area("kd"), area("dec"), area("mt"), area("xt")
        hnT_flat = hnT[:, :, :].rearrange("p k t -> p (k t)")
        hn_flat = hn[:, :, :].rearrange("p b c -> p (b c)")
        xi = hnT_flat[:, 0:1536]
        cm = hn_flat[:, 0:1536]
        vn = area("mt", 0, NB * DG).rearrange("p (b c) -> p b c", b=NB)
        s1 = area("mt", 768, 192)
        rr = area("mt", 960, DG)
        qs = area("xc", 0, DG)
        o = hn
        a0 = place["dec"][0]
        prob = work[:, a0:a0 + HW * 384].rearrange("p (h s) -> p h s", h=HW)
        probT = work[:, a0 + HW * 384:a0 + 2 * HW * 384].rearrange("p (h s) -> p h s", h=HW)
        zs = hnT_flat[:, 0:HS * 384].rearrange("p (h s) -> p h s", h=HS)
        es = area("xc", 0, HS * 384).rearrange("p (h s) -> p h s", h=HS)
        sps = area("qkv", 0, HS * 384).rearrange("p (h s) -> p h s", h=HS)
        osq = area("qkv", 0, NB * D)

        def part(start, width):
            return work[:, start:start + width]

        ffs = [part(256 * i, 256) for i in range(2)]
        ffg = [part(512 + 256 * i, 256) for i in range(4)]
        sig = [part(512 * i, 512) for i in range(2)]
        sgp = [part(1024 + 512 * i, 512) for i in range(2)]
        ms = [part(512 * i, 512) for i in range(2)]
        mg = [part(1024 + 512 * i, 512) for i in range(2)]
        mT = [part(2048 + 512 * i, 512) for i in range(2)]
        xg = part(3072, 1024).rearrange("p (k t) -> p k t", k=KC)
        pick = part(4096, 256).rearrange("p (b s) -> p b s", b=NB)
        pickg = part(4352, 256).rearrange("p (b s) -> p b s", b=NB)
        back = part(4608, 256)
        ysb = part(4864, 1024)
        R0 = 5888
        lg = part(R0, 16).rearrange("p (b e) -> p b e", b=NB)
        top = part(R0 + 16, 2)
        den = part(R0 + 18, 2)
        over = part(R0 + 20, 8)
        oidx = part(R0 + 28, 8)
        rank = part(R0 + 36, 16).rearrange("p (b e) -> p b e", b=NB)
        sel = part(R0 + 52, 16).rearrange("p (b e) -> p b e", b=NB)
        gate = part(R0 + 68, 16).rearrange("p (b e) -> p b e", b=NB)
        exl = part(R0 + 84, 16).rearrange("p (b e) -> p b e", b=NB)
        cum = part(R0 + 100, 24)
        pos1 = part(R0 + 124, 16).rearrange("p (b e) -> p b e", b=NB)
        tabf = part(R0 + 140, 8)
        posi = part(R0 + 148, NB * NI).rearrange("p (b i) -> p b i", b=NB)
        gati = part(R0 + 148 + NB * NI, NB * NI).rearrange("p (b i) -> p b i", b=NB)
        pairs = [part(R0 + 200 + 128 * i, 128).rearrange("p (b e f) -> p b e f", b=NB, e=NE) for i in range(2)]
        osel = part(R0 + 456, (MORE + 1) * NE).rearrange("p (r e) -> p r e", e=NE)
        oprd = part(R0 + 456 + 32, 5 * (MORE + 1) * NE).rearrange("p (a r e) -> p a r e", a=5, e=NE)
        assert R0 + 456 + 192 <= place["z"][0]
        f0 = place["dec"][0]
        finw = part(f0, D)
        res = part(f0 + D, NB * D).rearrange("p (b c) -> p b c", b=NB)

        s_in = sem("inputs_landed")
        s_fw = sem("final_weight_landed")
        s_land = [sem(f"weights_landed_{i}") for i in range(NSLOT)]
        s_fill = sem("psum_filled")
        s_down = sem("down_weights_used")
        s_free = {"v": sem("psum_drained_by_vector"), "a": sem("psum_drained_by_scalar")}
        s_out = sem("output_written")
        s_vstep, s_astep, s_pstep = sem("vector_step"), sem("scalar_step"), sem("gpsimd_step")
        s_sumsq, s_rstd = sem("row_squares_summed"), sem("row_rstd_ready")
        s_hn = {"v": sem("hn_block1_ready"), "a": sem("hn_block0_ready")}
        s_gin, s_gexp = sem("gate_arguments_ready"), sem("gate_exponentials_ready")
        s_gadd, s_gln, s_g = sem("exponentials_plus_one"), sem("softplus_logs_ready"), sem("gates_ready")
        s_gx, s_eg = sem("summed_gate_arguments_ready"), sem("summed_gate_exponentials_ready")
        s_dexp, s_dec = sem("decays_ready"), sem("decays_masked")
        s_conv, s_silu = sem("convolved"), sem("convolved_silu_ready")
        s_sq, s_qk = sem("qk_squares_ready"), sem("qk_normalised")
        s_cm, s_rr = sem("level_blocks_ready"), sem("chunk1_right_side_ready")
        s_qs = sem("q_state_decayed")
        s_nm, s_dex, s_dpr = sem("window_max_ready"), sem("window_exponentials_ready"), sem("window_weights_ready")
        s_zl, s_sps = sem("stick_logs_ready"), sem("stick_softplus_ready")
        s_ze, s_aT = sem("stick_exponentials_ready"), sem("stick_weights_ready")
        s_zg, s_oss, s_ors, s_o = sem("silu_z_ready"), sem("head_squares_summed"), sem("head_rstd"), sem("mixed_ready")
        s_ple = sem("ple_added")
        s_lsub, s_lex = sem("router_logits_shifted"), sem("router_exponentials_ready")
        s_sel, s_tab, s_pick = sem("experts_selected"), sem("item_table_ready"), sem("item_selection_ready")
        s_res = sem("result_ready")

        def bank(key, start=0, width=512):
            return ps[:, tiles.at[key]["bank"], start:start + width]

        def through(count, it, per):
            return count if it is None else it * per + count

        def filled(eng, key, it=None, back=0):
            eng.wait_ge(s_fill, through(tiles.at[key]["filled"] - back * per_fill, it, per_fill))

        def drained(eng, key, who, it=None, back=0):
            eng.wait_ge(s_free[who], through(tiles.at[key]["drained"][who] - back * per_drain[who], it, per_drain[who]))

        def weights(key, part_of=None):
            return ring[:, load_at[key] % NSLOT, :]

        def landed(eng, key, it=None):
            eng.wait_ge(s_land[load_at[key] % NSLOT], through(16 * (load_at[key] // NSLOT + 1), it, 16 * laps))

        ITEM_END = {"v": tiles.base["v"], "a": tiles.base["a"]}
        block = ctx.enter_context(nc.Block())

        @block.sync
        def _(sp):
            sp.dma_start(h[:, :, :], x.rearrange("(b p) c -> p b c", p=P)).then_inc(s_in, 16)
            sp.dma_start(cst[:, :], consts).then_inc(s_in, 16)
            sp.dma_start(cols[:, :], columns).then_inc(s_in, 16)
            sp.dma_start(rws[:, :], rows).then_inc(s_in, 16)

            def used(key, it=None, back=0):
                kind, what = release[key]
                if kind == "tile":
                    filled(sp, what, it, back)
                else:
                    sp.wait_ge(s_down, through(what - back * (NJ - 1), it, NJ - 1))

            for n in range(n_static):
                if n >= NSLOT:
                    used(load_order[n - NSLOT])
                sp.dma_start(ring[:, n % NSLOT, :], stream[n]).then_inc(s_land[n % NSLOT], 16)

            def expert_loads(e, i):
                for k in range(per_load):
                    if k >= NSLOT:
                        used(load_order[n_static + k - NSLOT], i)
                    elif i is None:
                        used(load_order[n_static + k - NSLOT])
                    else:
                        used(load_order[n_static + k - NSLOT + per_load], i, 1)
                    src = experts[k] if i is None else experts[bass.ds(e * per_load + k, 1), :, :]
                    slot = (n_static + k) % NSLOT
                    if i is not None:
                        src = src.rearrange("a p f -> (a p) f")
                    sp.dma_start(ring[:, slot, :], src).then_inc(s_land[slot], 16)

            expert_loads(0, None)
            with sp.Fori(1, NE) as e:
                expert_loads(e, e)
            sp.wait_ge(s_tab, 1)
            more = sp.value_load(table[0:1, MORE + 1:MORE + 2], min_val=0, max_val=MORE)
            with sp.If(more > 0):
                with sp.Fori(0, more) as r:
                    e = sp.value_load(table[0:1, bass.ds(r, 1)], min_val=0, max_val=NE - 1)
                    expert_loads(e, r + NE)
            for k in range(len(tail_loads)):
                n = n_static + k
                used(load_order[n - NSLOT + per_load], more + NE, 1)
                sp.dma_start(ring[:, n % NSLOT, :], stream[n]).then_inc(s_land[n % NSLOT], 16)
            filled(sp, ("WO", 1, 1, 1))
            sp.dma_start(finw, final_w).then_inc(s_fw, 16)
            sp.wait_ge(s_res, NB)
            sp.dma_start(out.rearrange("(b p) c -> p b c", p=P), res).then_inc(s_out, 16)
            sp.wait_ge(s_out, 16)

        @block.gpsimd
        def _(pool):
            st = Count(s_pstep)

            def rstd(occ):
                pool.wait_ge(s_sumsq, NB * (occ + 1))
                nc.gpsimd.tensor_scalar(area("rs", 66, 2), area("rs", 64, 2), 1.0 / D, EPS, ALU.mult,
                                        ALU.add).then_inc(st.sem, st.up())
                pool.wait_ge(st.sem, st.n)
                nc.gpsimd.tensor_tensor(area("mx", 10, 2), area("rs", 66, 2), area("rs", 32, 2), ALU.pow).then_inc(s_rstd, 1)

            def mixers(L):
                rstd(3 * L)
                for g in range(GS):
                    pool.wait_ge(s_dexp, GS * L + g + 1)
                    d = dec[:, GW * g:GW * g + GW].rearrange("p (s i) -> p s i", s=3)
                    nc.gpsimd.tensor_tensor(d, d, cc("upto").unsqueeze(1).broadcast_to([P, 3, P]),
                                            ALU.mult).then_inc(s_dec, 1)
                for lev in range(NLEV):
                    for g in range(GS):
                        if lev == 0:
                            drained(pool, ("KK", L, g), "v")
                        elif lev == 1:
                            drained(pool, ("C0", L, g), "v")
                        else:
                            filled(pool, ("P", L, lev - 1, g))
                        m = cc("levels", lev * P, P).unsqueeze(1).broadcast_to([P, 3, P])
                        nc.gpsimd.tensor_tensor(cm[:, GW * g:GW * g + GW].rearrange("p (s i) -> p s i", s=3),
                                                mt[:, GW * g:GW * g + GW].rearrange("p (s i) -> p s i", s=3),
                                                m, ALU.mult).then_inc(s_cm, 1)
                pool.wait_ge(s_oss, L + 1)
                nc.gpsimd.tensor_scalar(area("ss", 32, 32), area("ss", 0, 32), 1.0 / HD, EPS, ALU.mult,
                                        ALU.add).then_inc(st.sem, st.up())
                pool.wait_ge(st.sem, st.n)
                nc.gpsimd.tensor_tensor(area("rs", 0, 32), area("ss", 32, 32), area("rs", 32, 32),
                                        ALU.pow).then_inc(s_ors, 1)

            nc.gpsimd.memset(area("rs", 32, 32), -0.5).then_inc(st.sem, st.up())
            pool.wait_ge(st.sem, st.n)
            pool.wait_ge(s_in, 64)
            mixers(0)
            rstd(1)
            rstd(2)
            mixers(1)
            rstd(4)
            rstd(5)
            rstd(6)

        def residual_ready(eng, occ, items):
            if occ in (1, 4):
                drained(eng, ("WO", occ // 3, 1, 1), "v")
            elif occ == 2:
                drained(eng, ("Y2", 1, 1), "v")
            elif occ == 5:
                drained(eng, ("SC", 1, 1), "v", items, 1)
            elif occ in (3, 6):
                eng.wait_ge(s_ple, 4 * (occ // 3))

        @block.scalar
        def _(act):
            st = Count(s_astep)

            def norm(occ, items=None):
                if occ == 0:
                    act.wait_ge(s_in, 64)
                else:
                    residual_ready(act, occ, items)
                for b in range(NB):
                    nc.scalar.activation(hn[:, b, :], h[:, b, :], ACT.Square,
                                         accum_out=area("rs", 64 + b, 1)).then_inc(s_sumsq, 1)
                if occ == 6:
                    return
                act.wait_ge(s_rstd, occ + 1)
                nc.scalar.activation(hn[:, 0, :], h[:, 0, :], ACT.Copy,
                                     scale=area("mx", 10, 1)).then_inc(s_hn["a"], 1)
                for c in (1, 3):
                    key = ("T", occ, c)
                    filled(act, key, items)
                    nc.scalar.activation(hnT[:, 2 * c, :], bank(key, 0, T), ACT.Copy,
                                         scale=col(COL_NORM(occ) + 2 * c))
                    nc.scalar.activation(hnT[:, 2 * c + 1, :], bank(key, T, T), ACT.Copy,
                                         scale=col(COL_NORM(occ) + 2 * c + 1)).then_inc(s_free["a"], 1)

            def token_major(L, g):
                for b in range(NB):
                    key = ("J", L, b, g)
                    filled(act, key)
                    if g == 0:
                        nc.scalar.copy(zt[:, b, :], bank(key, 0, DG))
                        ins = nc.scalar.copy(ab[:, b, :], bank(key, DG, 2 * HG))
                    elif g == 1:
                        ins = nc.scalar.copy(dva[:, b, :, 0:HD], bank(key, 0, DW).rearrange("p (h e) -> p h e", h=HW))
                    else:
                        ins = nc.scalar.copy(sva[:, b, :], bank(key, 0, DS))
                    ins.then_inc(s_free["a"], 1)

            def mixers(L):
                norm(3 * L)
                token_major(L, 0)
                for t in range(1, 10, 2):
                    filled(act, ("I", L, t))
                    for c in (2 * t, 2 * t + 1):
                        if c < CQ + CA:
                            dst = xc[:, c, 3:3 + T] if c < CQ else att[:, c - CQ, :]
                            ins = nc.scalar.copy(dst, bank(("I", L, t), T * (c % 2), T))
                    ins.then_inc(s_free["a"], 1)
                token_major(L, 1)
                token_major(L, 2)
                act.wait_ge(s_gin, L + 1)
                nc.scalar.activation(area("em"), area("em"), ACT.Exp).then_inc(s_gexp, 1)
                act.wait_ge(s_gadd, L + 1)
                nc.scalar.activation(area("lnp"), area("e1", 0, 12), ACT.Ln).then_inc(s_gln, 1)
                act.wait_ge(s_gx, L + 1)
                nc.scalar.activation(area("eg"), area("gx"), ACT.Exp).then_inc(s_eg, 1)
                for g in range(GS):
                    drained(act, ("R", L, g), "v")
                    d = dec[:, GW * g:GW * g + GW]
                    nc.scalar.activation(d, d, ACT.Exp).then_inc(s_dexp, 1)
                for j in range(3):
                    act.wait_ge(s_conv, CQ * L + 3 * j + 3)
                    v = qkv[:, 3 * j:3 * j + 3, :]
                    nc.scalar.activation(v, v, ACT.Silu).then_inc(s_silu, 1)
                drained(act, ("J", L, 1, 0), "a")
                nc.scalar.activation(area("z"), area("z"), ACT.Silu).then_inc(s_zg, 1)
                for c in range(3):
                    filled(act, ("N2", L, c))
                    nc.scalar.activation(pbuf[:, 512 * c:512 * c + 512], bank(("N2", L, c)), ACT.Sqrt,
                                         bias=cc("eps")).then_inc(s_free["a"], 1)
                for b in range(NB):
                    filled(act, ("V", L, b))
                    nc.scalar.copy(vt[:, b, :], bank(("V", L, b), 0, DG)).then_inc(s_free["a"], 1)
                for lev in range(1, NLEV):
                    for g in range(GS):
                        filled(act, ("P", L, lev, g))
                        if lev == 1:
                            act.wait_ge(s_qk, 3 * L + 3)
                        else:
                            filled(act, ("Y", L, lev - 1, g))
                        nc.scalar.copy(pbuf[:, GW * g:GW * g + GW],
                                       bank(("P", L, lev, g), 0, GW)).then_inc(s_free["a"], 1)
                filled(act, ("S", L))
                nc.scalar.copy(s1, bank(("S", L), 0, 192)).then_inc(s_free["a"], 1)
                for parity in range(2):
                    key = (f"QS{parity}", L)
                    filled(act, key)
                    for k in range(parity, HG, 2):
                        ins = nc.scalar.activation(qs[:, k * HD:k * HD + HD], bank(key, k // 2 * HD, HD), ACT.Copy,
                                                   scale=area("eg", k, 1))
                    ins.then_inc(s_free["a"], 1)
                filled(act, ("O0", L))
                nc.scalar.copy(o[:, 0, 0:DG], bank(("O0", L), 0, DG)).then_inc(s_free["a"], 1)
                for k in range(HW):
                    act.wait_ge(s_nm, HW * L + k + 1)
                    for b in range(NB):
                        v = prob[:, k, 0:P] if b == 0 else prob[:, k, P:384]
                        ins = nc.scalar.activation(v, v, ACT.Exp, scale=SCALE, bias=area("nm", 2 * k + b, 1))
                    ins.then_inc(s_dex, 1)
                for k in range(HW):
                    filled(act, ("E", L, k))
                    nc.scalar.copy(probT[:, k, :], bank(("E", L, k), 0, 384)).then_inc(s_free["a"], 1)
                drained(act, ("O1", L), "v")
                for k in range(HS):
                    filled(act, ("Z", L, k))
                    nc.scalar.mul(zs[:, k, :], bank(("Z", L, k), 0, 384), SCALE).then_inc(s_free["a"], 1)
                drained(act, ("Z", L, HS - 1), "a")
                nc.scalar.activation(es, zs, ACT.Abs).then_inc(st.sem, st.up())
                act.wait_ge(st.sem, st.n)
                nc.scalar.activation(es, es, ACT.Exp, scale=-1.0).then_inc(st.sem, st.up())
                act.wait_ge(st.sem, st.n)
                nc.scalar.activation(es, es, ACT.Ln, bias=1.0).then_inc(s_zl, 1)
                for k in range(HS):
                    drained(act, ("CS", L, k), "v")
                    nc.scalar.activation(zs[:, k, :], zs[:, k, :], ACT.Exp).then_inc(s_ze, 1)
                filled(act, ("U", L))
                nc.scalar.copy(o[:, :, DG + DW:D],
                               bank(("U", L)).rearrange("p (b c) -> p b c", b=NB)).then_inc(s_free["a"], 1)
                for c in (1, 3):
                    filled(act, ("OT", L, c))
                    nc.scalar.copy(hnT_flat[:, 512 * c:512 * c + 512], bank(("OT", L, c))).then_inc(s_free["a"], 1)

            def ple(L, items=None):
                for n in range(4):
                    key = ("PG", L, n // 2, n % 2)
                    filled(act, key, items)
                    if n >= 2:
                        drained(act, ("PP", L, (n - 2) // 2, n % 2), "v", items)
                    nc.scalar.activation(sig[n % 2], bank(key), ACT.Sigmoid).then_inc(s_free["a"], 1)

            mixers(0)
            norm(1)
            for f in range(NF):
                filled(act, ("H", f))
                if f >= 2:
                    drained(act, ("H", f - 2), "v")
                nc.scalar.activation(ffs[f % 2], bank(("H", f), 0, T), ACT.Silu).then_inc(s_free["a"], 1)
            norm(2)
            ple(0)
            mixers(1)
            norm(4)
            act.wait_ge(s_lsub, 1)
            nc.scalar.activation(exl, exl, ACT.Exp).then_inc(s_lex, 1)

            def gathered(when, it):
                filled(act, ("GA", when, 1), it)
                for k in range(4, 8):
                    ins = nc.scalar.activation(xg[:, k, :], bank(("GA", when, 1), P * (k - 4), P), ACT.Copy,
                                               scale=col(COL_NORM(4) + k))
                ins.then_inc(s_free["a"], 1)

            def scatter_matrix(when, it):
                filled(act, ("GT", when), it)
                nc.scalar.copy(back, bank(("GT", when), 0, T)).then_inc(s_free["a"], 1)

            gathered("first", None)
            scatter_matrix("first", None)
            act.wait_ge(s_tab, 1)
            items = act.value_load(table[0:1, MORE + 2:MORE + 3], min_val=NE, max_val=NE + MORE)
            with act.Fori(0, items) as i:
                def turned(j):
                    filled(act, ("TT", j), i)
                    nc.scalar.copy(mT[j % 2], bank(("TT", j))).then_inc(s_free["a"], 1)

                for j in range(NJ):
                    filled(act, ("A", j), i)
                    drained(act, ("B", (j - 2) % NJ), "v", i, 1 if j < 2 else 0)
                    nc.scalar.activation(ms[j % 2], bank(("A", j)), ACT.Silu).then_inc(s_free["a"], 1)
                    if j:
                        turned(j - 1)
                gathered("next", i)
                turned(NJ - 1)
                for m in range(2):
                    filled(act, ("YY", m), i)
                    nc.scalar.copy(ysb[:, 512 * m:512 * m + 512], bank(("YY", m))).then_inc(s_free["a"], 1)
                scatter_matrix("next", i)
            norm(5, items)
            ple(1, items)
            norm(6)

        @block.vector
        def _(dve):
            st = Count(s_vstep)

            def step():
                dve.wait_ge(st.sem, st.n)

            def norm(occ, items=None):
                dve.wait_ge(s_rstd, occ + 1)
                nc.vector.tensor_scalar(hn[:, 1, :], h[:, 1, :], area("mx", 11, 1), None, ALU.mult).then_inc(s_hn["v"], 1)
                for c in (0, 2):
                    key = ("T", occ, c)
                    filled(dve, key, items)
                    nc.vector.tensor_scalar(hnT[:, 2 * c, :], bank(key, 0, T), col(COL_NORM(occ) + 2 * c), None, ALU.mult)
                    nc.vector.tensor_scalar(hnT[:, 2 * c + 1, :], bank(key, T, T), col(COL_NORM(occ) + 2 * c + 1), None,
                                            ALU.mult).then_inc(s_free["v"], 1)

            def heads(ap, n=HG):
                return ap.rearrange("p (h e) -> p h e", h=n)

            def per_head(ap, n=HG):
                return ap.unsqueeze(2).broadcast_to([P, n, HD])

            def gates(L):
                drained(dve, ("J", L, 1, 0), "a")
                xa = area("xa").rearrange("p (b h) -> p b h", b=NB)
                dt = rws[:, ROW_DT + L * HG:ROW_DT + (L + 1) * HG].unsqueeze(1).broadcast_to([P, NB, HG])
                nc.vector.tensor_tensor(xa, ab[:, :, 0:HG], dt, ALU.add).then_inc(st.sem, st.up())
                nc.vector.tensor_scalar(area("em", 12, 12).rearrange("p (b h) -> p b h", b=NB), ab[:, :, HG:2 * HG], -1.0,
                                        None, ALU.mult).then_inc(st.sem, st.up())
                nc.vector.tensor_copy(area("em", 24, 6), rws[:, ROW_ALOG + L * HG:ROW_ALOG + (L + 1) * HG]).then_inc(
                    st.sem, st.up())
                step()
                nc.vector.scalar_tensor_tensor(out=area("em", 0, 12), in0=area("xa"), scalar=-1.0, in1=area("xa"),
                                               op0=ALU.mult, op1=ALU.min).then_inc(s_gin, 1)
                dve.wait_ge(s_gexp, L + 1)
                nc.vector.tensor_scalar(area("e1"), area("em", 0, 24), 1.0, None, ALU.add).then_inc(s_gadd, 1)
                dve.wait_ge(s_gadd, L + 1)
                nc.vector.reciprocal(area("beta"), area("e1", 12, 12)).then_inc(st.sem, st.up())
                dve.wait_ge(s_gln, L + 1)
                nc.vector.scalar_tensor_tensor(out=area("xa"), in0=area("xa"), scalar=0.0, in1=area("lnp"), op0=ALU.max,
                                               op1=ALU.add).then_inc(st.sem, st.up())
                step()
                ea = area("em", 24, 6).unsqueeze(1).broadcast_to([P, NB, HG])
                nc.vector.scalar_tensor_tensor(out=area("g").rearrange("p (b h) -> p b h", b=NB), in0=xa, scalar=-1.0,
                                               in1=ea, op0=ALU.mult, op1=ALU.mult).then_inc(s_g, 1)

            def decays(L):
                filled(dve, ("G", L))
                nc.vector.tensor_copy(area("gc"), bank(("G", L), 0, 18)).then_inc(s_free["v"], 1)
                drained(dve, ("G", L), "v")
                nc.vector.tensor_copy(area("gx", 0, 6), area("gc", 6, 6)).then_inc(st.sem, st.up())
                nc.vector.tensor_tensor(area("gx", 6, 6), area("gc", 12, 6), area("gc", 0, 6),
                                        ALU.subtract).then_inc(st.sem, st.up())
                step()
                nc.vector.tensor_scalar(area("gx"), area("gx"), 0.0, None, ALU.min).then_inc(s_gx, 1)
                for g in range(GS):
                    filled(dve, ("R", L, g))
                    for k, b, at in group_heads(g):
                        ins = nc.vector.tensor_scalar(dec[:, system_at(k, b)],
                                                      bank(("R", L, g), at, P), area("gc", b * HG + k, 1), 0.0,
                                                      ALU.subtract, ALU.min)
                    ins.then_inc(s_free["v"], 1)

            def convolution(L):
                for tap in range(CONV):
                    for c in range(CQ):
                        if tap == 0:
                            if c % 4 in (2, 3) and c % 2 == 0:
                                drained(dve, ("I", L, c // 2), "a")
                            elif c % 2 == 0:
                                drained(dve, ("I", L, c // 2), "v")
                            w = col(COL_CONV + (L * CQ + c) * CONV)
                            nc.vector.tensor_scalar(qkv[:, c, :], xc[:, c, 0:T], w, None, ALU.mult).then_inc(st.sem, st.up())
                            continue
                        w = col(COL_CONV + (L * CQ + c) * CONV + tap)
                        ins = nc.vector.scalar_tensor_tensor(out=qkv[:, c, :], in0=xc[:, c, tap:tap + T], scalar=w,
                                                             in1=qkv[:, c, :], op0=ALU.mult, op1=ALU.add)
                        if tap < CONV - 1:
                            ins.then_inc(st.sem, st.up())
                        else:
                            ins.then_inc(s_conv, 1)
                    if tap < CONV - 1:
                        step()
                dve.wait_ge(s_silu, 3 * L + 2)
                dve.wait_ge(s_conv, CQ * (L + 1))
                nc.vector.tensor_tensor(squares, area("qkv", 0, 1536), area("qkv", 0, 1536), ALU.mult).then_inc(s_sq, 1)
                for c in range(3):
                    drained(dve, ("N2", L, c), "a")
                    nc.vector.reciprocal(pbuf[:, 512 * c:512 * c + 512],
                                         pbuf[:, 512 * c:512 * c + 512]).then_inc(st.sem, st.up())
                    step()
                    nc.vector.tensor_tensor(area("qkv", 512 * c, 512), area("qkv", 512 * c, 512),
                                            pbuf[:, 512 * c:512 * c + 512], ALU.mult).then_inc(s_qk, 1)

            def delta(L):
                filled(dve, ("V", L, 2))
                dve.wait_ge(s_eg, L + 1)
                nc.vector.tensor_tensor(heads(kd), heads(bank(("V", L, 2), 0, DG)), per_head(area("eg", 6, 6)),
                                        ALU.mult).then_inc(s_free["v"], 1)
                for g in range(GS):
                    filled(dve, ("KK", L, g))
                    dve.wait_ge(s_dec, GS * L + g + 1)
                    for k, b, at in group_heads(g):
                        ins = nc.vector.scalar_tensor_tensor(out=mt[:, system_at(k, b)], in0=bank(("KK", L, g), at, P),
                                                             scalar=area("beta", b * HG + k, 1),
                                                             in1=dec[:, system_at(k, b)], op0=ALU.mult, op1=ALU.mult)
                    ins.then_inc(s_free["v"], 1)
                for g in range(GS):
                    filled(dve, ("QK", L, g))
                    drained(dve, ("KK", L, g), "v")
                    d = dec[:, GW * g:GW * g + GW]
                    nc.vector.scalar_tensor_tensor(out=d, in0=bank(("QK", L, g), 0, GW), scalar=SCALE, in1=d, op0=ALU.mult,
                                                   op1=ALU.mult).then_inc(s_free["v"], 1)
                eye = ident.unsqueeze(1).broadcast_to([P, 3, P])

                def systems(ap):
                    return ap.rearrange("p (s i) -> p s i", s=3)

                for g in range(GS):
                    at = slice(GW * g, GW * g + GW)
                    dve.wait_ge(s_cm, GS * NLEV * L + g + 1)
                    nc.vector.scalar_tensor_tensor(out=systems(xt[:, at]), in0=systems(cm[:, at]), scalar=-1.0, in1=eye,
                                                   op0=ALU.mult, op1=ALU.add)
                    filled(dve, ("C0", L, g))
                    nc.vector.scalar_tensor_tensor(out=systems(xi[:, at]), in0=systems(bank(("C0", L, g), 0, GW)), scalar=-1.0,
                                                   in1=eye, op0=ALU.mult, op1=ALU.add).then_inc(s_free["v"], 1)
                for lev in range(1, NLEV):
                    for g in range(GS):
                        at = slice(GW * g, GW * g + GW)
                        for kind, dst in (("X", xi[:, at]), ("Y", xt[:, at])):
                            if (kind, L, lev, g) in tiles.at:
                                filled(dve, (kind, L, lev, g))
                                nc.vector.tensor_tensor(dst, dst, bank((kind, L, lev, g), 0, GW),
                                                        ALU.subtract).then_inc(s_free["v"], 1)
                filled(dve, ("W0", L))
                nc.vector.tensor_tensor(heads(vn[:, 0, :]), heads(bank(("W0", L), 0, DG)), per_head(area("beta", 0, 6)),
                                        ALU.mult).then_inc(s_free["v"], 1)
                for parity in range(2):
                    key = (f"KS{parity}", L)
                    filled(dve, key)
                    nc.vector.tensor_tensor(rr.rearrange("p (q two e) -> p q two e", two=2, e=HD)[:, :, parity, :],
                                            heads(bank(key, 0, 3 * HD), 3), per_head(area("eg", 0, 6)[:, parity::2], 3),
                                            ALU.mult).then_inc(s_free["v"], 1)
                drained(dve, ("KS1", L), "v")
                nc.vector.tensor_tensor(rr, vt[:, 1, :], rr, ALU.subtract).then_inc(s_rr, 1)
                filled(dve, ("W1", L))
                nc.vector.tensor_tensor(heads(vn[:, 1, :]), heads(bank(("W1", L), 0, DG)), per_head(area("beta", 6, 6)),
                                        ALU.mult).then_inc(s_free["v"], 1)
                filled(dve, ("O1", L))
                drained(dve, ("QS1", L), "a")
                nc.vector.scalar_tensor_tensor(out=o[:, 1, 0:DG], in0=qs, scalar=SCALE, in1=bank(("O1", L), 0, DG),
                                               op0=ALU.mult, op1=ALU.add).then_inc(s_free["v"], 1)

            def windows(L):
                for k in range(HW):
                    filled(dve, ("D", L, k))
                    nc.vector.scalar_tensor_tensor(out=prob[:, k, :], in0=cc("dist"), scalar=SLOPES[k] / SCALE,
                                                   in1=bank(("D", L, k), 0, 384), op0=ALU.mult,
                                                   op1=ALU.add).then_inc(s_free["v"], 1)
                    drained(dve, ("D", L, k), "v")
                    nc.vector.reduce_max(area("den2" if False else "rden", 2 * k, 1), prob[:, k, 0:P], AX_X).then_inc(st.sem, st.up())
                    nc.vector.reduce_max(area("rden", 2 * k + 1, 1), prob[:, k, P:384], AX_X).then_inc(st.sem, st.up())
                    step()
                    nc.vector.tensor_scalar(area("nm", 2 * k, 2), area("rden", 2 * k, 2), -SCALE, None,
                                            ALU.mult).then_inc(s_nm, 1)
                for k in range(HW):
                    dve.wait_ge(s_dex, HW * L + k + 1)
                    nc.vector.tensor_tensor(prob[:, k, :], prob[:, k, :], cc("mult"), ALU.mult).then_inc(s_dpr, 1)
                for k in range(HW):
                    filled(dve, ("F", L, k))
                    f = bank(("F", L, k), 0, NB * (HD + 1)).rearrange("p (b e) -> p b e", b=NB)
                    nc.vector.reciprocal(area("rden", 2 * k, 2), f[:, :, HD]).then_inc(st.sem, st.up())
                    step()
                    nc.vector.tensor_tensor(o[:, :, DG + HD * k:DG + HD * k + HD], f[:, :, 0:HD],
                                            per_head(area("rden", 2 * k, 2), NB), ALU.mult).then_inc(s_free["v"], 1)

            def stick(L):
                for k in range(HS):
                    if k == 0:
                        dve.wait_ge(s_zl, L + 1)
                    nc.vector.scalar_tensor_tensor(out=sps[:, k, :], in0=zs[:, k, :], scalar=0.0, in1=es[:, k, :],
                                                   op0=ALU.max, op1=ALU.add).then_inc(st.sem, st.up())
                    step()
                    nc.vector.tensor_tensor(sps[:, k, :], sps[:, k, :], cc("earlier"), ALU.mult).then_inc(s_sps, 1)
                for k in range(HS):
                    filled(dve, ("CS", L, k))
                    nc.vector.tensor_tensor(zs[:, k, :], zs[:, k, :], bank(("CS", L, k), 0, 384),
                                            ALU.subtract).then_inc(s_free["v"], 1)
                for k in range(HS):
                    dve.wait_ge(s_ze, HS * L + k + 1)
                    nc.vector.scalar_tensor_tensor(out=zs[:, k, :], in0=zs[:, k, :], scalar=1.0, in1=cc("earlier"),
                                                   op0=ALU.min, op1=ALU.mult).then_inc(s_aT, 1)

            def head_norms(L):
                drained(dve, ("O0", L), "a")
                drained(dve, ("U", L), "a")
                drained(dve, ("F", L, HW - 1), "v")
                nc.vector.tensor_tensor(osq, hn_flat, hn_flat, ALU.mult).then_inc(st.sem, st.up())
                step()
                nc.vector.tensor_reduce(area("ss", 0, 32), osq.rearrange("p (h e) -> p h e", e=HD), AX_X,
                                        ALU.add).then_inc(s_oss, 1)
                dve.wait_ge(s_ors, L + 1)
                of = hn_flat.rearrange("p (h e) -> p h e", e=HD)
                nc.vector.tensor_tensor(of, of, per_head(area("rs", 0, 32), 32), ALU.mult).then_inc(st.sem, st.up())
                step()
                for i, (start, n) in enumerate(((0, HG), (DG, HW), (DG + DW, HS))):
                    w = rws[:, ROW_HN(L, i):ROW_HN(L, i) + HD].unsqueeze(1).unsqueeze(1).broadcast_to([P, NB, n, HD])
                    v = o[:, :, start:start + n * HD].rearrange("p b (h e) -> p b h e", h=n)
                    nc.vector.tensor_tensor(v, v, w, ALU.mult).then_inc(st.sem, st.up())
                step()
                dve.wait_ge(s_zg, L + 1)
                nc.vector.tensor_tensor(o[:, :, 0:DG], o[:, :, 0:DG], zt[:, :, :], ALU.mult).then_inc(s_o, 1)
                for c in (0, 2):
                    filled(dve, ("OT", L, c))
                    nc.vector.tensor_copy(hnT_flat[:, 512 * c:512 * c + 512], bank(("OT", L, c))).then_inc(s_free["v"], 1)

            def add_to_residual(key, b, m, it=None):
                filled(dve, key, it)
                v = h[:, b, 512 * m:512 * m + 512]
                nc.vector.tensor_tensor(v, v, bank(key), ALU.add).then_inc(s_free["v"], 1)

            def mixers(L):
                if L:
                    residual_ready(dve, 3 * L, None)
                nc.vector.memset(xc[:, :, 0:3], 0.0).then_inc(st.sem, st.up())
                step()
                norm(3 * L)
                for t in range(0, 10, 2):
                    filled(dve, ("I", L, t))
                    for c in (2 * t, 2 * t + 1):
                        dst = xc[:, c, 3:3 + T] if c < CQ else att[:, c - CQ, :]
                        ins = nc.vector.tensor_copy(dst, bank(("I", L, t), T * (c % 2), T))
                    ins.then_inc(s_free["v"], 1)
                gates(L)
                decays(L)
                convolution(L)
                delta(L)
                windows(L)
                stick(L)
                head_norms(L)
                for b in range(NB):
                    for m in range(2):
                        add_to_residual(("WO", L, b, m), b, m)

            def ple(L, items=None):
                for n in range(4):
                    b, m = n // 2, n % 2
                    drained(dve, ("PG", L, b, m), "a", items)
                    filled(dve, ("PP", L, b, m), items)
                    nc.vector.tensor_tensor(sgp[m], sig[m], bank(("PP", L, b, m)), ALU.mult).then_inc(s_free["v"], 1)
                    drained(dve, ("PP", L, b, m), "v", items)
                    v = h[:, b, 512 * m:512 * m + 512]
                    nc.vector.tensor_tensor(v, v, sgp[m], ALU.add).then_inc(s_ple, 1)

            dve.wait_ge(s_in, 64)
            nc.vector.memset(dva[:, :, :, HD], 1.0).then_inc(st.sem, st.up())
            mixers(0)
            norm(1)
            for f in range(NF):
                drained(dve, ("H", f), "a")
                if f >= 4:
                    filled(dve, ("H", f))
                nc.vector.tensor_tensor(ffg[f % 4], ffs[f % 2], bank(("H", f), T, T), ALU.mult).then_inc(s_free["v"], 1)
            for b in range(NB):
                for m in range(2):
                    add_to_residual(("Y2", b, m), b, m)
            norm(2)
            ple(0)
            mixers(1)
            norm(4)

            filled(dve, ("LG",))
            nc.vector.tensor_copy(lg, bank(("LG",), 0, 16).rearrange("p (b e) -> p b e", b=NB)).then_inc(s_free["v"], 1)
            drained(dve, ("LG",), "v")
            nc.vector.tensor_reduce(top, lg, AX_X, ALU.max).then_inc(st.sem, st.up())
            other = [lg[:, b, :].unsqueeze(1).broadcast_to([P, NE, NE]) for b in range(NB)]
            own = [lg[:, b, :].unsqueeze(2).broadcast_to([P, NE, NE]) for b in range(NB)]
            lower8 = cc("lower8").rearrange("p (e f) -> p e f", e=NE)
            for b in range(NB):
                nc.vector.tensor_tensor(pairs[0][:, b], other[b], own[b], ALU.is_gt).then_inc(st.sem, st.up())
                nc.vector.tensor_tensor(pairs[1][:, b], other[b], own[b], ALU.is_ge).then_inc(st.sem, st.up())
            step()
            for b in range(NB):
                nc.vector.tensor_tensor(pairs[1][:, b], pairs[1][:, b], lower8, ALU.mult).then_inc(st.sem, st.up())
            nc.vector.tensor_tensor(exl, lg, top.unsqueeze(2).broadcast_to([P, NB, NE]), ALU.subtract).then_inc(s_lsub, 1)
            step()
            for b in range(NB):
                nc.vector.tensor_tensor(pairs[0][:, b], pairs[0][:, b], pairs[1][:, b], ALU.max).then_inc(st.sem, st.up())
            step()
            nc.vector.tensor_reduce(rank, pairs[0], AX_X, ALU.add).then_inc(st.sem, st.up())
            step()
            nc.vector.tensor_scalar(sel, rank, TOPK - 0.5, None, ALU.is_lt).then_inc(s_sel, 1)
            dve.wait_ge(s_sel, 1)
            dve.wait_ge(s_lex, 1)
            nc.vector.tensor_tensor(exl, exl, sel, ALU.mult).then_inc(st.sem, st.up())
            step()
            nc.vector.tensor_reduce(den, exl, AX_X, ALU.add).then_inc(st.sem, st.up())
            step()
            nc.vector.reciprocal(den, den).then_inc(st.sem, st.up())
            step()
            nc.vector.tensor_tensor(gate, exl, den.unsqueeze(2).broadcast_to([P, NB, NE]),
                                    ALU.mult).then_inc(st.sem, st.up())
            filled(dve, ("POS",))
            nc.vector.tensor_copy(cum, bank(("POS",), 0, 24)).then_inc(s_free["v"], 1)
            drained(dve, ("POS",), "v")
            nc.vector.tensor_tensor(pos1, cum[:, 0:16].rearrange("p (b e) -> p b e", b=NB), sel,
                                    ALU.mult).then_inc(st.sem, st.up())
            nc.vector.tensor_scalar(over, cum[:, 16:24], P + 0.5, None, ALU.is_gt).then_inc(st.sem, st.up())
            step()
            nc.vector.tensor_tensor(pairs[0][:, 0], over.unsqueeze(1).broadcast_to([P, NE, NE]), lower8,
                                    ALU.mult).then_inc(st.sem, st.up())
            nc.vector.tensor_scalar(posi[:, :, 0:NE], pos1, -1.0, None, ALU.add).then_inc(st.sem, st.up())
            nc.vector.tensor_copy(gati[:, :, 0:NE], gate).then_inc(st.sem, st.up())
            step()
            nc.vector.tensor_reduce(oidx, pairs[0][:, 0], AX_X, ALU.add).then_inc(st.sem, st.up())
            step()
            shape = [P, MORE + 1, NE]
            nc.vector.tensor_tensor(osel, oidx.unsqueeze(1).broadcast_to(shape), cc("item").unsqueeze(2).broadcast_to(shape),
                                    ALU.is_equal).then_inc(st.sem, st.up())
            step()
            nc.vector.tensor_tensor(osel, osel, over.unsqueeze(1).broadcast_to(shape), ALU.mult).then_inc(st.sem, st.up())
            step()
            for b in range(NB):
                nc.vector.tensor_tensor(oprd[:, b], osel, pos1[:, b, :].unsqueeze(1).broadcast_to(shape),
                                        ALU.mult).then_inc(st.sem, st.up())
                nc.vector.tensor_tensor(oprd[:, 2 + b], osel, gate[:, b, :].unsqueeze(1).broadcast_to(shape),
                                        ALU.mult).then_inc(st.sem, st.up())
            nc.vector.tensor_tensor(oprd[:, 4], osel, cc("expert").unsqueeze(1).broadcast_to(shape),
                                    ALU.mult).then_inc(st.sem, st.up())
            nc.vector.tensor_reduce(tabf[:, MORE + 1:MORE + 2], over, AX_X, ALU.add).then_inc(st.sem, st.up())
            step()
            nc.vector.tensor_reduce(posi[:, :, NE:NI], oprd[:, 0:2], AX_X, ALU.add).then_inc(st.sem, st.up())
            nc.vector.tensor_reduce(gati[:, :, NE:NI], oprd[:, 2:4], AX_X, ALU.add).then_inc(st.sem, st.up())
            nc.vector.tensor_reduce(tabf[:, 0:MORE + 1], oprd[:, 4], AX_X, ALU.add).then_inc(st.sem, st.up())
            nc.vector.tensor_scalar(tabf[:, MORE + 2:MORE + 3], tabf[:, MORE + 1:MORE + 2], float(NE), None,
                                    ALU.add).then_inc(st.sem, st.up())
            step()
            nc.vector.tensor_scalar(posi[:, :, NE:NI], posi[:, :, NE:NI], -1.0 - P, None,
                                    ALU.add).then_inc(st.sem, st.up())
            nc.vector.tensor_copy(table[0:1, 0:MORE + 3], tabf[0:1, 0:MORE + 3]).then_inc(s_tab, 1)
            step()

            def selection(i):
                for b in range(NB):
                    p = posi[:, b, bass.ds(i, 1)] if not isinstance(i, int) else posi[:, b, i:i + 1]
                    g = gati[:, b, bass.ds(i, 1)] if not isinstance(i, int) else gati[:, b, i:i + 1]
                    nc.vector.tensor_scalar(pick[:, b, :], cc("slots"), p, None, ALU.is_equal)
                    ins = nc.vector.tensor_scalar(pickg[:, b, :], cc("slots"), p, g, ALU.is_equal, ALU.mult)
                ins.then_inc(s_pick, 1)

            def gathered(when, it):
                filled(dve, ("GA", when, 0), it)
                for k in range(4):
                    ins = nc.vector.tensor_scalar(xg[:, k, :], bank(("GA", when, 0), P * k, P), col(COL_NORM(4) + k), None,
                                                  ALU.mult)
                ins.then_inc(s_free["v"], 1)

            selection(0)
            gathered("first", None)
            filled(dve, ("GT", "first"))
            dve.wait_ge(s_tab, 1)
            items = dve.value_load(table[0:1, MORE + 2:MORE + 3], min_val=NE, max_val=NE + MORE)
            with dve.Fori(0, items) as i:
                filled(dve, ("GT", "next"), i, 1)
                selection(i + 1)
                for j in range(NJ):
                    drained(dve, ("A", j), "a", i)
                    filled(dve, ("B", j), i)
                    nc.vector.tensor_tensor(mg[j % 2], ms[j % 2], bank(("B", j)), ALU.mult).then_inc(s_free["v"], 1)
                gathered("next", i)
                for m in range(2):
                    for b in range(NB):
                        add_to_residual(("SC", b, m), b, m, i)
            norm(5, items)
            ple(1, items)
            dve.wait_ge(s_rstd, 7)
            dve.wait_ge(s_fw, 16)
            for b in range(NB):
                nc.vector.scalar_tensor_tensor(out=res[:, b, :], in0=h[:, b, :], scalar=area("mx", 10 + b, 1), in1=finw,
                                               op0=ALU.mult, op1=ALU.mult).then_inc(s_res, 1)

        @block.tensor
        def _(pe):
            def opened(key, it=None):
                before = tiles.at[key]["before"]
                if before is None:
                    return
                back = tiles.at[key]["back"]
                for who, count in before["drained"].items():
                    pe.wait_ge(s_free[who], through(count - back * per_drain[who], it, per_drain[who]))

            def norm(occ, items=None):
                for c in range(4):
                    opened(("T", occ, c), items)
                    if c == 0:
                        pe.wait_ge(s_hn["a"], occ + 1)
                        pe.wait_ge(s_hn["v"], occ + 1)
                    for q in range(4):
                        k, b = 2 * c + q // 2, q % 2
                        ins = pe.transpose(bank(("T", occ, c), P * q, P), hn[:, b, P * k:P * k + P], ident)
                    ins.then_inc(s_fill, 1)

            def hnT_ready(occ, items=None):
                drained(pe, ("T", occ, 2), "v", items)
                drained(pe, ("T", occ, 3), "a", items)

            def rows_times(key, b, w, width, items=None, lhs=None):
                opened(key, items)
                for k in range(KC):
                    ins = pe.matmul(bank(key, 0, width), hnT[:, k, P * b:P * b + P], w[:, k * width:(k + 1) * width],
                                    start=(k == 0), stop=(k == KC - 1))
                ins.then_inc(s_fill, 1)

            def projections(L):
                hnT_ready(3 * L)

                def token_major(g, width):
                    landed(pe, ("J", L, g))
                    for b in range(NB):
                        rows_times(("J", L, b, g), b, weights(("J", L, g)), width)

                token_major(0, DG + 2 * HG)
                for t in range(10):
                    landed(pe, ("I", L, t // 2))
                    opened(("I", L, t))
                    w = weights(("I", L, t // 2)).rearrange("p (c k m) -> p c k m", c=4, k=KC)
                    for c in (2 * t, 2 * t + 1):
                        if c < CQ + CA:
                            for k in range(KC):
                                ins = pe.matmul(bank(("I", L, t), T * (c % 2), T), w[:, c % 4, k, :], hnT[:, k, :],
                                                start=(k == 0), stop=(k == KC - 1))
                    ins.then_inc(s_fill, 1)
                token_major(1, DW)
                token_major(2, DS)

            def lanes(k):
                return slice(HD * (k % 2), HD * (k % 2) + HD)

            def delta(L):
                opened(("G", L))
                pe.wait_ge(s_g, L + 1)
                g12 = area("g")
                for b in range(NB):
                    pe.matmul(bank(("G", L), HG * b, HG), cc("upto"), g12[:, HG * b:HG * b + HG], start=True, stop=True)
                pe.matmul(bank(("G", L), 2 * HG, HG), ones, g12[:, 0:HG], start=True, stop=True).then_inc(s_fill, 1)
                for g in range(GS):
                    opened(("R", L, g))
                    for k, b, at in group_heads(g):
                        ins = pe.matmul(bank(("R", L, g), at, P), area("g", b * HG + k, 1).broadcast_to([P, P]),
                                        cc("upto"), start=True, stop=True)
                    ins.then_inc(s_fill, 1)
                for c in range(3):
                    opened(("N2", L, c))
                    pe.wait_ge(s_sq, L + 1)
                    pe.matmul(bank(("N2", L, c)), cc("headsum"), squares[:, 512 * c:512 * c + 512], start=True,
                              stop=True).then_inc(s_fill, 1)
                for c in range(3):
                    opened(("V", L, c))
                    if c == 0:
                        pe.wait_ge(s_silu, 3 * L + 3)
                    if c == 2:
                        pe.wait_ge(s_qk, 3 * L + 3)
                    for k in range(3):
                        src = qkv[:, 6 + k, P * c:P * c + P] if c < 2 else qkv[:, 3 + k, 0:P]
                        ins = pe.transpose(bank(("V", L, c), P * k, P), src, ident)
                    ins.then_inc(s_fill, 1)
                for kind, first in (("KK", 3), ("QK", 0)):
                    for g in range(GS):
                        opened((kind, L, g))
                        for k, b, at in group_heads(g):
                            tok = slice(P * b, P * b + P)
                            ins = pe.matmul(bank((kind, L, g), at, P), qkv[lanes(k), 3 + k // 2, tok],
                                            qkv[lanes(k), first + k // 2, tok], start=True, stop=True)
                        ins.then_inc(s_fill, 1)

                def group(kind, lev, g, lhs, rhs):
                    key = (kind, L, g) if lev is None else (kind, L, lev, g)
                    opened(key)
                    for s in range(3):
                        at = slice(GW * g + P * s, GW * g + P * s + P)
                        if rhs is None:
                            ins = pe.transpose(bank(key, P * s, P), lhs[:, at], ident)
                        else:
                            ins = pe.matmul(bank(key, P * s, P), lhs[:, at], rhs[:, at], start=True, stop=True)
                    ins.then_inc(s_fill, 1)

                for g in range(GS):
                    pe.wait_ge(s_cm, GS * NLEV * L + g + 1)
                    group("C0", None, g, cm, None)
                for lev in range(1, NLEV):
                    for g in range(GS):
                        pe.wait_ge(s_cm, GS * NLEV * L + GS * lev + g + 1)
                        drained(pe, ("C0", L, g) if lev == 1 else ("X", L, lev - 1, g), "v")
                        group("P", lev, g, cm, xi)
                    for g in range(GS):
                        drained(pe, ("P", L, lev, g), "a")
                        if lev > 1:
                            drained(pe, ("Y", L, lev - 1, g), "v")
                        if lev < NLEV - 1:
                            group("X", lev, g, xt, pbuf)
                        group("Y", lev, g, pbuf, xt)

                def heads_of(key, wait, lhs, rhs, out=None, which=range(HG)):
                    opened(key)
                    wait()
                    for n, k in enumerate(which):
                        dst = bank(key, HD * n, HD) if out is None else out(k)
                        ins = pe.matmul(dst, lhs(k), rhs(k), start=True, stop=True)
                    ins.then_inc(s_fill, 1)

                def system(ap, b):
                    return lambda k: ap[:, system_at(k, b)]

                def state(k):
                    return s1[lanes(k), HD * (k // 2):HD * (k // 2) + HD]

                drained_y = lambda: [drained(pe, ("Y", L, NLEV - 1, g), "v") for g in range(GS)]
                heads_of(("W0", L), lambda: (drained_y(), drained(pe, ("V", L, 0), "a")), system(xt, 0),
                         lambda k: vt[:, 0, HD * k:HD * k + HD])
                heads_of(("S", L), lambda: drained(pe, ("W0", L), "v"), lambda k: kd[:, HD * k:HD * k + HD],
                         lambda k: vn[:, 0, HD * k:HD * k + HD],
                         lambda k: ps[lanes(k), tiles.at[("S", L)]["bank"], HD * (k // 2):HD * (k // 2) + HD])
                for name, first in (("KS", 3), ("QS", 0)):
                    for parity in range(2):
                        heads_of((f"{name}{parity}", L), lambda: drained(pe, ("S", L), "a"),
                                 lambda k: qkv[lanes(k), first + k // 2, P:T], state, which=range(parity, HG, 2))
                heads_of(("W1", L), lambda: pe.wait_ge(s_rr, L + 1), system(xt, 1), lambda k: rr[:, HD * k:HD * k + HD])
                heads_of(("O0", L), lambda: None, system(dec, 0), lambda k: vn[:, 0, HD * k:HD * k + HD])
                heads_of(("O1", L), lambda: drained(pe, ("W1", L), "v"), system(dec, 1),
                         lambda k: vn[:, 1, HD * k:HD * k + HD])

            def windows(L):
                for k in range(HW):
                    opened(("D", L, k))
                    q, kk = att[lanes(k), k // 2, :], att[lanes(k), 3 + k // 2, :]
                    pe.matmul(bank(("D", L, k), 0, P), q[:, 0:P], kk[:, 0:P], start=True, stop=True)
                    pe.matmul(bank(("D", L, k), P, T), q[:, P:T], kk, start=True, stop=True).then_inc(s_fill, 1)
                for k in range(HW):
                    opened(("E", L, k))
                    pe.wait_ge(s_dpr, HW * L + k + 1)
                    for s in range(3):
                        ins = pe.transpose(bank(("E", L, k), P * s, P), prob[:, k, P * s:P * s + P], ident)
                    ins.then_inc(s_fill, 1)
                for k in range(HW):
                    opened(("F", L, k))
                    drained(pe, ("E", L, k), "a")
                    w = HD + 1
                    pe.matmul(bank(("F", L, k), 0, w), probT[:, k, 0:P], dva[:, 0, k, :], start=True, stop=True)
                    pe.matmul(bank(("F", L, k), w, w), probT[:, k, P:T], dva[:, 0, k, :], start=True, stop=False)
                    pe.matmul(bank(("F", L, k), w, w), probT[:, k, T:384], dva[:, 1, k, :], start=False,
                              stop=True).then_inc(s_fill, 1)

            def stick(L):
                for k in range(HS):
                    opened(("Z", L, k))
                    q, kk = att[lanes(k), 6 + k // 2, :], att[lanes(k), 8 + k // 2, :]
                    pe.matmul(bank(("Z", L, k), 0, T), kk[:, 0:P], q, start=True, stop=True)
                    pe.matmul(bank(("Z", L, k), T, P), kk[:, P:T], q[:, P:T], start=True, stop=True).then_inc(s_fill, 1)
                for k in range(HS):
                    opened(("CS", L, k))
                    pe.wait_ge(s_sps, HS * L + k + 1)
                    pe.matmul(bank(("CS", L, k), 0, 384), cc("from"), sps[:, k, :], start=True, stop=False)
                    pe.matmul(bank(("CS", L, k), P, P), ones, sps[:, k, T:384], start=False, stop=True).then_inc(s_fill, 1)
                opened(("U", L))
                for k in range(HS):
                    pe.wait_ge(s_aT, HS * L + k + 1)
                    v = sva[:, :, HD * k:HD * k + HD]
                    pe.matmul(bank(("U", L), HD * k, HD), zs[:, k, 0:P], v[:, 0, :], start=True, stop=True)
                    pe.matmul(bank(("U", L), DS + HD * k, HD), zs[:, k, P:T], v[:, 0, :], start=True, stop=False)
                    ins = pe.matmul(bank(("U", L), DS + HD * k, HD), zs[:, k, T:384], v[:, 1, :], start=False, stop=True)
                ins.then_inc(s_fill, 1)

            def mixers(L):
                norm(3 * L)
                projections(L)
                delta(L)
                windows(L)
                stick(L)
                for c in range(4):
                    opened(("OT", L, c))
                    if c == 0:
                        pe.wait_ge(s_o, L + 1)
                    for q in range(4):
                        k, b = 2 * c + q // 2, q % 2
                        ins = pe.transpose(bank(("OT", L, c), P * q, P), o[:, b, P * k:P * k + P], ident)
                    ins.then_inc(s_fill, 1)
                drained(pe, ("OT", L, 2), "v")
                drained(pe, ("OT", L, 3), "a")
                for b in range(NB):
                    for m in range(2):
                        landed(pe, ("WO", L, m))
                        rows_times(("WO", L, b, m), b, weights(("WO", L, m)), 512)

            def ple(L, items=None):
                hnT_ready(3 * L + 2, items)
                landed(pe, ("PP", L), items)
                pw = weights(("PP", L))
                for b in range(NB):
                    for m in range(2):
                        landed(pe, ("PG", L, m), items)
                        rows_times(("PG", L, b, m), b, weights(("PG", L, m)), 512, items)
                        key = ("PP", L, b, m)
                        opened(key, items)
                        for k in range(PLE // P):
                            ins = pe.matmul(bank(key), pw[:, 2048 + T * k + P * b:2048 + T * k + P * b + P],
                                            pw[:, D * k + 512 * m:D * k + 512 * m + 512], start=(k == 0), stop=(k == 1))
                        ins.then_inc(s_fill, 1)

            pe.wait_ge(s_in, 64)
            mixers(0)
            norm(1)
            hnT_ready(1)

            def dense_down(f):
                drained(pe, ("H", f), "v")
                if f % 4 == 0:
                    landed(pe, ("w2", f // 4))
                w = weights(("w2", f // 4))
                for b in range(NB):
                    for m in range(2):
                        if f == 0:
                            opened(("Y2", b, m))
                        ins = pe.matmul(bank(("Y2", b, m)), ffg[f % 4][:, P * b:P * b + P],
                                        w[:, D * (f % 4) + 512 * m:D * (f % 4) + 512 * m + 512], start=(f == 0),
                                        stop=(f == NF - 1))
                        if f == NF - 1:
                            ins.then_inc(s_fill, 1)
                if f % 4 == 3:
                    ins.then_inc(s_down, 1)

            for f in range(NF):
                opened(("H", f))
                for side, name in ((0, "w1"), (1, "w3")):
                    if f % 4 == 0:
                        landed(pe, (name, f // 4))
                    w = weights((name, f // 4)).rearrange("p (c k m) -> p c k m", c=4, k=KC)
                    for k in range(KC):
                        ins = pe.matmul(bank(("H", f), T * side, T), w[:, f % 4, k, :], hnT[:, k, :], start=(k == 0),
                                        stop=(k == KC - 1))
                ins.then_inc(s_fill, 1)
                if f >= 1:
                    dense_down(f - 1)
            dense_down(NF - 1)
            norm(2)
            ple(0)
            mixers(1)
            norm(4)
            hnT_ready(4)
            opened(("LG",))
            for b in range(NB):
                for k in range(KC):
                    ins = pe.matmul(bank(("LG",), NE * b, NE), hnT[:, k, P * b:P * b + P],
                                    cols[:, COL_ROUTER + NE * k:COL_ROUTER + NE * k + NE], start=(k == 0),
                                    stop=(k == KC - 1))
            ins.then_inc(s_fill, 1)
            opened(("POS",))
            pe.wait_ge(s_sel, 1)
            pe.matmul(bank(("POS",), 0, NE), cc("upto"), sel[:, 0, :], start=True, stop=True)
            for start in (NE, 2 * NE):
                pe.matmul(bank(("POS",), start, NE), ones, sel[:, 0, :], start=True, stop=False)
                ins = pe.matmul(bank(("POS",), start, NE), cc("upto") if start == NE else ones, sel[:, 1, :], start=False,
                                stop=True)
            ins.then_inc(s_fill, 1)

            def gather(when, it, number):
                pe.wait_ge(s_pick, number)
                for half in range(2):
                    key = ("GA", when, half)
                    opened(key, it)
                    for q in range(4):
                        k = 4 * half + q
                        for b in range(NB):
                            ins = pe.matmul(bank(key, P * q, P), hn[:, b, P * k:P * k + P], pick[:, b, :], start=(b == 0),
                                            stop=(b == NB - 1))
                    ins.then_inc(s_fill, 1)

            def scatter_matrix(when, it):
                opened(("GT", when), it)
                for b in range(NB):
                    ins = pe.transpose(bank(("GT", when), P * b, P), pickg[:, b, :], ident)
                ins.then_inc(s_fill, 1)

            gather("first", None, 1)
            scatter_matrix("first", None)
            for who in "va":
                pe.wait_ge(s_free[who], tiles.base[who])
            pe.wait_ge(s_tab, 1)
            items = pe.value_load(table[0:1, MORE + 2:MORE + 3], min_val=NE, max_val=NE + MORE)
            with pe.Fori(0, items) as i:
                def up(kind, j):
                    opened((kind, j), i)
                    landed(pe, (kind, j), i)
                    for k in range(KC):
                        ins = pe.matmul(bank((kind, j)), xg[:, k, :], weights((kind, j))[:, 512 * k:512 * k + 512],
                                        start=(k == 0), stop=(k == KC - 1))
                    ins.then_inc(s_fill, 1)

                def turn(j):
                    opened(("TT", j), i)
                    drained(pe, ("B", j), "v", i)
                    for q in range(4):
                        ins = pe.transpose(bank(("TT", j), P * q, P), mg[j % 2][:, P * q:P * q + P], ident)
                    ins.then_inc(s_fill, 1)

                def down(j):
                    drained(pe, ("TT", j), "a", i)
                    landed(pe, ("C", j), i)
                    w = weights(("C", j))
                    if j == 0:
                        opened(("YY", 0), i)
                        opened(("YY", 1), i)
                    for m in range(2):
                        for c in range(4):
                            ins = pe.matmul(bank(("YY", m)), mT[j % 2][:, P * c:P * c + P],
                                            w[:, D * c + 512 * m:D * c + 512 * m + 512], start=(j == 0 and c == 0),
                                            stop=(j == NJ - 1 and c == 3))
                        if j == NJ - 1:
                            ins.then_inc(s_fill, 1)
                    if j < NJ - 1:
                        ins.then_inc(s_down, 1)

                drained(pe, ("GA", "next", 0), "v", i, 1)
                drained(pe, ("GA", "next", 1), "a", i, 1)
                for j in range(NJ):
                    up("A", j)
                    if j:
                        turn(j - 1)
                    up("B", j)
                    if j:
                        down(j - 1)
                gather("next", i, i + 2)
                turn(NJ - 1)
                down(NJ - 1)
                drained(pe, ("GT", "next"), "a", i, 1)
                for m in range(2):
                    drained(pe, ("YY", m), "a", i)
                    for b in range(NB):
                        opened(("SC", b, m), i)
                        pe.matmul(bank(("SC", b, m)), back[:, P * b:P * b + P], ysb[:, 512 * m:512 * m + 512], start=True,
                                  stop=True).then_inc(s_fill, 1)
                scatter_matrix("next", i)
            for who in "va":
                pe.wait_ge(s_free[who], through(tiles.base[who], items, per_drain[who]))
            norm(5, items)
            ple(1, items)


def chunks_of(w):
    k, c = w.shape
    return w.reshape(k // P, P, c // P, P).transpose(1, 2, 0, 3)


def slot(*parts):
    flat = np.concatenate([a.reshape(P, -1) for a in parts], 1)
    out = np.zeros((P, SLOT), np.float32)
    out[:, :flat.shape[1]] = flat
    return out


def k_major(w):
    return w.reshape(-1, P, w.shape[1]).transpose(1, 0, 2)


def kernel(**inputs):
    import concourse.bacc as bacc
    from concourse.bass_utils import run_bass_kernel_spmd

    a = {k: np.asarray(v) for k, v in inputs.items()}
    order, _, n_static, per_load, tail = plan_loads()
    w_in = a["w_in"]
    q0, z0, dq0 = 0, 3 * DG, 4 * DG + 2 * HG
    dv0 = dq0 + 2 * DW
    sq0 = dv0 + DW
    sv0 = sq0 + 2 * DS

    def load(key):
        kind = key[0]
        if kind == "J":
            L, g = key[1:]
            lo, hi = ((z0, dq0), (dv0, sq0), (sv0, sv0 + DS))[g]
            return slot(k_major(w_in[L][:, lo:hi]))
        if kind == "I":
            L, c = key[1:]
            every = np.concatenate([w_in[L][:, q0:z0], w_in[L][:, dq0:dv0], w_in[L][:, sq0:sv0]], 1)
            return slot(chunks_of(every[:, 512 * c:min(512 * c + 512, every.shape[1])]))
        if kind == "WO":
            return slot(k_major(a["w_out"][key[1]][:, 512 * key[2]:512 * key[2] + 512]))
        if kind in ("w1", "w3"):
            return slot(chunks_of(a["ffn_" + kind][0][:, 512 * key[1]:min(512 * key[1] + 512, FF)]))
        if kind == "w2":
            return slot(k_major(a["ffn_w2"][0][512 * key[1]:min(512 * key[1] + 512, FF)]))
        if kind == "PP":
            return slot(k_major(a["ple_proj"][key[1]]), k_major(np.ascontiguousarray(a["p"][key[1], 0].T)))
        return slot(k_major(a["ple_gate"][key[1]][:, 512 * key[2]:512 * key[2] + 512]))

    stream = np.stack([load(key) for key in order[:n_static] + tail])
    experts = np.empty((NE, per_load, P, SLOT), np.float32)
    for n, (kind, j) in enumerate(order[n_static:]):
        at = slice(512 * j, 512 * j + 512)
        if kind == "C":
            experts[:, n] = a["moe_w2"][0][:, at].reshape(NE, 4, P, D).transpose(0, 2, 1, 3).reshape(NE, P, SLOT)
        else:
            w = a["moe_w1" if kind == "A" else "moe_w3"][0][:, :, at]
            experts[:, n] = w.reshape(NE, KC, P, 512).transpose(0, 2, 1, 3).reshape(NE, P, SLOT)
    norms = np.stack([a["attn_norm_w"], a["ffn_norm_w"], a["ple_norm_w"]], 1)
    columns = np.concatenate([
        norms.reshape(-1, P).T,
        a["conv_w"].reshape(DEPTH, CONV, CQ, P).transpose(3, 0, 2, 1).reshape(P, -1),
        k_major(a["router_w"][0]).reshape(P, -1)], 1)
    heads = np.stack([a["gdn_norm_w"], a["dsw_norm_w"], a["sb_norm_w"]], 1)
    rows = np.concatenate([a["a_log"].ravel(), a["dt_bias"].ravel(), heads.ravel()])

    given = dict(x=a["x"][0], stream=stream, experts=experts.reshape(NE * per_load, P, SLOT), columns=columns,
                 rows=np.broadcast_to(rows, (P, NROW)), final_w=np.broadcast_to(a["final_norm_w"], (P, D)),
                 consts=shape_constants())
    nc = bacc.Bacc("TRN2", target_bir_lowering=False, num_devices=1)
    arrays, args = {}, {}
    for name, v in given.items():
        v = np.ascontiguousarray(v)
        arrays[f"in_{name}"] = v
        args[name] = nc.dram_tensor(f"in_{name}", v.shape, mybir.dt.from_np(v.dtype), kind="ExternalInput").ap()
    out = nc.dram_tensor("out", (T, D), F32, kind="ExternalOutput").ap()
    build(nc, out=out, **args)
    r = run_bass_kernel_spmd(nc, [arrays], core_ids=[0])
    return r.results[0]["out"].reshape(1, T, D)
```

```python
from contextlib import ExitStack

import numpy as np

import concourse.bass as bass
from concourse import mybir

ALU = mybir.AluOpType
ACT = mybir.ActivationFunctionType
F32 = mybir.dt.float32
F32R = mybir.dt.float32r
I32 = mybir.dt.int32
AX_X = mybir.AxisListType.X

P = 128
T, D = 256, 1024
NB = T // P
KC = D // P
DEPTH = 2
HD = 64
HG, HW, HS = 6, 6, 4
DG, DW, DS = HG * HD, HW * HD, HS * HD
CONV = 4
FF = 2816
NF = FF // P
NE, TOPK, MFF = 8, 2, 3584
NJ = MFF // 512
PLE = 256
EPS = 1e-6
SCALE = HD ** -0.5
SLOPES = [2.0 ** (-8.0 * (i + 1.0) / HW) for i in range(HW)]
WINDOWS = ((128, 1), (512, 4), (2048, 16))
FAR = -1e30
MORE = T * TOPK // (P + 1)
NI = NE + MORE + 1
RING = 6
LEAD = 4
SLOT = 2048
NG = -(-NF // 4)
GS, GW = 4, 384
NLEV = 7
CQ = 9
CA = 10


class Count:

    def __init__(self, sem):
        self.sem, self.k, self.items = sem, 0, None

    def up(self):
        self.k += 1
        return 1

    @property
    def n(self):
        return self.k if self.items is None else self.items + self.k


class Tiles:

    def __init__(self):
        self.at, self.filled, self.drained, self.last, self.phase = {}, 0, {"v": 0, "a": 0}, {}, "before"

    def add(self, key, bank, who):
        self.filled += 1
        for w in who:
            self.drained[w] += 1
        before = self.last.get(bank)
        self.at[key] = dict(bank=bank, filled=self.filled, before=before, phase=self.phase,
                            back=int(self.phase == "after" and before["phase"] == "round"),
                            drained={w: self.drained[w] for w in who})
        self.last[bank] = self.at[key]


def system_at(k, b):
    n = GW * (2 * (k % 2) + b) + P * (k // 2)
    return slice(n, n + P)


def group_heads(g):
    return [(2 * q + g // 2, g % 2, P * q) for q in range(3)]


def norm_tiles(t, occ):
    for c in range(4):
        t.add(("T", occ, c), c, "av")


def mixer_tiles(t, L):
    n = [0]

    def add(key, who):
        t.add(key, n[0] % 8, who)
        n[0] += 1

    norm_tiles(t, 3 * L)
    for b in range(NB):
        add(("J", L, b, 0), "a")
    for c in range(10):
        add(("I", L, c), "va"[c % 2])
    for g in (1, 2):
        for b in range(NB):
            add(("J", L, b, g), "a")
    add(("G", L), "v")
    for g in range(GS):
        add(("R", L, g), "v")
    for c in range(3):
        add(("N2", L, c), "a")
    for c in range(3):
        add(("V", L, c), "aav"[c])
    for kind in ("KK", "QK", "C0"):
        for g in range(GS):
            add((kind, L, g), "v")
    for lev in range(1, NLEV):
        for g in range(GS):
            add(("P", L, lev, g), "a")
        for g in range(GS):
            if lev < NLEV - 1:
                add(("X", L, lev, g), "v")
            add(("Y", L, lev, g), "v")
    for key, who in (("W0", "v"), ("S", "a"), ("KS0", "v"), ("KS1", "v"), ("QS0", "a"), ("QS1", "a"), ("W1", "v"), ("O0", "a"),
                     ("O1", "v")):
        add((key, L), who)
    for kind, who, heads in (("D", "v", HW), ("E", "a", HW), ("F", "v", HW), ("Z", "a", HS), ("CS", "v", HS)):
        for k in range(heads):
            add((kind, L, k), who)
    add(("U", L), "a")
    for c in range(4):
        add(("OT", L, c), "av")
    for m in range(2):
        for b in range(NB):
            add(("WO", L, b, m), "v")


def ple_tiles(t, L):
    for m in range(2):
        for b in range(NB):
            t.add(("PP", L, b, m), 4 + 2 * m + b, "v")
    for m in range(2):
        for b in range(NB):
            t.add(("PG", L, b, m), 2 * m + b, "a")


def gather_tiles(t, when):
    t.add(("GA", when, 0), 2, "av")
    t.add(("GA", when, 1), 3, "av")


def round_tiles(t, last):
    ph = "last" if last else "each"
    for j in range(1, NJ):
        t.add(("A", ph, j), 2 * (j % 2), "a")
        t.add(("TT", ph, j - 1), 6 + (j - 1) % 2, "av")
        if j == NJ - 1 and not last:
            gather_tiles(t, ph)
        t.add(("B", ph, j), 2 * (j % 2) + 1, "v")
    t.add(("TT", ph, NJ - 1), 6 + (NJ - 1) % 2, "av")
    if not last:
        t.add(("A", ph, 0), 0, "a")
    for m in range(2):
        t.add(("YY", ph, m), 4 + m, "a")
    if not last:
        t.add(("B", ph, 0), 1, "v")
    for m, b, bank in ((0, 0, 2), (0, 1, 6), (1, 0, 7), (1, 1, 3)):
        t.add(("SC", ph, b, m), bank, "v")
    if not last:
        t.add(("GT", ph), 0, "a")


def plan_tiles():
    t = Tiles()
    mixer_tiles(t, 0)
    norm_tiles(t, 1)
    for f in range(NF):
        t.add(("H", f), f % 4, "av")
    for m in range(2):
        for b in range(NB):
            t.add(("Y2", b, m), 4 + 2 * b + m, "v")
    norm_tiles(t, 2)
    ple_tiles(t, 0)
    mixer_tiles(t, 1)
    norm_tiles(t, 4)
    t.add(("LG",), 4, "v")
    t.add(("POS",), 5, "v")
    gather_tiles(t, "first")
    t.add(("A", "first", 0), 0, "a")
    t.add(("GT", "first"), 6, "a")
    t.add(("B", "first", 0), 1, "v")
    t.base_filled, t.base = t.filled, dict(t.drained)
    t.phase = "round"
    round_tiles(t, False)
    per_fill = t.filled - t.base_filled
    per_drain = {w: t.drained[w] - t.base[w] for w in "va"}
    for tile in t.at.values():
        if tile["phase"] == "round" and tile["before"]["phase"] == "before":
            tile["before"], tile["back"] = t.last[tile["bank"]], 1
    t.filled, t.drained, t.phase = t.base_filled, dict(t.base), "after"
    round_tiles(t, True)
    norm_tiles(t, 5)
    ple_tiles(t, 1)
    return t, per_fill, per_drain


def plan_loads(tiles):
    order, until, turn = [], {}, {}
    early = [0]

    def add(key, tile, signal=False, behind=None):
        order.append(key)
        if signal:
            early[0] += 1
            until[key] = ("signal", early[0])
        else:
            until[key] = ("tile", tile)
        turn[key] = tiles.at[behind or tile]["filled"]

    for L in range(DEPTH):
        add(("J", L, 0, 0), ("J", L, 1, 0), signal=True)
        add(("J", L, 0, 1), ("J", L, 1, 0))
        for c in range(10):
            add(("I", L, c), ("I", L, c))
        for g in (1, 2):
            add(("J", L, g, 0), ("J", L, 1, g), signal=True)
            add(("J", L, g, 1), ("J", L, 1, g))
        for m in range(2):
            add(("WO", L, m, 0), ("WO", L, 1, m), signal=True)
            add(("WO", L, m, 1), ("WO", L, 1, m))
        if L == 0:
            for f in range(NF):
                add(("w13", f), ("H", f))
                if f % 2 and f < NF - 1:
                    add(("w2", f // 2), ("H", f + 1), signal=True)
            add(("w2", NF // 2 - 1), ("Y2", 1, 1))
            ple_loads(add, 0)

    def group(ph, j, kinds="AB"):
        for kind in kinds:
            add((kind, ph, j, 0), (kind, ph, j), signal=True)
            add((kind, ph, j, 1), (kind, ph, j))

    def rest_of_item(ph):
        for j in range(1, NJ):
            group(ph, j)
            for half in range(2):
                add(("C", ph, j - 1, half), ("B", ph, j), signal=True)
        if ph == "each":
            group(ph, 0, "A")
        add(("C", ph, NJ - 1, 0), ("YY", ph, 0), signal=True)
        add(("C", ph, NJ - 1, 1), ("YY", ph, 1))
        if ph == "each":
            group(ph, 0, "B")

    group("first", 0)
    before, signals = len(order), early[0]
    rest_of_item("each")
    each = order[before:]
    per_signal = early[0] - signals
    del order[before:]
    early[0] = signals
    rest_of_item("last")
    last = len(order) - before
    ple_loads(add, 1)
    after = order[before:]
    return dict(before=order[:before], each=each, after=after, last=last, until=until, turn=turn,
                per_signal=per_signal)


def expert_place(key):
    kind, _, j, half = key
    return 4 * NJ + 2 * j + half if kind == "C" else 4 * j + 2 * (kind == "B") + half


def ple_loads(add, L):
    add(("PT", L), ("PP", L, 1, 1))
    add(("PP", L), ("PP", L, 1, 1))
    for m in range(2):
        add(("PG", L, m, 0), ("PG", L, 1, m), signal=True)
        add(("PG", L, m, 1), ("PG", L, 1, m))


CONSTS = {}
_at = 0
for _name, _w in (("ident", P), ("ones", P), ("upto", P), ("before", P), ("from", P), ("headsum", P), ("slots", P),
                  ("levels", NLEV * P), ("dist", 384), ("mult", 384), ("earlier", 384), ("lower8", NE * NE),
                  ("expert", NE), ("item", MORE + 1), ("eps", 1)):
    CONSTS[_name] = (_at, _w)
    _at += _w
NCONST = _at


def shape_constants():
    c = np.zeros((P, NCONST), np.float32)
    i = np.arange(P)

    def put(name, value):
        a, w = CONSTS[name]
        c[:, a:a + w] = np.asarray(value, np.float32).reshape(-1, w)

    put("ident", np.eye(P))
    put("ones", np.ones((P, P)))
    put("upto", i[:, None] <= i[None, :])
    put("before", i[:, None] < i[None, :])
    put("from", i[:, None] >= i[None, :])
    put("headsum", i[:, None] // HD == i[None, :] // HD)
    put("slots", np.tile(i, (P, 1)))
    lev = []
    for s in range(NLEV):
        w = 1 << s
        same = i[:, None] // (2 * w) == i[None, :] // (2 * w)
        lev.append(same & (i[:, None] // w % 2 == 0) & (i[None, :] // w % 2 == 1))
    put("levels", np.concatenate(lev, 1))
    q = np.concatenate([i[:, None] - i[None, :], P + i[:, None] - np.arange(T)[None, :]], 1)
    m = sum((q >= 0) & (q <= window) & (q % r == 0) for window, r in WINDOWS)
    put("dist", np.where(m > 0, -q, FAR))
    put("mult", m)
    b = i[:, None] < i[None, :]
    put("earlier", np.concatenate([b, np.ones((P, P)), b], 1))
    put("lower8", np.tile((np.arange(NE)[None, :] < np.arange(NE)[:, None]).reshape(1, -1), (P, 1)))
    put("expert", np.tile(np.arange(NE), (P, 1)))
    put("item", np.tile(np.arange(MORE + 1), (P, 1)))
    put("eps", np.full((P, 1), EPS))
    return c


COL_NORM = lambda occ: occ * KC
COL_CONV = 3 * DEPTH * KC
COL_ROUTER = COL_CONV + DEPTH * CQ * CONV
NCOL = COL_ROUTER + KC * NE
ROW_ALOG, ROW_DT = 0, DEPTH * HG
ROW_HN = lambda L, i: 2 * DEPTH * HG + (L * 3 + i) * HD
NROW = 2 * DEPTH * HG + DEPTH * 3 * HD


def build(nc, x, stream, experts, columns, rows, final_w, consts, out):
    tiles, per_fill, per_drain = plan_tiles()
    plan = plan_loads(tiles)
    n_before, per_load, per_signal = len(plan["before"]), len(plan["each"]), plan["per_signal"]
    in_round, after = plan["before"] + plan["each"], plan["before"] + plan["after"]
    load_at = {key: n for order in (in_round, after) for n, key in enumerate(order)}
    assert per_load % RING == 0
    laps = per_load // RING
    n_stream = n_before - 4

    with ExitStack() as ctx:
        def sb(name, shape, dt=F32):
            return ctx.enter_context(nc.sbuf_tensor(name, shape, dt))

        def sem(name):
            return ctx.enter_context(nc.semaphore(name))

        ps = ctx.enter_context(nc.psum_tensor("ps", [P, 8, 512], F32))
        with nc.sbuf_tensor("raw", [P, RING, SLOT], F32) as raw:
            pass
        wlo = sb("wlo", [P, RING, SLOT], F32R)
        whi = sb("whi", [P, RING, SLOT], F32R)
        cst = sb("cst", [P, NCONST])
        cols = sb("cols", [P, NCOL])
        rws = sb("rws", [P, NROW])
        h = sb("h", [P, NB, D])
        hn = sb("hn", [P, NB, D])
        xh = sb("xh", [P, KC * T], F32R)
        xl = sb("xl", [P, KC * T], F32R)
        gh = sb("gh", [P, 2, T], F32R)
        gl = sb("gl", [P, 2, T], F32R)
        table = sb("table", [1, 8], I32)

        sizes = dict(xc=CQ * (T + 3) + 1, qkv=CQ * T, att=CA * T, z=NB * DG, dva=NB * HW * (HD + 1), sva=NB * DS,
                     dec=1536, mt=1536, xt=1536, xi=1536, ab=24, em=30, lnp=12, beta=12, g=12, gc=18, xa=12,
                     e1=24, gx=12, eg=12, ss=64, rs=68, mx=12, nm=12, rden=12)
        off, place = 0, {}
        for k, w in sizes.items():
            place[k] = (off, w)
            off += w
        work = sb("work", [P, off])

        def area(name, start=0, width=None):
            a, w = place[name]
            return work[:, a + start:a + start + (w - start if width is None else width)]

        def cc(name, start=0, width=None):
            a, w = CONSTS[name]
            return cst[:, a + start:a + start + (w - start if width is None else width)]

        def col(n):
            return cols[:, n:n + 1]

        ident, ones = cc("ident"), cc("ones")

        xc = area("xc", 0, CQ * (T + 3)).rearrange("p (c t) -> p c t", c=CQ)
        qkv = area("qkv").rearrange("p (c t) -> p c t", c=CQ)
        att = area("att").rearrange("p (c t) -> p c t", c=CA)
        zt = area("z").rearrange("p (b c) -> p b c", b=NB)
        dva = area("dva").rearrange("p (b h e) -> p b h e", b=NB, h=HW)
        sva = area("sva").rearrange("p (b c) -> p b c", b=NB)
        ab = area("ab").rearrange("p (b c) -> p b c", b=NB)
        squares = area("xc", 0, 1536)
        pbuf = area("xc", 0, 1536)
        vt = area("xc", 1536, NB * DG).rearrange("p (b c) -> p b c", b=NB)
        dec, mt, xt, xi = area("dec"), area("mt"), area("xt"), area("xi")
        hn_flat = hn[:, :, :].rearrange("p b c -> p (b c)")
        cm = hn_flat[:, 0:1536]
        kd = hn_flat[:, 1536:1536 + DG]
        vn = area("mt", 0, NB * DG).rearrange("p (b c) -> p b c", b=NB)
        s1 = area("mt", 768, 192)
        rr = area("mt", 960, DG)
        qs = area("xc", 0, DG)
        o = hn
        a0 = place["dec"][0]
        prob = work[:, a0:a0 + HW * 384].rearrange("p (h s) -> p h s", h=HW)
        probT = work[:, a0 + HW * 384:a0 + 2 * HW * 384].rearrange("p (h s) -> p h s", h=HW)
        zs = area("xi", 0, HS * 384).rearrange("p (h s) -> p h s", h=HS)
        es = area("xc", 0, HS * 384).rearrange("p (h s) -> p h s", h=HS)
        sps = area("qkv", 0, HS * 384).rearrange("p (h s) -> p h s", h=HS)
        osq = area("qkv", 0, NB * D)

        def part(start, width):
            return work[:, start:start + width]

        ffs = [part(256 * i, 256) for i in range(2)]
        ffp = [part(512 + 256 * i, 256) for i in range(2)]
        sig = [part(512 * i, 512) for i in range(2)]
        sgp = [part(1024 + 512 * i, 512) for i in range(2)]
        ms = [part(512 * i, 512) for i in range(2)]
        mg = [part(1024 + 512 * i, 512) for i in range(2)]
        mTh, mTl = ([x[:, 1024 + 512 * i:1536 + 512 * i] for i in range(2)] for x in (xh, xl))
        pick = part(4096, 256).rearrange("p (b s) -> p b s", b=NB)
        pickg = part(4352, 256).rearrange("p (b s) -> p b s", b=NB)
        back = part(4608, 256)
        ysb = part(4864, 1024)
        R0 = 5888
        lg = part(R0, 16).rearrange("p (b e) -> p b e", b=NB)
        top = part(R0 + 16, 2)
        den = part(R0 + 18, 2)
        over = part(R0 + 20, 8)
        oidx = part(R0 + 28, 8)
        rank = part(R0 + 36, 16).rearrange("p (b e) -> p b e", b=NB)
        sel = part(R0 + 52, 16).rearrange("p (b e) -> p b e", b=NB)
        gate = part(R0 + 68, 16).rearrange("p (b e) -> p b e", b=NB)
        exl = part(R0 + 84, 16).rearrange("p (b e) -> p b e", b=NB)
        cum = part(R0 + 100, 24)
        pos1 = part(R0 + 124, 16).rearrange("p (b e) -> p b e", b=NB)
        tabf = part(R0 + 140, 8)
        posi = part(R0 + 148, NB * NI).rearrange("p (b i) -> p b i", b=NB)
        gati = part(R0 + 148 + NB * NI, NB * NI).rearrange("p (b i) -> p b i", b=NB)
        pairs = [part(R0 + 200 + 128 * i, 128).rearrange("p (b e f) -> p b e f", b=NB, e=NE) for i in range(2)]
        osel = part(R0 + 456, (MORE + 1) * NE).rearrange("p (r e) -> p r e", e=NE)
        oprd = part(R0 + 456 + 32, 5 * (MORE + 1) * NE).rearrange("p (a r e) -> p a r e", a=5, e=NE)
        assert R0 + 456 + 192 <= place["z"][0]
        f0 = place["dec"][0]
        finw = part(f0, D)
        res = part(f0 + D, NB * D).rearrange("p (b c) -> p b c", b=NB)

        s_in = sem("inputs_landed")
        s_fw = sem("final_weight_landed")
        s_land = [sem(f"weights_landed_{i}") for i in range(RING)]
        s_fill = sem("psum_filled")
        s_used = sem("weights_used_within_a_tile")
        s_hi, s_lo = sem("weights_upper_part_ready"), sem("weights_split")
        s_free = {"v": sem("psum_drained_by_vector"), "a": sem("psum_drained_by_scalar")}
        s_out = sem("output_written")
        s_vstep, s_astep, s_pstep = sem("vector_step"), sem("scalar_step"), sem("gpsimd_step")
        s_sumsq, s_rstd = sem("row_squares_summed"), sem("row_rstd_ready")
        s_hn = {"v": sem("hn_block1_ready"), "a": sem("hn_block0_ready")}
        s_gin, s_gexp = sem("gate_arguments_ready"), sem("gate_exponentials_ready")
        s_gadd, s_gln, s_g = sem("exponentials_plus_one"), sem("softplus_logs_ready"), sem("gates_ready")
        s_gx, s_eg = sem("summed_gate_arguments_ready"), sem("summed_gate_exponentials_ready")
        s_dexp, s_dec = sem("decays_ready"), sem("decays_masked")
        s_conv, s_silu = sem("convolved"), sem("convolved_silu_ready")
        s_sq, s_qk = sem("qk_squares_ready"), sem("qk_normalised")
        s_cm, s_rr = sem("level_blocks_ready"), sem("chunk1_right_side_ready")
        s_qs = sem("q_state_decayed")
        s_nm, s_dex, s_dpr = sem("window_max_ready"), sem("window_exponentials_ready"), sem("window_weights_ready")
        s_zl, s_sps = sem("stick_logs_ready"), sem("stick_softplus_ready")
        s_ze, s_aT = sem("stick_exponentials_ready"), sem("stick_weights_ready")
        s_zg, s_oss, s_ors, s_o = sem("silu_z_ready"), sem("head_squares_summed"), sem("head_rstd"), sem("mixed_ready")
        s_ple = sem("ple_added")
        s_ffg = sem("dense_product_split")
        s_lsub, s_lex = sem("router_logits_shifted"), sem("router_exponentials_ready")
        s_sel, s_tab, s_pick = sem("experts_selected"), sem("item_table_ready"), sem("item_selection_ready")
        s_res = sem("result_ready")

        def bank(key, start=0, width=512):
            return ps[:, tiles.at[key]["bank"], start:start + width]

        def through(count, it, per):
            return count if it is None else it * per + count

        def filled(eng, key, it=None, back=0):
            eng.wait_ge(s_fill, through(tiles.at[key]["filled"] - back * per_fill, it, per_fill))

        def drained(eng, key, who, it=None, back=0):
            eng.wait_ge(s_free[who], through(tiles.at[key]["drained"][who] - back * per_drain[who], it, per_drain[who]))

        class Split:

            def __init__(self, one):
                self.one, self.next, self.end, self.order = one, 0, n_before + LEAD, in_round

            def in_round(self):
                assert self.next == n_before + LEAD
                self.end = n_before + per_load + LEAD

            def after(self):
                assert self.next == self.end
                self.next, self.end, self.order = n_before + LEAD, len(after), after

            def behind(self, key, it=None):
                now = tiles.at[key]["filled"]
                while self.next < self.end and (self.next < LEAD or plan["turn"][self.order[self.next - LEAD]] <= now):
                    self.one(self.next, it)
                    self.next += 1

        def split_upper(n, it):
            nc.scalar.wait_ge(s_land[n % RING], through(16 * (n // RING + 1), it, 16 * laps))
            nc.scalar.copy(whi[:, n % RING, :], raw[:, n % RING, :]).then_inc(s_hi, 1)

        def split_lower(n, it):
            nc.vector.wait_ge(s_hi, through(n + 1, it, per_load))
            nc.vector.tensor_tensor(wlo[:, n % RING, :], raw[:, n % RING, :], whi[:, n % RING, :].bitcast(F32),
                                    ALU.subtract).then_inc(s_lo, 1)

        def ready(eng, key, it=None):
            eng.wait_ge(s_lo, through(load_at[key] + 1, it, per_load))

        def weights(key, start, width):
            n = load_at[key] % RING
            return whi[:, n, start:start + width], wlo[:, n, start:start + width]

        block = ctx.enter_context(nc.Block())

        @block.sync
        def _(sp):
            sp.dma_start(h[:, :, :], x.rearrange("(b p) c -> p b c", p=P)).then_inc(s_in, 16)
            sp.dma_start(cst[:, :], consts).then_inc(s_in, 16)
            sp.dma_start(cols[:, :], columns).then_inc(s_in, 16)
            sp.dma_start(rws[:, :], rows).then_inc(s_in, 16)

            def load(src, order, n, it=None):
                if n >= RING:
                    kind, what = plan["until"][order[n - RING]]
                    if kind == "tile":
                        filled(sp, what, it)
                    else:
                        sp.wait_ge(s_used, through(what, it, per_signal))
                sp.dma_start(raw[:, n % RING, :], src).then_inc(s_land[n % RING], 16)

            def expert_slot(e, key):
                return experts[bass.ds(e * per_load + expert_place(key), 1), :, :].rearrange("a p f -> (a p) f")

            def of_round(e, following, it):
                for k in range(RING, per_load + RING):
                    key = plan["each"][k % per_load]
                    of_next = k >= per_load or key[0] in "AB" and key[2] == 0
                    load(expert_slot(following if of_next else e, key), in_round + plan["each"], n_before + k, it)

            for n in range(n_before + RING):
                key = (in_round)[n]
                load(experts[expert_place(key)] if n >= n_stream else stream[n], in_round, n)
            with sp.Fori(0, NE - 1) as e:
                of_round(e, e + 1, e)
            sp.wait_ge(s_tab, 1)
            more = sp.value_load(table[0:1, MORE + 2:MORE + 3], min_val=0, max_val=MORE)
            with sp.If(more > 0):
                with sp.Fori(0, more) as r:
                    e = sp.value_load(table[0:1, bass.ds(r, 1)], min_val=0, max_val=NE - 1)
                    following = sp.value_load(table[0:1, bass.ds(r + 1, 1)], min_val=0, max_val=NE - 1)
                    of_round(e, following, r + NE - 1)
            e = sp.value_load(table[0:1, bass.ds(more, 1)], min_val=0, max_val=NE - 1)
            for k in range(RING, len(plan["after"])):
                key = plan["after"][k]
                load(expert_slot(e, key) if k < plan["last"] else stream[n_stream + k - plan["last"]], after,
                     n_before + k, more + NE - 1)
            filled(sp, ("WO", 1, 1, 1))
            sp.dma_start(finw, final_w).then_inc(s_fw, 16)
            sp.wait_ge(s_res, NB)
            sp.dma_start(out.rearrange("(b p) c -> p b c", p=P), res).then_inc(s_out, 16)
            sp.wait_ge(s_out, 16)

        @block.gpsimd
        def _(pool):
            st = Count(s_pstep)

            def rstd(occ):
                pool.wait_ge(s_sumsq, NB * (occ + 1))
                nc.gpsimd.tensor_scalar(area("rs", 66, 2), area("rs", 64, 2), 1.0 / D, EPS, ALU.mult,
                                        ALU.add).then_inc(st.sem, st.up())
                pool.wait_ge(st.sem, st.n)
                nc.gpsimd.tensor_tensor(area("mx", 10, 2), area("rs", 66, 2), area("rs", 32, 2), ALU.pow).then_inc(s_rstd, 1)

            def mixers(L):
                rstd(3 * L)
                for g in range(GS):
                    pool.wait_ge(s_dexp, GS * L + g + 1)
                    d = dec[:, GW * g:GW * g + GW].rearrange("p (s i) -> p s i", s=3)
                    nc.gpsimd.tensor_tensor(d, d, cc("upto").unsqueeze(1).broadcast_to([P, 3, P]),
                                            ALU.mult).then_inc(s_dec, 1)
                for lev in range(NLEV):
                    for g in range(GS):
                        if lev == 0:
                            drained(pool, ("KK", L, g), "v")
                        elif lev == 1:
                            drained(pool, ("C0", L, g), "v")
                        else:
                            filled(pool, ("P", L, lev - 1, g))
                        m = cc("levels", lev * P, P).unsqueeze(1).broadcast_to([P, 3, P])
                        nc.gpsimd.tensor_tensor(cm[:, GW * g:GW * g + GW].rearrange("p (s i) -> p s i", s=3),
                                                mt[:, GW * g:GW * g + GW].rearrange("p (s i) -> p s i", s=3),
                                                m, ALU.mult).then_inc(s_cm, 1)
                pool.wait_ge(s_oss, L + 1)
                nc.gpsimd.tensor_scalar(area("ss", 32, 32), area("ss", 0, 32), 1.0 / HD, EPS, ALU.mult,
                                        ALU.add).then_inc(st.sem, st.up())
                pool.wait_ge(st.sem, st.n)
                nc.gpsimd.tensor_tensor(area("rs", 0, 32), area("ss", 32, 32), area("rs", 32, 32),
                                        ALU.pow).then_inc(s_ors, 1)

            nc.gpsimd.memset(area("rs", 32, 32), -0.5).then_inc(st.sem, st.up())
            pool.wait_ge(st.sem, st.n)
            pool.wait_ge(s_in, 64)
            mixers(0)
            rstd(1)
            rstd(2)
            mixers(1)
            rstd(4)
            rstd(5)
            rstd(6)

        def residual_ready(eng, occ, items):
            if occ in (1, 4):
                drained(eng, ("WO", occ // 3, 1, 1), "v")
            elif occ == 2:
                drained(eng, ("Y2", 1, 1), "v")
            elif occ == 5:
                drained(eng, ("SC", "last", 1, 1), "v", items)
            elif occ in (3, 6):
                eng.wait_ge(s_ple, 4 * (occ // 3))

        @block.scalar
        def _(act):
            st = Count(s_astep)
            split = Split(split_upper)

            def norm(occ, items=None):
                if occ == 0:
                    act.wait_ge(s_in, 64)
                else:
                    residual_ready(act, occ, items)
                for b in range(NB):
                    nc.scalar.activation(hn[:, b, :], h[:, b, :], ACT.Square,
                                         accum_out=area("rs", 64 + b, 1)).then_inc(s_sumsq, 1)
                if occ == 6:
                    return
                act.wait_ge(s_rstd, occ + 1)
                nc.scalar.activation(hn[:, 0, :], h[:, 0, :], ACT.Copy,
                                     scale=area("mx", 10, 1)).then_inc(s_hn["a"], 1)
                for c in range(4):
                    key = ("T", occ, c)
                    filled(act, key, items)
                    for k in (2 * c, 2 * c + 1):
                        ins = nc.scalar.activation(xh[:, T * k:T * k + T], bank(key, T * (k % 2), T), ACT.Copy,
                                                   scale=col(COL_NORM(occ) + k))
                    ins.then_inc(s_free["a"], 1)

            def token_major(L, g):
                for b in range(NB):
                    key = ("J", L, b, g)
                    filled(act, key)
                    if g == 0:
                        nc.scalar.copy(zt[:, b, :], bank(key, 0, DG))
                        ins = nc.scalar.copy(ab[:, b, :], bank(key, DG, 2 * HG))
                    elif g == 1:
                        ins = nc.scalar.copy(dva[:, b, :, 0:HD], bank(key, 0, DW).rearrange("p (h e) -> p h e", h=HW))
                    else:
                        ins = nc.scalar.copy(sva[:, b, :], bank(key, 0, DS))
                    ins.then_inc(s_free["a"], 1)
                split.behind(key)

            def mixers(L):
                norm(3 * L)
                if L == 0:
                    split.behind(("T", 0, 3))
                token_major(L, 0)
                for t in range(10):
                    if t % 2 == 0:
                        split.behind(("I", L, t))
                        continue
                    filled(act, ("I", L, t))
                    for c in (2 * t, 2 * t + 1):
                        if c < CQ + CA:
                            dst = xc[:, c, 3:3 + T] if c < CQ else att[:, c - CQ, :]
                            ins = nc.scalar.copy(dst, bank(("I", L, t), T * (c % 2), T))
                    ins.then_inc(s_free["a"], 1)
                    split.behind(("I", L, t))
                token_major(L, 1)
                token_major(L, 2)
                act.wait_ge(s_gin, L + 1)
                nc.scalar.activation(area("em"), area("em"), ACT.Exp).then_inc(s_gexp, 1)
                act.wait_ge(s_gadd, L + 1)
                nc.scalar.activation(area("lnp"), area("e1", 0, 12), ACT.Ln).then_inc(s_gln, 1)
                act.wait_ge(s_gx, L + 1)
                nc.scalar.activation(area("eg"), area("gx"), ACT.Exp).then_inc(s_eg, 1)
                for g in range(GS):
                    drained(act, ("R", L, g), "v")
                    d = dec[:, GW * g:GW * g + GW]
                    nc.scalar.activation(d, d, ACT.Exp).then_inc(s_dexp, 1)
                for j in range(3):
                    act.wait_ge(s_conv, CQ * L + 3 * j + 3)
                    v = qkv[:, 3 * j:3 * j + 3, :]
                    nc.scalar.activation(v, v, ACT.Silu).then_inc(s_silu, 1)
                drained(act, ("J", L, 1, 0), "a")
                nc.scalar.activation(area("z"), area("z"), ACT.Silu).then_inc(s_zg, 1)
                for c in range(3):
                    filled(act, ("N2", L, c))
                    nc.scalar.activation(pbuf[:, 512 * c:512 * c + 512], bank(("N2", L, c)), ACT.Sqrt,
                                         bias=cc("eps")).then_inc(s_free["a"], 1)
                for b in range(NB):
                    filled(act, ("V", L, b))
                    nc.scalar.copy(vt[:, b, :], bank(("V", L, b), 0, DG)).then_inc(s_free["a"], 1)
                for lev in range(1, NLEV):
                    for g in range(GS):
                        filled(act, ("P", L, lev, g))
                        if lev == 1:
                            act.wait_ge(s_qk, 3 * L + 3)
                        else:
                            filled(act, ("Y", L, lev - 1, g))
                        nc.scalar.copy(pbuf[:, GW * g:GW * g + GW],
                                       bank(("P", L, lev, g), 0, GW)).then_inc(s_free["a"], 1)
                filled(act, ("S", L))
                nc.scalar.copy(s1, bank(("S", L), 0, 192)).then_inc(s_free["a"], 1)
                for parity in range(2):
                    key = (f"QS{parity}", L)
                    filled(act, key)
                    for k in range(parity, HG, 2):
                        ins = nc.scalar.activation(qs[:, k * HD:k * HD + HD], bank(key, k // 2 * HD, HD), ACT.Copy,
                                                   scale=area("eg", k, 1))
                    ins.then_inc(s_free["a"], 1)
                filled(act, ("O0", L))
                nc.scalar.copy(o[:, 0, 0:DG], bank(("O0", L), 0, DG)).then_inc(s_free["a"], 1)
                for k in range(HW):
                    act.wait_ge(s_nm, HW * L + k + 1)
                    for b in range(NB):
                        v = prob[:, k, 0:P] if b == 0 else prob[:, k, P:384]
                        ins = nc.scalar.activation(v, v, ACT.Exp, scale=SCALE, bias=area("nm", 2 * k + b, 1))
                    ins.then_inc(s_dex, 1)
                for k in range(HW):
                    filled(act, ("E", L, k))
                    nc.scalar.copy(probT[:, k, :], bank(("E", L, k), 0, 384)).then_inc(s_free["a"], 1)
                drained(act, ("O1", L), "v")
                for k in range(HS):
                    filled(act, ("Z", L, k))
                    nc.scalar.mul(zs[:, k, :], bank(("Z", L, k), 0, 384), SCALE).then_inc(s_free["a"], 1)
                drained(act, ("Z", L, HS - 1), "a")
                nc.scalar.activation(es, zs, ACT.Abs).then_inc(st.sem, st.up())
                act.wait_ge(st.sem, st.n)
                nc.scalar.activation(es, es, ACT.Exp, scale=-1.0).then_inc(st.sem, st.up())
                act.wait_ge(st.sem, st.n)
                nc.scalar.activation(es, es, ACT.Ln, bias=1.0).then_inc(s_zl, 1)
                for k in range(HS):
                    drained(act, ("CS", L, k), "v")
                    nc.scalar.activation(zs[:, k, :], zs[:, k, :], ACT.Exp).then_inc(s_ze, 1)
                filled(act, ("U", L))
                nc.scalar.copy(o[:, :, DG + DW:D],
                               bank(("U", L)).rearrange("p (b c) -> p b c", b=NB)).then_inc(s_free["a"], 1)
                for c in range(4):
                    filled(act, ("OT", L, c))
                    nc.scalar.copy(xh[:, 512 * c:512 * c + 512], bank(("OT", L, c))).then_inc(s_free["a"], 1)
                split.behind(("WO", L, 1, 1))

            def ple(L, items=None):
                split.behind(("PP", L, 1, 1), items)
                for m in range(2):
                    for b in range(NB):
                        key = ("PG", L, b, m)
                        filled(act, key, items)
                        if m:
                            drained(act, ("PP", L, b, 0), "v", items)
                        nc.scalar.activation(sig[b], bank(key), ACT.Sigmoid).then_inc(s_free["a"], 1)
                    split.behind(key, items)

            mixers(0)
            norm(1)
            for f in range(NF):
                filled(act, ("H", f))
                if f >= 2:
                    drained(act, ("H", f - 2), "v")
                nc.scalar.activation(ffs[f % 2], bank(("H", f), 0, T), ACT.Silu).then_inc(s_free["a"], 1)
                split.behind(("H", f))
            split.behind(("Y2", 1, 1))
            norm(2)
            ple(0)
            mixers(1)
            norm(4)
            act.wait_ge(s_lsub, 1)
            nc.scalar.activation(exl, exl, ACT.Exp).then_inc(s_lex, 1)

            def gathered(when, it):
                if when == "each":
                    filled(act, ("B", when, NJ - 1), it)
                for half in range(2):
                    filled(act, ("GA", when, half), it)
                    for q in range(4):
                        k = 4 * half + q
                        ins = nc.scalar.activation(xh[:, P * k:P * k + P], bank(("GA", when, half), P * q, P), ACT.Copy,
                                                   scale=col(COL_NORM(4) + k))
                    ins.then_inc(s_free["a"], 1)

            def scatter_matrix(when, it):
                filled(act, ("GT", when), it)
                nc.scalar.copy(back, bank(("GT", when), 0, T)).then_inc(s_free["a"], 1)

            def silu(ph, j, it):
                key = ("A", ph, j)
                filled(act, key, it)
                nc.scalar.activation(ms[j % 2], bank(key), ACT.Silu).then_inc(s_free["a"], 1)

            def turned(ph, j, it):
                filled(act, ("TT", ph, j), it)
                nc.scalar.copy(mTh[j % 2], bank(("TT", ph, j))).then_inc(s_free["a"], 1)

            def rest_of_item(ph, it):
                for j in range(1, NJ):
                    if j > 2:
                        drained(act, ("B", ph, j - 2), "v", it)
                    elif j == 2:
                        drained(act, ("B", "each", 0), "v", it, 1)
                    silu(ph, j, it)
                    turned(ph, j - 1, it)
                    split.behind(("A", ph, j), it)
                    if j < NJ - 1 or ph == "last":
                        split.behind(("B", ph, j), it)
                if ph == "each":
                    gathered(ph, it)
                    split.behind(("B", ph, NJ - 1), it)
                turned(ph, NJ - 1, it)
                if ph == "each":
                    drained(act, ("B", ph, NJ - 1), "v", it)
                    silu(ph, 0, it)
                    split.behind(("A", ph, 0), it)
                for m in range(2):
                    filled(act, ("YY", ph, m), it)
                    nc.scalar.copy(ysb[:, 512 * m:512 * m + 512], bank(("YY", ph, m))).then_inc(s_free["a"], 1)
                split.behind(("YY", ph, 1), it)
                if ph == "each":
                    scatter_matrix(ph, it)
                    split.behind(("B", ph, 0), it)

            gathered("first", None)
            silu("first", 0, None)
            split.behind(("A", "first", 0))
            scatter_matrix("first", None)
            split.behind(("B", "first", 0))
            drained(act, ("B", "first", 0), "v")
            act.wait_ge(s_tab, 1)
            items = act.value_load(table[0:1, MORE + 3:MORE + 4], min_val=NE - 1, max_val=NE - 1 + MORE)
            split.in_round()
            with act.Fori(0, items) as i:
                rest_of_item("each", i)
            split.after()
            rest_of_item("last", items)
            norm(5, items)
            ple(1, items)
            norm(6)

        @block.vector
        def _(dve):
            st = Count(s_vstep)
            split = Split(split_lower)

            def step():
                dve.wait_ge(st.sem, st.n)

            def norm(occ, items=None):
                dve.wait_ge(s_rstd, occ + 1)
                nc.vector.tensor_scalar(hn[:, 1, :], h[:, 1, :], area("mx", 11, 1), None, ALU.mult).then_inc(s_hn["v"], 1)
                for c in range(4):
                    key = ("T", occ, c)
                    drained(dve, key, "a", items)
                    for k in (2 * c, 2 * c + 1):
                        ins = nc.vector.scalar_tensor_tensor(out=xl[:, T * k:T * k + T], in0=bank(key, T * (k % 2), T),
                                                             scalar=col(COL_NORM(occ) + k),
                                                             in1=xh[:, T * k:T * k + T].bitcast(F32), op0=ALU.mult,
                                                             op1=ALU.subtract)
                    ins.then_inc(s_free["v"], 1)

            def lower_part(key, hi, lo, it=None):
                drained(dve, key, "a", it)
                nc.vector.tensor_tensor(lo, bank(key), hi.bitcast(F32), ALU.subtract).then_inc(s_free["v"], 1)

            def heads(ap, n=HG):
                return ap.rearrange("p (h e) -> p h e", h=n)

            def per_head(ap, n=HG):
                return ap.unsqueeze(2).broadcast_to([P, n, HD])

            def gates(L):
                drained(dve, ("J", L, 1, 0), "a")
                xa = area("xa").rearrange("p (b h) -> p b h", b=NB)
                dt = rws[:, ROW_DT + L * HG:ROW_DT + (L + 1) * HG].unsqueeze(1).broadcast_to([P, NB, HG])
                nc.vector.tensor_tensor(xa, ab[:, :, 0:HG], dt, ALU.add).then_inc(st.sem, st.up())
                nc.vector.tensor_scalar(area("em", 12, 12).rearrange("p (b h) -> p b h", b=NB), ab[:, :, HG:2 * HG], -1.0,
                                        None, ALU.mult).then_inc(st.sem, st.up())
                nc.vector.tensor_copy(area("em", 24, 6), rws[:, ROW_ALOG + L * HG:ROW_ALOG + (L + 1) * HG]).then_inc(
                    st.sem, st.up())
                step()
                nc.vector.scalar_tensor_tensor(out=area("em", 0, 12), in0=area("xa"), scalar=-1.0, in1=area("xa"),
                                               op0=ALU.mult, op1=ALU.min).then_inc(s_gin, 1)
                dve.wait_ge(s_gexp, L + 1)
                nc.vector.tensor_scalar(area("e1"), area("em", 0, 24), 1.0, None, ALU.add).then_inc(s_gadd, 1)
                dve.wait_ge(s_gadd, L + 1)
                nc.vector.reciprocal(area("beta"), area("e1", 12, 12)).then_inc(st.sem, st.up())
                dve.wait_ge(s_gln, L + 1)
                nc.vector.scalar_tensor_tensor(out=area("xa"), in0=area("xa"), scalar=0.0, in1=area("lnp"), op0=ALU.max,
                                               op1=ALU.add).then_inc(st.sem, st.up())
                step()
                ea = area("em", 24, 6).unsqueeze(1).broadcast_to([P, NB, HG])
                nc.vector.scalar_tensor_tensor(out=area("g").rearrange("p (b h) -> p b h", b=NB), in0=xa, scalar=-1.0,
                                               in1=ea, op0=ALU.mult, op1=ALU.mult).then_inc(s_g, 1)

            def decays(L):
                filled(dve, ("G", L))
                nc.vector.tensor_copy(area("gc"), bank(("G", L), 0, 18)).then_inc(s_free["v"], 1)
                drained(dve, ("G", L), "v")
                nc.vector.tensor_copy(area("gx", 0, 6), area("gc", 6, 6)).then_inc(st.sem, st.up())
                nc.vector.tensor_tensor(area("gx", 6, 6), area("gc", 12, 6), area("gc", 0, 6),
                                        ALU.subtract).then_inc(st.sem, st.up())
                step()
                nc.vector.tensor_scalar(area("gx"), area("gx"), 0.0, None, ALU.min).then_inc(s_gx, 1)
                for g in range(GS):
                    filled(dve, ("R", L, g))
                    for k, b, at in group_heads(g):
                        ins = nc.vector.tensor_scalar(dec[:, system_at(k, b)],
                                                      bank(("R", L, g), at, P), area("gc", b * HG + k, 1), 0.0,
                                                      ALU.subtract, ALU.min)
                    ins.then_inc(s_free["v"], 1)

            def convolution(L):
                for tap in range(CONV):
                    for c in range(CQ):
                        if tap == 0:
                            if c % 4 in (2, 3) and c % 2 == 0:
                                drained(dve, ("I", L, c // 2), "a")
                            elif c % 2 == 0:
                                drained(dve, ("I", L, c // 2), "v")
                            w = col(COL_CONV + (L * CQ + c) * CONV)
                            nc.vector.tensor_scalar(qkv[:, c, :], xc[:, c, 0:T], w, None, ALU.mult).then_inc(st.sem, st.up())
                            continue
                        w = col(COL_CONV + (L * CQ + c) * CONV + tap)
                        ins = nc.vector.scalar_tensor_tensor(out=qkv[:, c, :], in0=xc[:, c, tap:tap + T], scalar=w,
                                                             in1=qkv[:, c, :], op0=ALU.mult, op1=ALU.add)
                        if tap < CONV - 1:
                            ins.then_inc(st.sem, st.up())
                        else:
                            ins.then_inc(s_conv, 1)
                    if tap < CONV - 1:
                        step()
                dve.wait_ge(s_silu, 3 * L + 2)
                dve.wait_ge(s_conv, CQ * (L + 1))
                nc.vector.tensor_tensor(squares, area("qkv", 0, 1536), area("qkv", 0, 1536), ALU.mult).then_inc(s_sq, 1)
                for c in range(3):
                    drained(dve, ("N2", L, c), "a")
                    nc.vector.reciprocal(pbuf[:, 512 * c:512 * c + 512],
                                         pbuf[:, 512 * c:512 * c + 512]).then_inc(st.sem, st.up())
                    step()
                    nc.vector.tensor_tensor(area("qkv", 512 * c, 512), area("qkv", 512 * c, 512),
                                            pbuf[:, 512 * c:512 * c + 512], ALU.mult).then_inc(s_qk, 1)

            def delta(L):
                filled(dve, ("V", L, 2))
                dve.wait_ge(s_eg, L + 1)
                nc.vector.tensor_tensor(heads(kd), heads(bank(("V", L, 2), 0, DG)), per_head(area("eg", 6, 6)),
                                        ALU.mult).then_inc(s_free["v"], 1)
                for g in range(GS):
                    filled(dve, ("KK", L, g))
                    dve.wait_ge(s_dec, GS * L + g + 1)
                    for k, b, at in group_heads(g):
                        ins = nc.vector.scalar_tensor_tensor(out=mt[:, system_at(k, b)], in0=bank(("KK", L, g), at, P),
                                                             scalar=area("beta", b * HG + k, 1),
                                                             in1=dec[:, system_at(k, b)], op0=ALU.mult, op1=ALU.mult)
                    ins.then_inc(s_free["v"], 1)
                for g in range(GS):
                    filled(dve, ("QK", L, g))
                    drained(dve, ("KK", L, g), "v")
                    d = dec[:, GW * g:GW * g + GW]
                    nc.vector.scalar_tensor_tensor(out=d, in0=bank(("QK", L, g), 0, GW), scalar=SCALE, in1=d, op0=ALU.mult,
                                                   op1=ALU.mult).then_inc(s_free["v"], 1)
                eye = ident.unsqueeze(1).broadcast_to([P, 3, P])

                def systems(ap):
                    return ap.rearrange("p (s i) -> p s i", s=3)

                for g in range(GS):
                    at = slice(GW * g, GW * g + GW)
                    dve.wait_ge(s_cm, GS * NLEV * L + g + 1)
                    nc.vector.scalar_tensor_tensor(out=systems(xt[:, at]), in0=systems(cm[:, at]), scalar=-1.0, in1=eye,
                                                   op0=ALU.mult, op1=ALU.add)
                    filled(dve, ("C0", L, g))
                    nc.vector.scalar_tensor_tensor(out=systems(xi[:, at]), in0=systems(bank(("C0", L, g), 0, GW)), scalar=-1.0,
                                                   in1=eye, op0=ALU.mult, op1=ALU.add).then_inc(s_free["v"], 1)
                for lev in range(1, NLEV):
                    for g in range(GS):
                        at = slice(GW * g, GW * g + GW)
                        for kind, dst in (("X", xi[:, at]), ("Y", xt[:, at])):
                            if (kind, L, lev, g) in tiles.at:
                                filled(dve, (kind, L, lev, g))
                                nc.vector.tensor_tensor(dst, dst, bank((kind, L, lev, g), 0, GW),
                                                        ALU.subtract).then_inc(s_free["v"], 1)
                filled(dve, ("W0", L))
                nc.vector.tensor_tensor(heads(vn[:, 0, :]), heads(bank(("W0", L), 0, DG)), per_head(area("beta", 0, 6)),
                                        ALU.mult).then_inc(s_free["v"], 1)
                for parity in range(2):
                    key = (f"KS{parity}", L)
                    filled(dve, key)
                    nc.vector.tensor_tensor(rr.rearrange("p (q two e) -> p q two e", two=2, e=HD)[:, :, parity, :],
                                            heads(bank(key, 0, 3 * HD), 3), per_head(area("eg", 0, 6)[:, parity::2], 3),
                                            ALU.mult).then_inc(s_free["v"], 1)
                drained(dve, ("KS1", L), "v")
                nc.vector.tensor_tensor(rr, vt[:, 1, :], rr, ALU.subtract).then_inc(s_rr, 1)
                filled(dve, ("W1", L))
                nc.vector.tensor_tensor(heads(vn[:, 1, :]), heads(bank(("W1", L), 0, DG)), per_head(area("beta", 6, 6)),
                                        ALU.mult).then_inc(s_free["v"], 1)
                filled(dve, ("O1", L))
                drained(dve, ("QS1", L), "a")
                nc.vector.scalar_tensor_tensor(out=o[:, 1, 0:DG], in0=qs, scalar=SCALE, in1=bank(("O1", L), 0, DG),
                                               op0=ALU.mult, op1=ALU.add).then_inc(s_free["v"], 1)

            def windows(L):
                for k in range(HW):
                    filled(dve, ("D", L, k))
                    nc.vector.scalar_tensor_tensor(out=prob[:, k, :], in0=cc("dist"), scalar=SLOPES[k] / SCALE,
                                                   in1=bank(("D", L, k), 0, 384), op0=ALU.mult,
                                                   op1=ALU.add).then_inc(s_free["v"], 1)
                    drained(dve, ("D", L, k), "v")
                    nc.vector.reduce_max(area("den2" if False else "rden", 2 * k, 1), prob[:, k, 0:P], AX_X).then_inc(st.sem, st.up())
                    nc.vector.reduce_max(area("rden", 2 * k + 1, 1), prob[:, k, P:384], AX_X).then_inc(st.sem, st.up())
                    step()
                    nc.vector.tensor_scalar(area("nm", 2 * k, 2), area("rden", 2 * k, 2), -SCALE, None,
                                            ALU.mult).then_inc(s_nm, 1)
                for k in range(HW):
                    dve.wait_ge(s_dex, HW * L + k + 1)
                    nc.vector.tensor_tensor(prob[:, k, :], prob[:, k, :], cc("mult"), ALU.mult).then_inc(s_dpr, 1)
                for k in range(HW):
                    filled(dve, ("F", L, k))
                    f = bank(("F", L, k), 0, NB * (HD + 1)).rearrange("p (b e) -> p b e", b=NB)
                    nc.vector.reciprocal(area("rden", 2 * k, 2), f[:, :, HD]).then_inc(st.sem, st.up())
                    step()
                    nc.vector.tensor_tensor(o[:, :, DG + HD * k:DG + HD * k + HD], f[:, :, 0:HD],
                                            per_head(area("rden", 2 * k, 2), NB), ALU.mult).then_inc(s_free["v"], 1)

            def stick(L):
                for k in range(HS):
                    if k == 0:
                        dve.wait_ge(s_zl, L + 1)
                    nc.vector.scalar_tensor_tensor(out=sps[:, k, :], in0=zs[:, k, :], scalar=0.0, in1=es[:, k, :],
                                                   op0=ALU.max, op1=ALU.add).then_inc(st.sem, st.up())
                    step()
                    nc.vector.tensor_tensor(sps[:, k, :], sps[:, k, :], cc("earlier"), ALU.mult).then_inc(s_sps, 1)
                for k in range(HS):
                    filled(dve, ("CS", L, k))
                    nc.vector.tensor_tensor(zs[:, k, :], zs[:, k, :], bank(("CS", L, k), 0, 384),
                                            ALU.subtract).then_inc(s_free["v"], 1)
                for k in range(HS):
                    dve.wait_ge(s_ze, HS * L + k + 1)
                    nc.vector.scalar_tensor_tensor(out=zs[:, k, :], in0=zs[:, k, :], scalar=1.0, in1=cc("earlier"),
                                                   op0=ALU.min, op1=ALU.mult).then_inc(s_aT, 1)

            def head_norms(L):
                drained(dve, ("O0", L), "a")
                drained(dve, ("U", L), "a")
                drained(dve, ("F", L, HW - 1), "v")
                nc.vector.tensor_tensor(osq, hn_flat, hn_flat, ALU.mult).then_inc(st.sem, st.up())
                step()
                nc.vector.tensor_reduce(area("ss", 0, 32), osq.rearrange("p (h e) -> p h e", e=HD), AX_X,
                                        ALU.add).then_inc(s_oss, 1)
                dve.wait_ge(s_ors, L + 1)
                of = hn_flat.rearrange("p (h e) -> p h e", e=HD)
                nc.vector.tensor_tensor(of, of, per_head(area("rs", 0, 32), 32), ALU.mult).then_inc(st.sem, st.up())
                step()
                for i, (start, n) in enumerate(((0, HG), (DG, HW), (DG + DW, HS))):
                    w = rws[:, ROW_HN(L, i):ROW_HN(L, i) + HD].unsqueeze(1).unsqueeze(1).broadcast_to([P, NB, n, HD])
                    v = o[:, :, start:start + n * HD].rearrange("p b (h e) -> p b h e", h=n)
                    nc.vector.tensor_tensor(v, v, w, ALU.mult).then_inc(st.sem, st.up())
                step()
                dve.wait_ge(s_zg, L + 1)
                nc.vector.tensor_tensor(o[:, :, 0:DG], o[:, :, 0:DG], zt[:, :, :], ALU.mult).then_inc(s_o, 1)
                for c in range(4):
                    lower_part(("OT", L, c), xh[:, 512 * c:512 * c + 512], xl[:, 512 * c:512 * c + 512])

            def add_to_residual(key, b, m, it=None):
                filled(dve, key, it)
                v = h[:, b, 512 * m:512 * m + 512]
                nc.vector.tensor_tensor(v, v, bank(key), ALU.add).then_inc(s_free["v"], 1)

            def mixers(L):
                if L:
                    residual_ready(dve, 3 * L, None)
                nc.vector.memset(xc[:, :, 0:3], 0.0).then_inc(st.sem, st.up())
                step()
                norm(3 * L)
                if L == 0:
                    split.behind(("T", 0, 3))
                split.behind(("J", L, 1, 0))
                for t in range(10):
                    if t % 2:
                        split.behind(("I", L, t))
                        continue
                    filled(dve, ("I", L, t))
                    for c in (2 * t, 2 * t + 1):
                        dst = xc[:, c, 3:3 + T] if c < CQ else att[:, c - CQ, :]
                        ins = nc.vector.tensor_copy(dst, bank(("I", L, t), T * (c % 2), T))
                    ins.then_inc(s_free["v"], 1)
                    split.behind(("I", L, t))
                split.behind(("J", L, 1, 2))
                gates(L)
                decays(L)
                convolution(L)
                delta(L)
                windows(L)
                stick(L)
                head_norms(L)
                for m in range(2):
                    for b in range(NB):
                        add_to_residual(("WO", L, b, m), b, m)
                    split.behind(("WO", L, 1, m))

            def ple(L, items=None):
                split.behind(("PP", L, 1, 1), items)
                for m in range(2):
                    for b in range(NB):
                        drained(dve, ("PG", L, b, m), "a", items)
                        if m:
                            dve.wait_ge(s_ple, 4 * L + b + 1)
                        nc.vector.tensor_tensor(sgp[b], sig[b], bank(("PP", L, b, m)), ALU.mult).then_inc(s_free["v"], 1)
                        drained(dve, ("PP", L, b, m), "v", items)
                        v = h[:, b, 512 * m:512 * m + 512]
                        nc.vector.tensor_tensor(v, v, sgp[b], ALU.add).then_inc(s_ple, 1)
                    split.behind(("PG", L, 1, m), items)

            dve.wait_ge(s_in, 64)
            nc.vector.memset(dva[:, :, :, HD], 1.0).then_inc(st.sem, st.up())
            mixers(0)
            norm(1)
            for f in range(NF):
                drained(dve, ("H", f), "a")
                if f >= 2:
                    dve.wait_ge(s_ffg, f - 1)
                nc.vector.tensor_tensor(ffp[f % 2], ffs[f % 2], bank(("H", f), T, T), ALU.mult).then_inc(s_free["v"], 1)
                drained(dve, ("H", f), "v")
                nc.vector.tensor_copy(gh[:, f % 2, :], ffp[f % 2]).then_inc(st.sem, st.up())
                step()
                nc.vector.tensor_tensor(gl[:, f % 2, :], ffp[f % 2], gh[:, f % 2, :].bitcast(F32),
                                        ALU.subtract).then_inc(s_ffg, 1)
                split.behind(("H", f))
            split.behind(("Y2", 1, 1))
            for m in range(2):
                for b in range(NB):
                    add_to_residual(("Y2", b, m), b, m)
            norm(2)
            ple(0)
            mixers(1)
            norm(4)

            filled(dve, ("LG",))
            nc.vector.tensor_copy(lg, bank(("LG",), 0, 16).rearrange("p (b e) -> p b e", b=NB)).then_inc(s_free["v"], 1)
            drained(dve, ("LG",), "v")
            nc.vector.tensor_reduce(top, lg, AX_X, ALU.max).then_inc(st.sem, st.up())
            other = [lg[:, b, :].unsqueeze(1).broadcast_to([P, NE, NE]) for b in range(NB)]
            own = [lg[:, b, :].unsqueeze(2).broadcast_to([P, NE, NE]) for b in range(NB)]
            lower8 = cc("lower8").rearrange("p (e f) -> p e f", e=NE)
            for b in range(NB):
                nc.vector.tensor_tensor(pairs[0][:, b], other[b], own[b], ALU.is_gt).then_inc(st.sem, st.up())
                nc.vector.tensor_tensor(pairs[1][:, b], other[b], own[b], ALU.is_ge).then_inc(st.sem, st.up())
            step()
            for b in range(NB):
                nc.vector.tensor_tensor(pairs[1][:, b], pairs[1][:, b], lower8, ALU.mult).then_inc(st.sem, st.up())
            nc.vector.tensor_tensor(exl, lg, top.unsqueeze(2).broadcast_to([P, NB, NE]), ALU.subtract).then_inc(s_lsub, 1)
            step()
            for b in range(NB):
                nc.vector.tensor_tensor(pairs[0][:, b], pairs[0][:, b], pairs[1][:, b], ALU.max).then_inc(st.sem, st.up())
            step()
            nc.vector.tensor_reduce(rank, pairs[0], AX_X, ALU.add).then_inc(st.sem, st.up())
            step()
            nc.vector.tensor_scalar(sel, rank, TOPK - 0.5, None, ALU.is_lt).then_inc(s_sel, 1)
            dve.wait_ge(s_sel, 1)
            dve.wait_ge(s_lex, 1)
            nc.vector.tensor_tensor(exl, exl, sel, ALU.mult).then_inc(st.sem, st.up())
            step()
            nc.vector.tensor_reduce(den, exl, AX_X, ALU.add).then_inc(st.sem, st.up())
            step()
            nc.vector.reciprocal(den, den).then_inc(st.sem, st.up())
            step()
            nc.vector.tensor_tensor(gate, exl, den.unsqueeze(2).broadcast_to([P, NB, NE]),
                                    ALU.mult).then_inc(st.sem, st.up())
            filled(dve, ("POS",))
            nc.vector.tensor_copy(cum, bank(("POS",), 0, 24)).then_inc(s_free["v"], 1)
            drained(dve, ("POS",), "v")
            nc.vector.tensor_tensor(pos1, cum[:, 0:16].rearrange("p (b e) -> p b e", b=NB), sel,
                                    ALU.mult).then_inc(st.sem, st.up())
            nc.vector.tensor_scalar(over, cum[:, 16:24], P + 0.5, None, ALU.is_gt).then_inc(st.sem, st.up())
            step()
            nc.vector.tensor_tensor(pairs[0][:, 0], over.unsqueeze(1).broadcast_to([P, NE, NE]), lower8,
                                    ALU.mult).then_inc(st.sem, st.up())
            nc.vector.tensor_scalar(posi[:, :, 0:NE], pos1, -1.0, None, ALU.add).then_inc(st.sem, st.up())
            nc.vector.tensor_copy(gati[:, :, 0:NE], gate).then_inc(st.sem, st.up())
            step()
            nc.vector.tensor_reduce(oidx, pairs[0][:, 0], AX_X, ALU.add).then_inc(st.sem, st.up())
            step()
            shape = [P, MORE + 1, NE]
            nc.vector.tensor_tensor(osel, oidx.unsqueeze(1).broadcast_to(shape), cc("item").unsqueeze(2).broadcast_to(shape),
                                    ALU.is_equal).then_inc(st.sem, st.up())
            step()
            nc.vector.tensor_tensor(osel, osel, over.unsqueeze(1).broadcast_to(shape), ALU.mult).then_inc(st.sem, st.up())
            step()
            for b in range(NB):
                nc.vector.tensor_tensor(oprd[:, b], osel, pos1[:, b, :].unsqueeze(1).broadcast_to(shape),
                                        ALU.mult).then_inc(st.sem, st.up())
                nc.vector.tensor_tensor(oprd[:, 2 + b], osel, gate[:, b, :].unsqueeze(1).broadcast_to(shape),
                                        ALU.mult).then_inc(st.sem, st.up())
            nc.vector.tensor_tensor(oprd[:, 4], osel, cc("expert").unsqueeze(1).broadcast_to(shape),
                                    ALU.mult).then_inc(st.sem, st.up())
            nc.vector.tensor_reduce(tabf[:, MORE + 2:MORE + 3], over, AX_X, ALU.add).then_inc(st.sem, st.up())
            step()
            nc.vector.tensor_reduce(posi[:, :, NE:NI], oprd[:, 0:2], AX_X, ALU.add).then_inc(st.sem, st.up())
            nc.vector.tensor_reduce(gati[:, :, NE:NI], oprd[:, 2:4], AX_X, ALU.add).then_inc(st.sem, st.up())
            nc.vector.tensor_reduce(tabf[:, 1:MORE + 2], oprd[:, 4], AX_X, ALU.add).then_inc(st.sem, st.up())
            nc.vector.tensor_scalar(tabf[:, 0:1], tabf[:, MORE + 2:MORE + 3], 0.0, NE - 1.0, ALU.mult,
                                    ALU.add).then_inc(st.sem, st.up())
            nc.vector.tensor_scalar(tabf[:, MORE + 3:MORE + 4], tabf[:, MORE + 2:MORE + 3], NE - 1.0, None,
                                    ALU.add).then_inc(st.sem, st.up())
            step()
            nc.vector.tensor_scalar(posi[:, :, NE:NI], posi[:, :, NE:NI], -1.0 - P, None,
                                    ALU.add).then_inc(st.sem, st.up())
            nc.vector.tensor_copy(table[0:1, 0:MORE + 4], tabf[0:1, 0:MORE + 4]).then_inc(s_tab, 1)
            step()

            def selection(i):
                for b in range(NB):
                    p = posi[:, b, bass.ds(i, 1)] if not isinstance(i, int) else posi[:, b, i:i + 1]
                    g = gati[:, b, bass.ds(i, 1)] if not isinstance(i, int) else gati[:, b, i:i + 1]
                    nc.vector.tensor_scalar(pick[:, b, :], cc("slots"), p, None, ALU.is_equal)
                    ins = nc.vector.tensor_scalar(pickg[:, b, :], cc("slots"), p, g, ALU.is_equal, ALU.mult)
                ins.then_inc(s_pick, 1)

            def gathered(when, it):
                for half in range(2):
                    drained(dve, ("GA", when, half), "a", it)
                    for q in range(4):
                        k = 4 * half + q
                        ins = nc.vector.scalar_tensor_tensor(out=xl[:, P * k:P * k + P], in0=bank(("GA", when, half), P * q, P),
                                                             scalar=col(COL_NORM(4) + k),
                                                             in1=xh[:, P * k:P * k + P].bitcast(F32), op0=ALU.mult,
                                                             op1=ALU.subtract)
                    ins.then_inc(s_free["v"], 1)

            def product(ph, j, it):
                drained(dve, ("A", ph, j), "a", it)
                filled(dve, ("B", ph, j), it)
                nc.vector.tensor_tensor(mg[j % 2], ms[j % 2], bank(("B", ph, j)), ALU.mult).then_inc(s_free["v"], 1)

            def turned(ph, j, it):
                lower_part(("TT", ph, j), mTh[j % 2], mTl[j % 2], it)

            def rest_of_item(ph, it):
                for j in range(1, NJ):
                    turned(ph, j - 1, it)
                    split.behind(("A", ph, j), it)
                    product(ph, j, it)
                    if j < NJ - 1 or ph == "last":
                        split.behind(("B", ph, j), it)
                if ph == "each":
                    gathered(ph, it)
                    split.behind(("B", ph, NJ - 1), it)
                turned(ph, NJ - 1, it)
                if ph == "each":
                    split.behind(("A", ph, 0), it)
                split.behind(("YY", ph, 1), it)
                if ph == "each":
                    product(ph, 0, it)
                for m in range(2):
                    for b in range(NB):
                        add_to_residual(("SC", ph, b, m), b, m, it)
                if ph == "each":
                    split.behind(("B", ph, 0), it)

            selection(0)
            gathered("first", None)
            split.behind(("A", "first", 0))
            product("first", 0, None)
            split.behind(("B", "first", 0))
            dve.wait_ge(s_tab, 1)
            items = dve.value_load(table[0:1, MORE + 3:MORE + 4], min_val=NE - 1, max_val=NE - 1 + MORE)
            split.in_round()
            with dve.Fori(0, items) as i:
                filled(dve, ("GT", "each"), i, 1)
                selection(i + 1)
                rest_of_item("each", i)
            split.after()
            rest_of_item("last", items)
            norm(5, items)
            ple(1, items)
            dve.wait_ge(s_rstd, 7)
            dve.wait_ge(s_fw, 16)
            for b in range(NB):
                nc.vector.scalar_tensor_tensor(out=res[:, b, :], in0=h[:, b, :], scalar=area("mx", 10 + b, 1), in1=finw,
                                               op0=ALU.mult, op1=ALU.mult).then_inc(s_res, 1)

        @block.tensor
        def _(pe):
            def opened(key, it=None):
                before = tiles.at[key]["before"]
                if before is None:
                    return
                back = tiles.at[key]["back"]
                for who, count in before["drained"].items():
                    pe.wait_ge(s_free[who], through(count - back * per_drain[who], it, per_drain[who]))

            def norm(occ, items=None):
                for c in range(4):
                    opened(("T", occ, c), items)
                    if c == 0:
                        pe.wait_ge(s_hn["a"], occ + 1)
                        pe.wait_ge(s_hn["v"], occ + 1)
                    for q in range(4):
                        k, b = 2 * c + q // 2, q % 2
                        ins = pe.transpose(bank(("T", occ, c), P * q, P), hn[:, b, P * k:P * k + P], ident)
                    ins.then_inc(s_fill, 1)

            def hnT_ready(occ, items=None):
                drained(pe, ("T", occ, 3), "v", items)

            def product(out, a, b, start, stop):
                (ah, al), (bh, bl) = a, b
                pe.matmul(out, ah, bh, start=start, stop=False)
                pe.matmul(out, ah, bl, start=False, stop=False)
                return pe.matmul(out, al, bh, start=False, stop=stop)

            def x_part(start, width):
                return xh[:, start:start + width], xl[:, start:start + width]

            def both_blocks(keys, name, width, items=None):
                for half in range(2):
                    ready(pe, name + (half,), items)
                    for b, key in enumerate(keys):
                        if half == 0:
                            opened(key, items)
                        for q in range(4):
                            k = 4 * half + q
                            ins = product(bank(key, 0, width), x_part(T * k + P * b, P),
                                          weights(name + (half,), width * q, width), k == 0, k == KC - 1)
                        if half:
                            ins.then_inc(s_fill, 1)
                    if half == 0:
                        ins.then_inc(s_used, 1)

            def projections(L):
                hnT_ready(3 * L)

                def token_major(g, width):
                    both_blocks([("J", L, b, g) for b in range(NB)], ("J", L, g), width)

                token_major(0, DG + 2 * HG)
                for t in range(10):
                    ready(pe, ("I", L, t))
                    opened(("I", L, t))
                    for c in (2 * t, 2 * t + 1):
                        if c < CQ + CA:
                            for k in range(KC):
                                ins = product(bank(("I", L, t), T * (c % 2), T),
                                              weights(("I", L, t), P * (KC * (c % 2) + k), P), x_part(T * k, T), k == 0,
                                              k == KC - 1)
                    ins.then_inc(s_fill, 1)
                token_major(1, DW)
                token_major(2, DS)

            def lanes(k):
                return slice(HD * (k % 2), HD * (k % 2) + HD)

            def delta(L):
                opened(("G", L))
                pe.wait_ge(s_g, L + 1)
                g12 = area("g")
                for b in range(NB):
                    pe.matmul(bank(("G", L), HG * b, HG), cc("upto"), g12[:, HG * b:HG * b + HG], start=True, stop=True)
                pe.matmul(bank(("G", L), 2 * HG, HG), ones, g12[:, 0:HG], start=True, stop=True).then_inc(s_fill, 1)
                for g in range(GS):
                    opened(("R", L, g))
                    for k, b, at in group_heads(g):
                        ins = pe.matmul(bank(("R", L, g), at, P), area("g", b * HG + k, 1).broadcast_to([P, P]),
                                        cc("upto"), start=True, stop=True)
                    ins.then_inc(s_fill, 1)
                for c in range(3):
                    opened(("N2", L, c))
                    pe.wait_ge(s_sq, L + 1)
                    pe.matmul(bank(("N2", L, c)), cc("headsum"), squares[:, 512 * c:512 * c + 512], start=True,
                              stop=True).then_inc(s_fill, 1)
                for c in range(3):
                    opened(("V", L, c))
                    if c == 0:
                        pe.wait_ge(s_silu, 3 * L + 3)
                    if c == 2:
                        pe.wait_ge(s_qk, 3 * L + 3)
                    for k in range(3):
                        src = qkv[:, 6 + k, P * c:P * c + P] if c < 2 else qkv[:, 3 + k, 0:P]
                        ins = pe.transpose(bank(("V", L, c), P * k, P), src, ident)
                    ins.then_inc(s_fill, 1)
                for kind, first in (("KK", 3), ("QK", 0)):
                    for g in range(GS):
                        opened((kind, L, g))
                        for k, b, at in group_heads(g):
                            tok = slice(P * b, P * b + P)
                            ins = pe.matmul(bank((kind, L, g), at, P), qkv[lanes(k), 3 + k // 2, tok],
                                            qkv[lanes(k), first + k // 2, tok], start=True, stop=True)
                        ins.then_inc(s_fill, 1)

                def group(kind, lev, g, lhs, rhs):
                    key = (kind, L, g) if lev is None else (kind, L, lev, g)
                    opened(key)
                    for s in range(3):
                        at = slice(GW * g + P * s, GW * g + P * s + P)
                        if rhs is None:
                            ins = pe.transpose(bank(key, P * s, P), lhs[:, at], ident)
                        else:
                            ins = pe.matmul(bank(key, P * s, P), lhs[:, at], rhs[:, at], start=True, stop=True)
                    ins.then_inc(s_fill, 1)

                for g in range(GS):
                    pe.wait_ge(s_cm, GS * NLEV * L + g + 1)
                    group("C0", None, g, cm, None)
                for lev in range(1, NLEV):
                    for g in range(GS):
                        pe.wait_ge(s_cm, GS * NLEV * L + GS * lev + g + 1)
                        drained(pe, ("C0", L, g) if lev == 1 else ("X", L, lev - 1, g), "v")
                        group("P", lev, g, cm, xi)
                    for g in range(GS):
                        drained(pe, ("P", L, lev, g), "a")
                        if lev > 1:
                            drained(pe, ("Y", L, lev - 1, g), "v")
                        if lev < NLEV - 1:
                            group("X", lev, g, xt, pbuf)
                        group("Y", lev, g, pbuf, xt)

                def heads_of(key, wait, lhs, rhs, out=None, which=range(HG)):
                    opened(key)
                    wait()
                    for n, k in enumerate(which):
                        dst = bank(key, HD * n, HD) if out is None else out(k)
                        ins = pe.matmul(dst, lhs(k), rhs(k), start=True, stop=True)
                    ins.then_inc(s_fill, 1)

                def system(ap, b):
                    return lambda k: ap[:, system_at(k, b)]

                def state(k):
                    return s1[lanes(k), HD * (k // 2):HD * (k // 2) + HD]

                drained_y = lambda: [drained(pe, ("Y", L, NLEV - 1, g), "v") for g in range(GS)]
                heads_of(("W0", L), lambda: (drained_y(), drained(pe, ("V", L, 0), "a")), system(xt, 0),
                         lambda k: vt[:, 0, HD * k:HD * k + HD])
                heads_of(("S", L), lambda: drained(pe, ("W0", L), "v"), lambda k: kd[:, HD * k:HD * k + HD],
                         lambda k: vn[:, 0, HD * k:HD * k + HD],
                         lambda k: ps[lanes(k), tiles.at[("S", L)]["bank"], HD * (k // 2):HD * (k // 2) + HD])
                for name, first in (("KS", 3), ("QS", 0)):
                    for parity in range(2):
                        heads_of((f"{name}{parity}", L), lambda: drained(pe, ("S", L), "a"),
                                 lambda k: qkv[lanes(k), first + k // 2, P:T], state, which=range(parity, HG, 2))
                heads_of(("W1", L), lambda: pe.wait_ge(s_rr, L + 1), system(xt, 1), lambda k: rr[:, HD * k:HD * k + HD])
                heads_of(("O0", L), lambda: None, system(dec, 0), lambda k: vn[:, 0, HD * k:HD * k + HD])
                heads_of(("O1", L), lambda: drained(pe, ("W1", L), "v"), system(dec, 1),
                         lambda k: vn[:, 1, HD * k:HD * k + HD])

            def windows(L):
                for k in range(HW):
                    opened(("D", L, k))
                    q, kk = att[lanes(k), k // 2, :], att[lanes(k), 3 + k // 2, :]
                    pe.matmul(bank(("D", L, k), 0, P), q[:, 0:P], kk[:, 0:P], start=True, stop=True)
                    pe.matmul(bank(("D", L, k), P, T), q[:, P:T], kk, start=True, stop=True).then_inc(s_fill, 1)
                for k in range(HW):
                    opened(("E", L, k))
                    pe.wait_ge(s_dpr, HW * L + k + 1)
                    for s in range(3):
                        ins = pe.transpose(bank(("E", L, k), P * s, P), prob[:, k, P * s:P * s + P], ident)
                    ins.then_inc(s_fill, 1)
                for k in range(HW):
                    opened(("F", L, k))
                    drained(pe, ("E", L, k), "a")
                    w = HD + 1
                    pe.matmul(bank(("F", L, k), 0, w), probT[:, k, 0:P], dva[:, 0, k, :], start=True, stop=True)
                    pe.matmul(bank(("F", L, k), w, w), probT[:, k, P:T], dva[:, 0, k, :], start=True, stop=False)
                    pe.matmul(bank(("F", L, k), w, w), probT[:, k, T:384], dva[:, 1, k, :], start=False,
                              stop=True).then_inc(s_fill, 1)

            def stick(L):
                for k in range(HS):
                    opened(("Z", L, k))
                    q, kk = att[lanes(k), 6 + k // 2, :], att[lanes(k), 8 + k // 2, :]
                    pe.matmul(bank(("Z", L, k), 0, T), kk[:, 0:P], q, start=True, stop=True)
                    pe.matmul(bank(("Z", L, k), T, P), kk[:, P:T], q[:, P:T], start=True, stop=True).then_inc(s_fill, 1)
                for k in range(HS):
                    opened(("CS", L, k))
                    pe.wait_ge(s_sps, HS * L + k + 1)
                    pe.matmul(bank(("CS", L, k), 0, 384), cc("from"), sps[:, k, :], start=True, stop=False)
                    pe.matmul(bank(("CS", L, k), P, P), ones, sps[:, k, T:384], start=False, stop=True).then_inc(s_fill, 1)
                opened(("U", L))
                for k in range(HS):
                    pe.wait_ge(s_aT, HS * L + k + 1)
                    v = sva[:, :, HD * k:HD * k + HD]
                    pe.matmul(bank(("U", L), HD * k, HD), zs[:, k, 0:P], v[:, 0, :], start=True, stop=True)
                    pe.matmul(bank(("U", L), DS + HD * k, HD), zs[:, k, P:T], v[:, 0, :], start=True, stop=False)
                    ins = pe.matmul(bank(("U", L), DS + HD * k, HD), zs[:, k, T:384], v[:, 1, :], start=False, stop=True)
                ins.then_inc(s_fill, 1)

            def mixers(L):
                norm(3 * L)
                projections(L)
                delta(L)
                windows(L)
                stick(L)
                for c in range(4):
                    opened(("OT", L, c))
                    if c == 0:
                        pe.wait_ge(s_o, L + 1)
                    for q in range(4):
                        k, b = 2 * c + q // 2, q % 2
                        ins = pe.transpose(bank(("OT", L, c), P * q, P), o[:, b, P * k:P * k + P], ident)
                    ins.then_inc(s_fill, 1)
                drained(pe, ("OT", L, 3), "v")
                for m in range(2):
                    both_blocks([("WO", L, b, m) for b in range(NB)], ("WO", L, m), 512)

            def ple(L, items=None):
                hnT_ready(3 * L + 2, items)
                ready(pe, ("PP", L), items)
                for m in range(2):
                    for b in range(NB):
                        key = ("PP", L, b, m)
                        opened(key, items)
                        for k in range(PLE // P):
                            ins = product(bank(key), weights(("PT", L), T * k + P * b, P),
                                          weights(("PP", L), D * k + 512 * m, 512), k == 0, k == 1)
                        ins.then_inc(s_fill, 1)
                for m in range(2):
                    both_blocks([("PG", L, b, m) for b in range(NB)], ("PG", L, m), 512, items)

            pe.wait_ge(s_in, 64)
            mixers(0)
            norm(1)
            hnT_ready(1)

            def dense_down(f):
                pe.wait_ge(s_ffg, f + 1)
                ready(pe, ("w2", f // 2))
                for m in range(2):
                    for b in range(NB):
                        if f == 0:
                            opened(("Y2", b, m))
                        ins = product(bank(("Y2", b, m)), (gh[:, f % 2, P * b:P * b + P], gl[:, f % 2, P * b:P * b + P]),
                                      weights(("w2", f // 2), D * (f % 2) + 512 * m, 512), f == 0, f == NF - 1)
                        if f == NF - 1:
                            ins.then_inc(s_fill, 1)
                if f % 2 and f < NF - 1:
                    ins.then_inc(s_used, 1)

            for f in range(NF):
                opened(("H", f))
                ready(pe, ("w13", f))
                for side in range(2):
                    for k in range(KC):
                        ins = product(bank(("H", f), T * side, T), weights(("w13", f), P * (KC * side + k), P),
                                      x_part(T * k, T), k == 0, k == KC - 1)
                ins.then_inc(s_fill, 1)
                if f >= 1:
                    dense_down(f - 1)
            dense_down(NF - 1)
            norm(2)
            ple(0)
            mixers(1)
            norm(4)
            hnT_ready(4)
            opened(("LG",))
            for b in range(NB):
                for k in range(KC):
                    for n, x in enumerate((xh, xl)):
                        ins = pe.matmul(bank(("LG",), NE * b, NE), x[:, T * k + P * b:T * k + P * b + P].bitcast(F32),
                                        cols[:, COL_ROUTER + NE * k:COL_ROUTER + NE * k + NE], start=(k == 0 and n == 0),
                                        stop=(k == KC - 1 and n == 1))
            ins.then_inc(s_fill, 1)
            opened(("POS",))
            pe.wait_ge(s_sel, 1)
            pe.matmul(bank(("POS",), 0, NE), cc("upto"), sel[:, 0, :], start=True, stop=True)
            for start in (NE, 2 * NE):
                pe.matmul(bank(("POS",), start, NE), ones, sel[:, 0, :], start=True, stop=False)
                ins = pe.matmul(bank(("POS",), start, NE), cc("upto") if start == NE else ones, sel[:, 1, :], start=False,
                                stop=True)
            ins.then_inc(s_fill, 1)

            def gather(when, it, number):
                pe.wait_ge(s_pick, number)
                for half in range(2):
                    key = ("GA", when, half)
                    opened(key, it)
                    for q in range(4):
                        k = 4 * half + q
                        for b in range(NB):
                            ins = pe.matmul(bank(key, P * q, P), hn[:, b, P * k:P * k + P], pick[:, b, :], start=(b == 0),
                                            stop=(b == NB - 1))
                    ins.then_inc(s_fill, 1)

            def scatter_matrix(when, it):
                opened(("GT", when), it)
                for b in range(NB):
                    ins = pe.transpose(bank(("GT", when), P * b, P), pickg[:, b, :], ident)
                ins.then_inc(s_fill, 1)

            def up(kind, ph, j, it):
                key = (kind, ph, j)
                opened(key, it)
                for half in range(2):
                    ready(pe, key + (half,), it)
                    for q in range(4):
                        k = 4 * half + q
                        ins = product(bank(key), x_part(P * k, P), weights(key + (half,), 512 * q, 512), k == 0, k == KC - 1)
                    ins.then_inc(s_fill if half else s_used, 1)

            def turn(ph, j, it):
                opened(("TT", ph, j), it)
                for q in range(4):
                    ins = pe.transpose(bank(("TT", ph, j), P * q, P), mg[j % 2][:, P * q:P * q + P], ident)
                ins.then_inc(s_fill, 1)

            def down(ph, j, it):
                drained(pe, ("TT", ph, j), "v", it)
                if j == 0:
                    opened(("YY", ph, 0), it)
                    opened(("YY", ph, 1), it)
                for half in range(2):
                    ready(pe, ("C", ph, j, half), it)
                    for m in range(2):
                        for q in range(2):
                            c = 2 * half + q
                            ins = product(bank(("YY", ph, m)), (mTh[j % 2][:, P * c:P * c + P], mTl[j % 2][:, P * c:P * c + P]),
                                          weights(("C", ph, j, half), D * q + 512 * m, 512), j == 0 and c == 0,
                                          j == NJ - 1 and c == 3)
                        if j == NJ - 1 and half:
                            ins.then_inc(s_fill, 1)
                    if j < NJ - 1 or half == 0:
                        ins.then_inc(s_used, 1)

            def rest_of_item(ph, it):
                for j in range(1, NJ):
                    up("A", ph, j, it)
                    if j == 1:
                        drained(pe, ("B", "each", 0), "v", it, 1)
                    else:
                        drained(pe, ("B", ph, j - 1), "v", it)
                    turn(ph, j - 1, it)
                    if j == NJ - 1 and ph == "each":
                        gather(ph, it, it + 2)
                    up("B", ph, j, it)
                    down(ph, j - 1, it)
                drained(pe, ("B", ph, NJ - 1), "v", it)
                turn(ph, NJ - 1, it)
                if ph == "each":
                    drained(pe, ("GA", ph, 1), "v", it)
                    up("A", ph, 0, it)
                down(ph, NJ - 1, it)
                if ph == "each":
                    up("B", ph, 0, it)
                drained(pe, ("GT", "each"), "a", it, 1)
                for m in range(2):
                    drained(pe, ("YY", ph, m), "a", it)
                    for b in range(NB):
                        opened(("SC", ph, b, m), it)
                        pe.matmul(bank(("SC", ph, b, m)), back[:, P * b:P * b + P], ysb[:, 512 * m:512 * m + 512], start=True,
                                  stop=True).then_inc(s_fill, 1)
                if ph == "each":
                    scatter_matrix(ph, it)

            gather("first", None, 1)
            drained(pe, ("GA", "first", 1), "v")
            up("A", "first", 0, None)
            scatter_matrix("first", None)
            up("B", "first", 0, None)
            for who in "va":
                pe.wait_ge(s_free[who], tiles.base[who])
            pe.wait_ge(s_tab, 1)
            items = pe.value_load(table[0:1, MORE + 3:MORE + 4], min_val=NE - 1, max_val=NE - 1 + MORE)
            with pe.Fori(0, items) as i:
                rest_of_item("each", i)
            rest_of_item("last", items)
            norm(5, items)
            ple(1, items)


def chunks_of(w):
    k, c = w.shape
    return w.reshape(k // P, P, c // P, P).transpose(1, 2, 0, 3)


def slot(*parts):
    flat = np.concatenate([a.reshape(P, -1) for a in parts], 1)
    out = np.zeros((P, SLOT), np.float32)
    out[:, :flat.shape[1]] = flat
    return out


def k_major(w):
    return w.reshape(-1, P, w.shape[1]).transpose(1, 0, 2)


def kernel(**inputs):
    import concourse.bacc as bacc
    from concourse.bass_utils import run_bass_kernel_spmd

    a = {k: np.asarray(v) for k, v in inputs.items()}
    plan = plan_loads(plan_tiles()[0])
    per_load = len(plan["each"])
    w_in = a["w_in"]
    q0, z0, dq0 = 0, 3 * DG, 4 * DG + 2 * HG
    dv0 = dq0 + 2 * DW
    sq0 = dv0 + DW
    sv0 = sq0 + 2 * DS

    def load(key):
        kind = key[0]
        if kind == "J":
            L, g, half = key[1:]
            lo, hi = ((z0, dq0), (dv0, sq0), (sv0, sv0 + DS))[g]
            return slot(k_major(w_in[L][:, lo:hi])[:, 4 * half:4 * half + 4])
        if kind == "I":
            L, c = key[1:]
            every = np.concatenate([w_in[L][:, q0:z0], w_in[L][:, dq0:dv0], w_in[L][:, sq0:sv0]], 1)
            return slot(chunks_of(every[:, 2 * P * c:2 * P * c + 2 * P]))
        if kind in ("WO", "PG"):
            L, m, half = key[1:]
            w = a["w_out" if kind == "WO" else "ple_gate"][L]
            return slot(k_major(w[:, 512 * m:512 * m + 512])[:, 4 * half:4 * half + 4])
        if kind == "w13":
            at = slice(P * key[1], P * key[1] + P)
            return slot(chunks_of(a["ffn_w1"][0][:, at]), chunks_of(a["ffn_w3"][0][:, at]))
        if kind == "w2":
            return slot(k_major(a["ffn_w2"][0][2 * P * key[1]:2 * P * key[1] + 2 * P]))
        if kind == "PP":
            return slot(k_major(a["ple_proj"][key[1]]))
        return slot(k_major(np.ascontiguousarray(a["p"][key[1], 0].T)))

    stream = np.stack([load(key) for key in plan["before"][:-4] + plan["after"][plan["last"]:]])
    experts = np.empty((NE, per_load, P, SLOT), np.float32)
    for key in plan["each"]:
        n, (kind, _, j, half) = expert_place(key), key
        if kind == "C":
            w = a["moe_w2"][0][:, 512 * j + T * half:512 * j + T * half + T]
            experts[:, n] = w.reshape(NE, 2, P, D).transpose(0, 2, 1, 3).reshape(NE, P, SLOT)
        else:
            w = a["moe_w1" if kind == "A" else "moe_w3"][0][:, 512 * half:512 * half + 512, 512 * j:512 * j + 512]
            experts[:, n] = w.reshape(NE, 4, P, 512).transpose(0, 2, 1, 3).reshape(NE, P, SLOT)
    norms = np.stack([a["attn_norm_w"], a["ffn_norm_w"], a["ple_norm_w"]], 1)
    columns = np.concatenate([
        norms.reshape(-1, P).T,
        a["conv_w"].reshape(DEPTH, CONV, CQ, P).transpose(3, 0, 2, 1).reshape(P, -1),
        k_major(a["router_w"][0]).reshape(P, -1)], 1)
    heads = np.stack([a["gdn_norm_w"], a["dsw_norm_w"], a["sb_norm_w"]], 1)
    rows = np.concatenate([a["a_log"].ravel(), a["dt_bias"].ravel(), heads.ravel()])

    given = dict(x=a["x"][0], stream=stream, experts=experts.reshape(NE * per_load, P, SLOT), columns=columns,
                 rows=np.broadcast_to(rows, (P, NROW)), final_w=np.broadcast_to(a["final_norm_w"], (P, D)),
                 consts=shape_constants())
    nc = bacc.Bacc("TRN2", target_bir_lowering=False, num_devices=1)
    arrays, args = {}, {}
    for name, v in given.items():
        v = np.ascontiguousarray(v)
        arrays[f"in_{name}"] = v
        args[name] = nc.dram_tensor(f"in_{name}", v.shape, mybir.dt.from_np(v.dtype), kind="ExternalInput").ap()
    out = nc.dram_tensor("out", (T, D), F32, kind="ExternalOutput").ap()
    build(nc, out=out, **args)
    r = run_bass_kernel_spmd(nc, [arrays], core_ids=[0])
    return r.results[0]["out"].reshape(1, T, D)
```

```python
from contextlib import ExitStack

import numpy as np

import concourse.bass as bass
from concourse import mybir

ALU = mybir.AluOpType
ACT = mybir.ActivationFunctionType
F32 = mybir.dt.float32
F32R = mybir.dt.float32r
I32 = mybir.dt.int32
AX_X = mybir.AxisListType.X

P = 128
T, D = 256, 1024
NB = T // P
KC = D // P
DEPTH = 2
HD = 64
HG, HW, HS = 6, 6, 4
DG, DW, DS = HG * HD, HW * HD, HS * HD
CONV = 4
FF = 2816
NF = FF // P
NE, TOPK, MFF = 8, 2, 3584
NJ = MFF // 512
PLE = 256
EPS = 1e-6
SCALE = HD ** -0.5
SLOPES = [2.0 ** (-8.0 * (i + 1.0) / HW) for i in range(HW)]
WINDOWS = ((128, 1), (512, 4), (2048, 16))
FAR = -1e30
MORE = T * TOPK // (P + 1)
NI = NE + MORE + 1
FIRST = 4
RING = 6
LEAD = 4
SLOT = 2048
GS, GW = 4, 384
HEAD_PARTS = ((DG, HW, 0), (0, HG, NB * HW), (DG + DW, HS, NB * (HW + HG)))
OUT_CHUNKS = (3, 4, 5, 0, 1, 2, 6, 7)
NLEV = 7
CQ = 9
CA = 10


class Count:

    def __init__(self, sem):
        self.sem, self.k = sem, 0

    def up(self):
        self.k += 1
        return 1

    @property
    def n(self):
        return self.k


class Tiles:

    def __init__(self):
        self.at, self.filled, self.drained, self.last, self.phase = {}, 0, {"v": 0, "a": 0}, {}, "before"

    def add(self, key, bank, who):
        self.filled += 1
        for w in who:
            self.drained[w] += 1
        before = self.last.get(bank)
        self.at[key] = dict(bank=bank, filled=self.filled, before=before, phase=self.phase,
                            back=int(self.phase == "after" and before["phase"] == "round"),
                            drained={w: self.drained[w] for w in who})
        self.last[bank] = self.at[key]

    def drain(self, key, who):
        for w in who:
            self.drained[w] += 1
        self.at[key]["drained"] = {w: self.drained[w] for w in who}


def system_at(k, b):
    n = GW * (2 * (k % 2) + b) + P * (k // 2)
    return slice(n, n + P)


def group_heads(g):
    return [(2 * q + g // 2, g % 2, P * q) for q in range(3)]


def norm_tiles(t, occ):
    for c in range(4):
        t.add(("T", occ, c), c, "av")


ASIDE = (("max", 0, 2), ("exp", 2, HW), ("weigh", 3, HW), ("E", 4, HW), ("F", 6, HW), ("Z", 12, HS), ("log1p", 16, 1),
         ("squares", 13, 1), ("scales", 17, 1), ("gate", 19, 1), ("softplus", 20, HS))
WHO_ASIDE = {"E": "a", "F": "v", "Z": "a"}


def aside(lev, g):
    n = GS * (lev - 1) + g
    return [(kind, n - first) for kind, first, count in ASIDE if 0 <= n - first < count]


def mixer_tiles(t, L):
    n = [0]
    cs = [0]

    def add(key, who):
        t.add(key, n[0] % 8, who)
        n[0] += 1

    norm_tiles(t, 3 * L)
    for b in range(NB):
        add(("J", L, b, 0), "a")
    for c in range(5):
        add(("I", L, c), "a")
    add(("G", L), "v")
    for g in range(GS):
        add(("R", L, g), "v")
    add(("I", L, 5), "v")
    add(("I", L, 6), "a")
    for c in range(3):
        add(("N2", L, c), "a")
    add(("I", L, 7), "v")
    for c in range(2):
        add(("V", L, c), "a")
    add(("I", L, 8), "a")
    add(("I", L, 9), "v")
    for g in (1, 2):
        for b in range(NB):
            add(("J", L, b, g), "a")
    add(("V", L, 2), "v")
    for kind in ("KK", "QK"):
        for g in range(GS):
            add((kind, L, g), "v")
    for k in range(HW):
        add(("D", L, k), "v")
    for g in range(GS):
        add(("C0", L, g), "v")
    for lev in range(1, NLEV):
        for g in range(GS):
            add(("P", L, lev, g), "a")
            if lev > 1:
                add(("Y", L, lev - 1, g), "a")
        for g in range(GS):
            add(("Y" if lev == NLEV - 1 else "X", L, lev, g), "v")
            for kind, k in aside(lev, g):
                if kind in WHO_ASIDE:
                    add((kind, L, k), WHO_ASIDE[kind])
    for key, who in (("W0", "v"), ("CS", "v"), ("S", "a"), ("CS", "v"), ("KS0", "v"), ("KS1", "v"), ("CS", "v"),
                     ("QS0", "a"), ("QS1", "a"), ("CS", "v"), ("W1", "v"), ("O0", "a"), ("O1", "v")):
        if key == "CS":
            add((key, L, cs[0]), who)
            cs[0] += 1
        else:
            add((key, L), who)
    add(("U", L), "a")
    for c in range(4):
        add(("OT", L, c), "av")
    for m in range(2):
        for b in range(NB):
            add(("WO", L, b, m), "v")


def ple_tiles(t, L):
    for m in range(2):
        for b in range(NB):
            t.add(("PP", L, b, m), 4 + 2 * m + b, "")
    norm_tiles(t, 3 * L + 2)
    for m in range(2):
        for b in range(NB):
            t.drain(("PP", L, b, m), "v")
    for m in range(2):
        for b in range(NB):
            t.add(("PG", L, b, m), 2 * m + b, "a")


def gather_tiles(t, when):
    t.add(("GA", when, 0), 2, "av")
    t.add(("GA", when, 1), 3, "av")


def round_tiles(t, last):
    ph = "last" if last else "each"
    for j in range(1, NJ):
        t.add(("A", ph, j), 2 * (j % 2), "a")
        t.add(("TT", ph, j - 1), 6 + (j - 1) % 2, "av")
        if j == NJ - 1 and not last:
            gather_tiles(t, ph)
        t.add(("B", ph, j), 2 * (j % 2) + 1, "v")
    t.add(("TT", ph, NJ - 1), 6 + (NJ - 1) % 2, "av")
    if not last:
        t.add(("A", ph, 0), 0, "a")
    for m in range(2):
        t.add(("YY", ph, m), 4 + m, "a")
    if not last:
        t.add(("B", ph, 0), 1, "v")
    for m, b, bank in ((0, 0, 2), (0, 1, 6), (1, 0, 7), (1, 1, 3)):
        t.add(("SC", ph, b, m), bank, "v")
    if not last:
        t.add(("GT", ph), 0, "a")


def plan_tiles():
    t = Tiles()
    mixer_tiles(t, 0)
    norm_tiles(t, 1)
    for f in range(NF):
        t.add(("H", f), f % 4, "av")
    for m in range(2):
        for b in range(NB):
            t.add(("Y2", b, m), 4 + 2 * b + m, "v")
    ple_tiles(t, 0)
    mixer_tiles(t, 1)
    norm_tiles(t, 4)
    t.add(("LG",), 4, "a")
    t.add(("LT",), 6, "v")
    t.add(("POS",), 5, "v")
    gather_tiles(t, "first")
    t.add(("A", "first", 0), 0, "a")
    t.add(("GT", "first"), 6, "a")
    t.add(("B", "first", 0), 1, "v")
    t.base_filled, t.base = t.filled, dict(t.drained)
    t.phase = "round"
    round_tiles(t, False)
    per_fill = t.filled - t.base_filled
    per_drain = {w: t.drained[w] - t.base[w] for w in "va"}
    for tile in t.at.values():
        if tile["phase"] == "round" and tile["before"]["phase"] == "before":
            tile["before"], tile["back"] = t.last[tile["bank"]], 1
    t.filled, t.drained, t.phase = t.base_filled, dict(t.base), "after"
    round_tiles(t, True)
    ple_tiles(t, 1)
    return t, per_fill, per_drain


def plan_loads(tiles):
    order, until, turn = [], {}, {}
    early = [0]

    def add(key, tile, signal=False, behind=None):
        order.append(key)
        if signal:
            early[0] += 1
            until[key] = ("signal", early[0])
        else:
            until[key] = ("tile", tile)
        turn[key] = tiles.at[behind or tile]["filled"]

    for L in range(DEPTH):
        add(("J", L, 0, 0), ("J", L, 1, 0), signal=True)
        add(("J", L, 0, 1), ("J", L, 1, 0))
        for c in range(10):
            add(("I", L, c), ("I", L, c))
        for g in (1, 2):
            add(("J", L, g, 0), ("J", L, 1, g), signal=True)
            add(("J", L, g, 1), ("J", L, 1, g))
        for m in range(2):
            add(("WO", L, m, 0), ("WO", L, 1, m), signal=True)
            add(("WO", L, m, 1), ("WO", L, 1, m))
        if L == 0:
            for f in range(NF):
                add(("w13", f), ("H", f))
                if f % 2 and f < NF - 1:
                    add(("w2", f // 2), ("H", f + 1), signal=True)
            add(("w2", NF // 2 - 1), ("Y2", 1, 1))
            ple_loads(add, 0)

    def group(ph, j, kinds="AB"):
        for kind in kinds:
            ahead = ("LG",) if (kind, ph) == ("A", "first") else None
            add((kind, ph, j, 0), (kind, ph, j), signal=True, behind=ahead)
            add((kind, ph, j, 1), (kind, ph, j), behind=ahead)

    def rest_of_item(ph):
        for j in range(1, NJ):
            group(ph, j)
            for half in range(2):
                add(("C", ph, j - 1, half), ("B", ph, j), signal=True)
        if ph == "each":
            group(ph, 0, "A")
        add(("C", ph, NJ - 1, 0), ("YY", ph, 0), signal=True)
        add(("C", ph, NJ - 1, 1), ("YY", ph, 1))
        if ph == "each":
            group(ph, 0, "B")

    group("first", 0)
    before, signals = len(order), early[0]
    rest_of_item("each")
    each = order[before:]
    per_signal = early[0] - signals
    del order[before:]
    early[0] = signals
    rest_of_item("last")
    last = len(order) - before
    ple_loads(add, 1)
    after = order[before:]
    return dict(before=order[:before], each=each, after=after, last=last, until=until, turn=turn,
                per_signal=per_signal)


def expert_place(key):
    kind, _, j, half = key
    return 4 * NJ + 2 * j + half if kind == "C" else 4 * j + 2 * (kind == "B") + half


def ple_loads(add, L):
    add(("PT", L), ("PP", L, 1, 1))
    add(("PP", L), ("PP", L, 1, 1))
    for m in range(2):
        add(("PG", L, m, 0), ("PG", L, 1, m), signal=True)
        add(("PG", L, m, 1), ("PG", L, 1, m))


CONSTS = {}
_at = 0
for _name, _w in (("ident", P), ("ones", P), ("upto", P), ("from", P), ("headsum", P), ("slots", P),
                  ("levels", NLEV * P), ("dist", 384), ("mult", 384), ("earlier", 384), ("lower8", NE * NE),
                  ("expert", NE), ("item", MORE + 1), ("eps", 1)):
    CONSTS[_name] = (_at, _w)
    _at += _w
NCONST = _at


def shape_constants():
    c = np.zeros((P, NCONST), np.float32)
    i = np.arange(P)

    def put(name, value):
        a, w = CONSTS[name]
        c[:, a:a + w] = np.asarray(value, np.float32).reshape(-1, w)

    put("ident", np.eye(P))
    put("ones", np.ones((P, P)))
    put("upto", i[:, None] <= i[None, :])
    put("from", i[:, None] >= i[None, :])
    put("headsum", i[:, None] // HD == i[None, :] // HD)
    put("slots", np.tile(i, (P, 1)))
    lev = []
    for s in range(NLEV):
        w = 1 << s
        same = i[:, None] // (2 * w) == i[None, :] // (2 * w)
        lev.append(same & (i[:, None] // w % 2 == 0) & (i[None, :] // w % 2 == 1))
    put("levels", np.concatenate(lev, 1))
    q = np.concatenate([i[:, None] - i[None, :], P + i[:, None] - np.arange(T)[None, :]], 1)
    m = sum((q >= 0) & (q <= window) & (q % r == 0) for window, r in WINDOWS)
    put("dist", np.where(m > 0, -q, FAR))
    put("mult", m)
    b = i[:, None] < i[None, :]
    put("earlier", np.concatenate([b, np.ones((P, P)), b], 1))
    put("lower8", np.tile((np.arange(NE)[None, :] < np.arange(NE)[:, None]).reshape(1, -1), (P, 1)))
    put("expert", np.tile(np.arange(NE), (P, 1)))
    put("item", np.tile(np.arange(MORE + 1), (P, 1)))
    put("eps", np.full((P, 1), EPS))
    return c


COL_NORM = lambda occ: occ * KC
COL_CONV = 3 * DEPTH * KC
COL_ROUTER = COL_CONV + DEPTH * CQ * CONV
NCOL = COL_ROUTER + KC * NE
ROW_ALOG, ROW_DT = 0, DEPTH * HG
ROW_HN = lambda L, i: 2 * DEPTH * HG + (L * 3 + i) * HD
NROW = 2 * DEPTH * HG + DEPTH * 3 * HD


def build(nc, x, stream, experts, columns, rows, final_w, consts, out):
    tiles, per_fill, per_drain = plan_tiles()
    plan = plan_loads(tiles)
    n_before, per_load, per_signal = len(plan["before"]), len(plan["each"]), plan["per_signal"]
    in_round, after = plan["before"] + plan["each"], plan["before"] + plan["after"]
    load_at = {key: n for order in (in_round, after) for n, key in enumerate(order)}
    assert per_load % RING == 0
    laps = per_load // RING
    n_stream = n_before - FIRST

    with ExitStack() as ctx:
        def sb(name, shape, dt=F32):
            return ctx.enter_context(nc.sbuf_tensor(name, shape, dt))

        def sem(name):
            return ctx.enter_context(nc.semaphore(name))

        ps = ctx.enter_context(nc.psum_tensor("ps", [P, 8, 512], F32))
        with nc.sbuf_tensor("raw", [P, RING, SLOT], F32) as raw:
            pass
        wlo = sb("wlo", [P, RING, SLOT], F32R)
        whi = sb("whi", [P, RING, SLOT], F32R)
        cst = sb("cst", [P, NCONST])
        cols = sb("cols", [P, NCOL])
        rws = sb("rws", [P, NROW])
        h = sb("h", [P, NB, D])
        hn = sb("hn", [P, NB, D])
        with nc.sbuf_tensor("attn", [P, 2 * KC * T], F32) as attn:
            pass
        xh = sb("xh", [P, KC * T], F32R)
        xl = sb("xl", [P, KC * T], F32R)
        gh = sb("gh", [P, 2, T], F32R)
        gl = sb("gl", [P, 2, T], F32R)
        rh, rl = gh[:, 0, 0:KC * NE], gl[:, 0, 0:KC * NE]
        table = sb("table", [1, 8], I32)

        sizes = dict(xc=CQ * (T + 3) + 1, qkv=CQ * T, att=CA * T, z=NB * DG, dva=NB * HW * (HD + 1), sva=NB * DS,
                     dec=1536, mt=1536, xt=1536, xi=1536, ab=24, em=30, lnp=12, beta=12, g=12, gc=18, xa=12,
                     e1=24, gx=12, eg=12, ss=64, rs=68, rstd=2, nm=12, rden=12)
        off, place = 0, {}
        for k, w in sizes.items():
            place[k] = (off, w)
            off += w
        work = sb("work", [P, off])

        def area(name, start=0, width=None):
            a, w = place[name]
            return work[:, a + start:a + start + (w - start if width is None else width)]

        def cc(name, start=0, width=None):
            a, w = CONSTS[name]
            return cst[:, a + start:a + start + (w - start if width is None else width)]

        def col(n):
            return cols[:, n:n + 1]

        ident, ones = cc("ident"), cc("ones")

        xc = area("xc", 0, CQ * (T + 3)).rearrange("p (c t) -> p c t", c=CQ)
        qkv = area("qkv").rearrange("p (c t) -> p c t", c=CQ)
        att = area("att").rearrange("p (c t) -> p c t", c=CA)
        zt = area("z").rearrange("p (b c) -> p b c", b=NB)
        dva = area("dva").rearrange("p (b h e) -> p b h e", b=NB, h=HW)
        sva = area("sva").rearrange("p (b c) -> p b c", b=NB)
        ab = area("ab").rearrange("p (b c) -> p b c", b=NB)
        squares = area("xc", 0, 1536)
        pbuf = area("xc", 0, 1536)
        vt = area("xc", 1536, NB * DG).rearrange("p (b c) -> p b c", b=NB)
        dec, mt, xt, xi = area("dec"), area("mt"), area("xt"), area("xi")
        cm = area("att", 0, 1536)
        kd = area("qkv", 6 * T, DG)
        vn = area("mt", 0, NB * DG).rearrange("p (b c) -> p b c", b=NB)
        s1 = area("mt", 768, 192)
        rr = area("mt", 960, DG)
        qs = area("xc", 0, DG)
        o = hn
        prob = attn[:, 0:HW * 384].rearrange("p (h s) -> p h s", h=HW)
        zs = prob[:, 0:HS, :]
        es = attn[:, HW * 384:(HW + HS) * 384].rearrange("p (h s) -> p h s", h=HS)
        osq = (attn[:, HS * 384:HW * 384], area("dec", 0, NB * DG), area("mt", 0, NB * DS))

        def part(start, width):
            return work[:, start:start + width]

        ffs = [part(256 * i, 256) for i in range(2)]
        ffp = [part(512 + 256 * i, 256) for i in range(2)]
        sig = [part(512 * i, 512) for i in range(2)]
        sgp = [part(1024 + 512 * i, 512) for i in range(2)]
        ms = [part(512 * i, 512) for i in range(2)]
        mg = [part(1024 + 512 * i, 512) for i in range(2)]
        mTh, mTl = ([x[:, 1024 + 512 * i:1536 + 512 * i] for i in range(2)] for x in (xh, xl))
        pick = part(4096, 256).rearrange("p (b s) -> p b s", b=NB)
        pickg = part(4352, 256).rearrange("p (b s) -> p b s", b=NB)
        back = part(4608, 256)
        logits = part(4608, 256)[0:NE]
        ysb = part(4864, 1024)
        R0 = 5888
        lg = part(R0, 16).rearrange("p (b e) -> p b e", b=NB)
        top = part(R0 + 16, 2)
        den = part(R0 + 18, 2)
        over = part(R0 + 20, 8)
        oidx = part(R0 + 28, 8)
        rank = part(R0 + 36, 16).rearrange("p (b e) -> p b e", b=NB)
        sel = part(R0 + 52, 16).rearrange("p (b e) -> p b e", b=NB)
        gate = part(R0 + 68, 16).rearrange("p (b e) -> p b e", b=NB)
        exl = part(R0 + 84, 16).rearrange("p (b e) -> p b e", b=NB)
        cum = part(R0 + 100, 24)
        pos1 = part(R0 + 124, 16).rearrange("p (b e) -> p b e", b=NB)
        tabf = part(R0 + 140, 8)
        posi = part(R0 + 148, NB * NI).rearrange("p (b i) -> p b i", b=NB)
        gati = part(R0 + 148 + NB * NI, NB * NI).rearrange("p (b i) -> p b i", b=NB)
        pairs = [part(R0 + 200 + 128 * i, 128).rearrange("p (b e f) -> p b e f", b=NB, e=NE) for i in range(2)]
        osel = part(R0 + 456, (MORE + 1) * NE).rearrange("p (r e) -> p r e", e=NE)
        oprd = part(R0 + 456 + 32, 5 * (MORE + 1) * NE).rearrange("p (a r e) -> p a r e", a=5, e=NE)
        assert R0 + 456 + 192 <= place["z"][0]
        f0 = place["dec"][0]
        finw = part(f0, D)
        res = part(f0 + D, NB * D).rearrange("p (b c) -> p b c", b=NB)

        s_in, s_small, s_cst = sem("x_landed"), sem("small_inputs_landed"), sem("constants_landed")
        s_fw = sem("final_weight_landed")
        s_land = [sem(f"weights_landed_{i}") for i in range(RING)]
        s_fill = sem("psum_filled")
        s_used = sem("weights_used_within_a_tile")
        s_hi, s_lo = sem("weights_upper_part_ready"), sem("weights_split")
        s_free = {"v": sem("psum_drained_by_vector"), "a": sem("psum_drained_by_scalar")}
        s_out = sem("output_written")
        s_vstep, s_astep, s_pstep = sem("vector_step"), sem("scalar_step"), sem("gpsimd_step")
        s_sumsq, s_rstd = sem("row_squares_summed"), sem("row_rstd_ready")
        s_hn = {"v": sem("hn_block1_ready"), "a": sem("hn_block0_ready")}
        s_gin, s_gexp = sem("gate_arguments_ready"), sem("gate_exponentials_ready")
        s_gadd, s_gln, s_g = sem("exponentials_plus_one"), sem("softplus_logs_ready"), sem("gates_ready")
        s_gx, s_eg = sem("summed_gate_arguments_ready"), sem("summed_gate_exponentials_ready")
        s_dexp, s_dec = sem("decays_ready"), sem("decays_masked")
        s_conv, s_silu = sem("convolved"), sem("convolved_silu_ready")
        s_sq, s_qk = sem("qk_squares_ready"), sem("qk_normalised")
        s_cm, s_rr = sem("level_blocks_ready"), sem("chunk1_right_side_ready")
        s_nm, s_dex, s_dpr = sem("window_max_ready"), sem("window_exponentials_ready"), sem("window_weights_ready")
        s_zl, s_sps = sem("stick_logs_ready"), sem("stick_softplus_ready")
        s_ze, s_aT = sem("stick_exponentials_ready"), sem("stick_weights_ready")
        s_zg, s_oss, s_ors, s_o = sem("silu_z_ready"), sem("head_squares_summed"), sem("head_rstd"), sem("mixed_ready")
        s_ple = sem("ple_added")
        s_ffg = sem("dense_product_split")
        s_router = sem("router_weights_split")
        s_lsub, s_lex = sem("router_logits_shifted"), sem("router_exponentials_ready")
        s_sel, s_tab, s_pick = sem("experts_selected"), sem("item_table_ready"), sem("item_selection_ready")
        s_res = sem("result_ready")

        def bank(key, start=0, width=512):
            return ps[:, tiles.at[key]["bank"], start:start + width]

        def through(count, it, per):
            return count if it is None else it * per + count

        def filled(eng, key, it=None, back=0):
            eng.wait_ge(s_fill, through(tiles.at[key]["filled"] - back * per_fill, it, per_fill))

        def drained(eng, key, who, it=None, back=0):
            eng.wait_ge(s_free[who], through(tiles.at[key]["drained"][who] - back * per_drain[who], it, per_drain[who]))

        class Split:

            def __init__(self, one):
                self.one, self.next, self.end, self.order = one, 0, n_before + LEAD, in_round

            def in_round(self):
                assert self.next == n_before + LEAD
                self.end = n_before + per_load + LEAD

            def after(self):
                assert self.next == self.end
                self.next, self.end, self.order = n_before + LEAD, len(after), after

            def behind(self, key, it=None, most=RING):
                now = tiles.at[key]["filled"]
                end = min(self.next + most, self.end)
                while self.next < end and (self.next < LEAD or plan["turn"][self.order[self.next - LEAD]] <= now):
                    self.one(self.next, it)
                    self.next += 1

        def split_upper(n, it):
            nc.scalar.wait_ge(s_land[n % RING], through(16 * (n // RING + 1), it, 16 * laps))
            nc.scalar.copy(whi[:, n % RING, :], raw[:, n % RING, :]).then_inc(s_hi, 1)

        def split_lower(n, it):
            nc.vector.wait_ge(s_hi, through(n + 1, it, per_load))
            nc.vector.tensor_tensor(wlo[:, n % RING, :], raw[:, n % RING, :], whi[:, n % RING, :].bitcast(F32),
                                    ALU.subtract).then_inc(s_lo, 1)

        def ready(eng, key, it=None):
            eng.wait_ge(s_lo, through(load_at[key] + 1, it, per_load))

        def weights(key, start, width):
            n = load_at[key] % RING
            return whi[:, n, start:start + width], wlo[:, n, start:start + width]

        def joined(ap, lev, odd):
            w = 1 << lev
            return ap.rearrange("p (c two w) -> p c two w", two=2, w=w)[:, :, odd, :]

        def packed(ap, lev):
            return ap.rearrange("p (c w) -> p c w", w=1 << lev)

        block = ctx.enter_context(nc.Block())

        @block.sync
        def _(sp):
            sp.dma_start(h[:, :, :], x.rearrange("(b p) c -> p b c", p=P)).then_inc(s_in, 16)
            sp.dma_start(cst[:, 0:P], consts[:, 0:P]).then_inc(s_small, 16)
            sp.dma_start(cols[:, :], columns).then_inc(s_small, 16)
            sp.dma_start(rws[:, :], rows).then_inc(s_small, 16)

            def load(src, order, n, it=None):
                if n >= RING:
                    kind, what = plan["until"][order[n - RING]]
                    if kind == "tile":
                        filled(sp, what, it)
                    else:
                        sp.wait_ge(s_used, through(what, it, per_signal))
                sp.dma_start(raw[:, n % RING, :], src).then_inc(s_land[n % RING], 16)

            def expert_slot(e, key):
                return experts[bass.ds(e * per_load + expert_place(key), 1), :, :].rearrange("a p f -> (a p) f")

            def of_round(e, following, it):
                for k in range(RING, per_load + RING):
                    key = plan["each"][k % per_load]
                    of_next = k >= per_load or key[0] in "AB" and key[2] == 0
                    load(expert_slot(following if of_next else e, key), in_round + plan["each"], n_before + k, it)

            for n in range(n_before + RING):
                key = in_round[n]
                load(experts[expert_place(key)] if n >= n_stream else stream[n], in_round, n)
                if n == 2:
                    sp.dma_start(cst[:, P:NCONST], consts[:, P:NCONST]).then_inc(s_cst, 16)
            with sp.Fori(0, NE - 1) as e:
                of_round(e, e + 1, e)
            sp.wait_ge(s_tab, 1)
            more = sp.value_load(table[0:1, MORE + 2:MORE + 3], min_val=0, max_val=MORE)
            with sp.If(more > 0):
                with sp.Fori(0, more) as r:
                    e = sp.value_load(table[0:1, bass.ds(r, 1)], min_val=0, max_val=NE - 1)
                    following = sp.value_load(table[0:1, bass.ds(r + 1, 1)], min_val=0, max_val=NE - 1)
                    of_round(e, following, r + NE - 1)
            e = sp.value_load(table[0:1, bass.ds(more, 1)], min_val=0, max_val=NE - 1)
            for k in range(RING, len(plan["after"])):
                key = plan["after"][k]
                load(expert_slot(e, key) if k < plan["last"] else stream[n_stream + k - plan["last"]], after,
                     n_before + k, more + NE - 1)
            filled(sp, ("WO", 1, 1, 1))
            sp.dma_start(finw, final_w).then_inc(s_fw, 16)
            for b in range(NB):
                sp.wait_ge(s_res, b + 1)
                sp.dma_start(out[P * b:P * b + P, :], res[:, b, :]).then_inc(s_out, 16)
            sp.wait_ge(s_out, 16 * NB)

        @block.gpsimd
        def _(pool):
            st = Count(s_pstep)

            def rstd(occ):
                pool.wait_ge(s_sumsq, NB * (occ + 1))
                nc.gpsimd.tensor_scalar(area("rs", 66, 2), area("rs", 64, 2), 1.0 / D, EPS, ALU.mult,
                                        ALU.add).then_inc(st.sem, st.up())
                pool.wait_ge(st.sem, st.n)
                nc.gpsimd.tensor_tensor(area("rstd", 0, 2), area("rs", 66, 2), area("rs", 32, 2), ALU.pow).then_inc(s_rstd, 1)

            def head_rstd(L, n):
                _, count, start = HEAD_PARTS[n]
                width = NB * count
                pool.wait_ge(s_oss, 3 * L + n + 1)
                nc.gpsimd.tensor_scalar(area("ss", 32 + start, width), area("ss", start, width), 1.0 / HD, EPS, ALU.mult,
                                        ALU.add).then_inc(st.sem, st.up())
                pool.wait_ge(st.sem, st.n)
                nc.gpsimd.tensor_tensor(area("rs", start, width), area("ss", 32 + start, width), area("rs", 32, width),
                                        ALU.pow).then_inc(s_ors, 1)

            def mixers(L):
                rstd(3 * L)
                if L == 0:
                    pool.wait_ge(s_cst, 16)
                for g in range(GS):
                    pool.wait_ge(s_dexp, GS * L + g + 1)
                    d = dec[:, GW * g:GW * g + GW].rearrange("p (s i) -> p s i", s=3)
                    nc.gpsimd.tensor_tensor(d, d, cc("upto").unsqueeze(1).broadcast_to([P, 3, P]),
                                            ALU.mult).then_inc(s_dec, 1)
                for lev in range(NLEV):
                    if lev == NLEV - 1:
                        head_rstd(L, 0)
                    for g in range(GS):
                        if lev == 0:
                            drained(pool, ("KK", L, g), "v")
                            filled(pool, ("D", L, HW - 1))
                        elif lev == 1:
                            drained(pool, ("C0", L, g), "v")
                        else:
                            filled(pool, ("P", L, lev - 1, g))
                        m = cc("levels", lev * P, P).unsqueeze(1).broadcast_to([P, 3, P])
                        nc.gpsimd.tensor_tensor(cm[:, GW * g:GW * g + GW].rearrange("p (s i) -> p s i", s=3),
                                                mt[:, GW * g:GW * g + GW].rearrange("p (s i) -> p s i", s=3),
                                                m, ALU.mult).then_inc(s_cm, 1)
                head_rstd(L, 1)
                head_rstd(L, 2)

            nc.gpsimd.memset(area("rs", 32, 32), -0.5).then_inc(st.sem, st.up())
            pool.wait_ge(st.sem, st.n)
            mixers(0)
            rstd(1)
            rstd(2)
            mixers(1)
            rstd(4)
            rstd(5)
            rstd(6)

        def residual_ready(eng, occ, b, items):
            if occ in (1, 4):
                drained(eng, ("WO", occ // 3, b, 1), "v")
            elif occ == 2:
                drained(eng, ("Y2", b, 1), "v")
            elif occ == 5:
                drained(eng, ("SC", "last", b, 1), "v", items)
            elif occ in (3, 6):
                eng.wait_ge(s_ple, 4 * (occ // 3) - 1 + b)

        @block.scalar
        def _(act):
            st = Count(s_astep)
            split = Split(split_upper)

            def norm(occ, items=None):
                if occ == 0:
                    act.wait_ge(s_in, 16)
                for b in range(NB):
                    residual_ready(act, occ, b, items)
                    nc.scalar.activation(hn[:, b, :], h[:, b, :], ACT.Square,
                                         accum_out=area("rs", 64 + b, 1)).then_inc(s_sumsq, 1)
                if occ == 6:
                    return
                act.wait_ge(s_rstd, occ + 1)
                if occ == 0:
                    act.wait_ge(s_small, 48)
                nc.scalar.activation(hn[:, 0, :], h[:, 0, :], ACT.Copy,
                                     scale=area("rstd", 0, 1)).then_inc(s_hn["a"], 1)
                for c in range(4):
                    key = ("T", occ, c)
                    filled(act, key, items)
                    for k in (2 * c, 2 * c + 1):
                        ins = nc.scalar.activation(xh[:, T * k:T * k + T], bank(key, T * (k % 2), T), ACT.Copy,
                                                   scale=col(COL_NORM(occ) + k))
                    ins.then_inc(s_free["a"], 1)

            def token_major(L, g):
                for b in range(NB):
                    key = ("J", L, b, g)
                    filled(act, key)
                    if g == 0:
                        nc.scalar.copy(zt[:, b, :], bank(key, 0, DG))
                        ins = nc.scalar.copy(ab[:, b, :], bank(key, DG, 2 * HG))
                    elif g == 1:
                        ins = nc.scalar.copy(dva[:, b, :, 0:HD], bank(key, 0, DW).rearrange("p (h e) -> p h e", h=HW))
                    else:
                        ins = nc.scalar.copy(sva[:, b, :], bank(key, 0, DS))
                    ins.then_inc(s_free["a"], 1)
                split.behind(key)

            def mixers(L):
                norm(3 * L)
                split.behind(("T", 3 * L, 3))
                token_major(L, 0)
                act.wait_ge(s_gin, L + 1)
                nc.scalar.activation(area("em"), area("em"), ACT.Exp).then_inc(s_gexp, 1)
                act.wait_ge(s_gadd, L + 1)
                nc.scalar.activation(area("lnp"), area("e1", 0, 12), ACT.Ln).then_inc(s_gln, 1)

                def channels(t):
                    filled(act, ("I", L, t))
                    for c in (2 * t, 2 * t + 1):
                        if c < CQ + CA:
                            dst = xc[:, c, 3:3 + T] if c < CQ else att[:, c - CQ, :]
                            ins = nc.scalar.copy(dst, bank(("I", L, t), T * (c % 2), T))
                    ins.then_inc(s_free["a"], 1)
                    split.behind(("I", L, t))

                def silu(j):
                    act.wait_ge(s_conv, CQ * L + 3 * j + 3)
                    v = qkv[:, 3 * j:3 * j + 3, :]
                    nc.scalar.activation(v, v, ACT.Silu).then_inc(s_silu, 1)

                for t in range(5):
                    channels(t)
                    if t == 2:
                        silu(0)
                silu(1)
                act.wait_ge(s_gx, L + 1)
                nc.scalar.activation(area("eg"), area("gx"), ACT.Exp).then_inc(s_eg, 1)
                for g in range(GS):
                    drained(act, ("R", L, g), "v")
                    d = dec[:, GW * g:GW * g + GW]
                    nc.scalar.activation(d, d, ACT.Exp).then_inc(s_dexp, 1)
                split.behind(("I", L, 5))
                silu(2)
                drained(act, ("J", L, 1, 0), "a")
                nc.scalar.activation(area("z"), area("z"), ACT.Silu).then_inc(s_zg, 1)
                channels(6)
                if L == 0:
                    act.wait_ge(s_cst, 16)
                for c in range(3):
                    filled(act, ("N2", L, c))
                    nc.scalar.activation(pbuf[:, 512 * c:512 * c + 512], bank(("N2", L, c)), ACT.Sqrt,
                                         bias=cc("eps")).then_inc(s_free["a"], 1)
                split.behind(("I", L, 7))
                for b in range(NB):
                    filled(act, ("V", L, b))
                    nc.scalar.copy(vt[:, b, :], bank(("V", L, b), 0, DG)).then_inc(s_free["a"], 1)
                channels(8)
                split.behind(("I", L, 9))
                token_major(L, 1)
                token_major(L, 2)

                def beside(kind, k):
                    if kind == "exp":
                        act.wait_ge(s_nm, 2 * L + k // 3 + 1)
                        for b in range(NB):
                            v = prob[:, k, 0:P] if b == 0 else prob[:, k, P:384]
                            ins = nc.scalar.activation(v, v, ACT.Exp, scale=SCALE, bias=area("nm", HW * b + k, 1))
                        ins.then_inc(s_dex, 1)
                    elif kind == "E":
                        filled(act, ("E", L, k))
                        nc.scalar.copy(prob[:, k, :], bank(("E", L, k), 0, 384)).then_inc(s_free["a"], 1)
                    elif kind == "Z":
                        filled(act, ("Z", L, k))
                        nc.scalar.activation(es[:, k, :], bank(("Z", L, k), 0, 384), ACT.Abs, scale=SCALE)
                        nc.scalar.mul(zs[:, k, :], bank(("Z", L, k), 0, 384), SCALE).then_inc(s_free["a"], 1)
                    elif kind == "log1p":
                        drained(act, ("Z", L, HS - 1), "a")
                        nc.scalar.activation(es, es, ACT.Exp, scale=-1.0).then_inc(st.sem, st.up())
                        act.wait_ge(st.sem, st.n)
                        nc.scalar.activation(es, es, ACT.Ln, bias=1.0).then_inc(s_zl, 1)

                for lev in range(1, NLEV):
                    for g in range(GS):
                        at = slice(GW * g, GW * g + GW)
                        filled(act, ("P", L, lev, g))
                        if lev == 1:
                            act.wait_ge(s_qk, 3 * L + 3)
                        nc.scalar.copy(pbuf[:, at], bank(("P", L, lev, g), 0, GW)).then_inc(s_free["a"], 1)
                        if lev > 1:
                            filled(act, ("Y", L, lev - 1, g))
                            nc.scalar.copy(xt[:, at], bank(("Y", L, lev - 1, g), 0, GW)).then_inc(s_free["a"], 1)
                    for g in range(GS):
                        for kind, k in aside(lev, g):
                            beside(kind, k)

                def grown(k):
                    drained(act, ("CS", L, k), "v")
                    nc.scalar.activation(zs[:, k, :], zs[:, k, :], ACT.Exp).then_inc(s_ze, 1)

                grown(0)
                filled(act, ("S", L))
                nc.scalar.copy(s1, bank(("S", L), 0, 192)).then_inc(s_free["a"], 1)
                grown(1)
                grown(2)
                for parity in range(2):
                    key = (f"QS{parity}", L)
                    filled(act, key)
                    for k in range(parity, HG, 2):
                        ins = nc.scalar.activation(qs[:, k * HD:k * HD + HD], bank(key, k // 2 * HD, HD), ACT.Copy,
                                                   scale=area("eg", k, 1))
                    ins.then_inc(s_free["a"], 1)
                grown(3)
                filled(act, ("O0", L))
                nc.scalar.copy(o[:, 0, 0:DG], bank(("O0", L), 0, DG)).then_inc(s_free["a"], 1)
                filled(act, ("U", L))
                nc.scalar.copy(o[:, :, DG + DW:D],
                               bank(("U", L)).rearrange("p (b c) -> p b c", b=NB)).then_inc(s_free["a"], 1)
                for c in range(4):
                    filled(act, ("OT", L, c))
                    nc.scalar.copy(xh[:, 512 * c:512 * c + 512], bank(("OT", L, c))).then_inc(s_free["a"], 1)
                split.behind(("WO", L, 1, 0))

            def ple(L, items=None):
                split.behind(("PP", L, 1, 1), items)
                for m in range(2):
                    for b in range(NB):
                        key = ("PG", L, b, m)
                        filled(act, key, items)
                        if m:
                            drained(act, ("PP", L, b, 0), "v", items)
                        nc.scalar.activation(sig[b], bank(key), ACT.Sigmoid).then_inc(s_free["a"], 1)
                    if m == 0:
                        split.behind(key, items)

            mixers(0)
            norm(1)
            split.behind(("WO", 0, 1, 1))
            for f in range(NF):
                filled(act, ("H", f))
                if f >= 2:
                    drained(act, ("H", f - 2), "v")
                nc.scalar.activation(ffs[f % 2], bank(("H", f), 0, T), ACT.Silu).then_inc(s_free["a"], 1)
                split.behind(("H", f))
            norm(2)
            nc.scalar.copy(rh, cols[:, COL_ROUTER:NCOL]).then_inc(s_router, 1)
            split.behind(("Y2", 1, 1))
            ple(0)
            mixers(1)
            norm(4)
            split.behind(("WO", 1, 1, 1))
            filled(act, ("LG",))
            nc.scalar.copy(logits, bank(("LG",), 0, T)[0:NE]).then_inc(s_free["a"], 1)
            act.wait_ge(s_lsub, 1)
            nc.scalar.activation(exl, exl, ACT.Exp).then_inc(s_lex, 1)
            split.behind(("LG",))

            def gathered(when, it):
                if when == "each":
                    filled(act, ("B", when, NJ - 1), it)
                for half in range(2):
                    filled(act, ("GA", when, half), it)
                    for q in range(4):
                        k = 4 * half + q
                        ins = nc.scalar.activation(xh[:, P * k:P * k + P], bank(("GA", when, half), P * q, P), ACT.Copy,
                                                   scale=col(COL_NORM(4) + k))
                    ins.then_inc(s_free["a"], 1)

            def scatter_matrix(when, it):
                filled(act, ("GT", when), it)
                nc.scalar.copy(back, bank(("GT", when), 0, T)).then_inc(s_free["a"], 1)

            def silu(ph, j, it):
                key = ("A", ph, j)
                filled(act, key, it)
                nc.scalar.activation(ms[j % 2], bank(key), ACT.Silu).then_inc(s_free["a"], 1)

            def turned(ph, j, it):
                filled(act, ("TT", ph, j), it)
                nc.scalar.copy(mTh[j % 2], bank(("TT", ph, j))).then_inc(s_free["a"], 1)

            def rest_of_item(ph, it):
                for j in range(1, NJ):
                    if j > 2:
                        drained(act, ("B", ph, j - 2), "v", it)
                    elif j == 2:
                        drained(act, ("B", "each", 0), "v", it, 1)
                    silu(ph, j, it)
                    turned(ph, j - 1, it)
                    split.behind(("A", ph, j), it)
                    if j < NJ - 1:
                        split.behind(("B", ph, j), it)
                if ph == "each":
                    gathered(ph, it)
                    split.behind(("B", ph, NJ - 1), it, most=2)
                turned(ph, NJ - 1, it)
                if ph == "each":
                    split.behind(("B", ph, NJ - 1), it)
                    drained(act, ("B", ph, NJ - 1), "v", it)
                    silu(ph, 0, it)
                    split.behind(("A", ph, 0), it)
                else:
                    split.behind(("B", ph, NJ - 1), it)
                for m in range(2):
                    filled(act, ("YY", ph, m), it)
                    nc.scalar.copy(ysb[:, 512 * m:512 * m + 512], bank(("YY", ph, m))).then_inc(s_free["a"], 1)
                if ph == "each":
                    split.behind(("YY", ph, 1), it)
                    scatter_matrix(ph, it)
                    split.behind(("B", ph, 0), it)

            gathered("first", None)
            silu("first", 0, None)
            split.behind(("A", "first", 0))
            scatter_matrix("first", None)
            split.behind(("B", "first", 0))
            drained(act, ("B", "first", 0), "v")
            act.wait_ge(s_tab, 1)
            items = act.value_load(table[0:1, MORE + 3:MORE + 4], min_val=NE - 1, max_val=NE - 1 + MORE)
            split.in_round()
            with act.Fori(0, items) as i:
                rest_of_item("each", i)
            split.after()
            rest_of_item("last", items)
            norm(5, items)
            ple(1, items)
            norm(6)

        @block.vector
        def _(dve):
            st = Count(s_vstep)
            split = Split(split_lower)

            def step():
                dve.wait_ge(st.sem, st.n)

            def norm(occ, items=None):
                dve.wait_ge(s_rstd, occ + 1)
                nc.vector.tensor_scalar(hn[:, 1, :], h[:, 1, :], area("rstd", 1, 1), None, ALU.mult).then_inc(s_hn["v"], 1)
                for c in range(4):
                    key = ("T", occ, c)
                    drained(dve, key, "a", items)
                    for k in (2 * c, 2 * c + 1):
                        ins = nc.vector.scalar_tensor_tensor(out=xl[:, T * k:T * k + T], in0=bank(key, T * (k % 2), T),
                                                             scalar=col(COL_NORM(occ) + k),
                                                             in1=xh[:, T * k:T * k + T].bitcast(F32), op0=ALU.mult,
                                                             op1=ALU.subtract)
                    ins.then_inc(s_free["v"], 1)

            def lower_part(key, hi, lo, it=None):
                drained(dve, key, "a", it)
                nc.vector.tensor_tensor(lo, bank(key), hi.bitcast(F32), ALU.subtract).then_inc(s_free["v"], 1)

            def heads(ap, n=HG):
                return ap.rearrange("p (h e) -> p h e", h=n)

            def per_head(ap, n=HG):
                return ap.unsqueeze(2).broadcast_to([P, n, HD])

            def gates(L):
                drained(dve, ("J", L, 1, 0), "a")
                xa = area("xa").rearrange("p (b h) -> p b h", b=NB)
                dt = rws[:, ROW_DT + L * HG:ROW_DT + (L + 1) * HG].unsqueeze(1).broadcast_to([P, NB, HG])
                nc.vector.tensor_tensor(xa, ab[:, :, 0:HG], dt, ALU.add).then_inc(st.sem, st.up())
                nc.vector.tensor_scalar(area("em", 12, 12).rearrange("p (b h) -> p b h", b=NB), ab[:, :, HG:2 * HG], -1.0,
                                        None, ALU.mult).then_inc(st.sem, st.up())
                nc.vector.tensor_copy(area("em", 24, 6), rws[:, ROW_ALOG + L * HG:ROW_ALOG + (L + 1) * HG]).then_inc(
                    st.sem, st.up())
                step()
                nc.vector.scalar_tensor_tensor(out=area("em", 0, 12), in0=area("xa"), scalar=-1.0, in1=area("xa"),
                                               op0=ALU.mult, op1=ALU.min).then_inc(s_gin, 1)
                dve.wait_ge(s_gexp, L + 1)
                nc.vector.tensor_scalar(area("e1"), area("em", 0, 24), 1.0, None, ALU.add).then_inc(s_gadd, 1)
                dve.wait_ge(s_gadd, L + 1)
                nc.vector.reciprocal(area("beta"), area("e1", 12, 12)).then_inc(st.sem, st.up())
                dve.wait_ge(s_gln, L + 1)
                nc.vector.scalar_tensor_tensor(out=area("xa"), in0=area("xa"), scalar=0.0, in1=area("lnp"), op0=ALU.max,
                                               op1=ALU.add).then_inc(st.sem, st.up())
                step()
                ea = area("em", 24, 6).unsqueeze(1).broadcast_to([P, NB, HG])
                nc.vector.scalar_tensor_tensor(out=area("g").rearrange("p (b h) -> p b h", b=NB), in0=xa, scalar=-1.0,
                                               in1=ea, op0=ALU.mult, op1=ALU.mult).then_inc(s_g, 1)

            def decays(L):
                filled(dve, ("G", L))
                nc.vector.tensor_copy(area("gc"), bank(("G", L), 0, 18)).then_inc(s_free["v"], 1)
                drained(dve, ("G", L), "v")
                nc.vector.tensor_copy(area("gx", 0, 6), area("gc", 6, 6)).then_inc(st.sem, st.up())
                nc.vector.tensor_tensor(area("gx", 6, 6), area("gc", 12, 6), area("gc", 0, 6),
                                        ALU.subtract).then_inc(st.sem, st.up())
                step()
                nc.vector.tensor_scalar(area("gx"), area("gx"), 0.0, None, ALU.min).then_inc(s_gx, 1)
                for g in range(GS):
                    filled(dve, ("R", L, g))
                    for k, b, at in group_heads(g):
                        ins = nc.vector.tensor_scalar(dec[:, system_at(k, b)],
                                                      bank(("R", L, g), at, P), area("gc", b * HG + k, 1), 0.0,
                                                      ALU.subtract, ALU.min)
                    ins.then_inc(s_free["v"], 1)

            def convolved(L, t):
                drained(dve, ("I", L, t), "a")
                chunks = [c for c in (2 * t, 2 * t + 1) if c < CQ]
                for tap in range(CONV):
                    for c in chunks:
                        w = col(COL_CONV + (L * CQ + c) * CONV + tap)
                        if tap == 0:
                            ins = nc.vector.tensor_scalar(qkv[:, c, :], xc[:, c, 0:T], w, None, ALU.mult)
                        else:
                            ins = nc.vector.scalar_tensor_tensor(out=qkv[:, c, :], in0=xc[:, c, tap:tap + T], scalar=w,
                                                                 in1=qkv[:, c, :], op0=ALU.mult, op1=ALU.add)
                        if tap < CONV - 1:
                            ins.then_inc(st.sem, st.up())
                        else:
                            ins.then_inc(s_conv, 1)
                    if tap < CONV - 1:
                        step()

            def squares_of_qk(L):
                dve.wait_ge(s_silu, 3 * L + 2)
                dve.wait_ge(s_conv, CQ * (L + 1))
                nc.vector.tensor_tensor(squares, area("qkv", 0, 1536), area("qkv", 0, 1536), ALU.mult).then_inc(s_sq, 1)

            def qk_normalised(L, c):
                drained(dve, ("N2", L, c), "a")
                nc.vector.reciprocal(pbuf[:, 512 * c:512 * c + 512],
                                     pbuf[:, 512 * c:512 * c + 512]).then_inc(st.sem, st.up())
                step()
                nc.vector.tensor_tensor(area("qkv", 512 * c, 512), area("qkv", 512 * c, 512),
                                        pbuf[:, 512 * c:512 * c + 512], ALU.mult).then_inc(s_qk, 1)

            def delta(L):
                if L == 0:
                    dve.wait_ge(s_cst, 16)
                filled(dve, ("V", L, 2))
                dve.wait_ge(s_eg, L + 1)
                nc.vector.tensor_tensor(heads(kd), heads(bank(("V", L, 2), 0, DG)), per_head(area("eg", 6, 6)),
                                        ALU.mult).then_inc(s_free["v"], 1)
                for g in range(GS):
                    filled(dve, ("KK", L, g))
                    dve.wait_ge(s_dec, GS * L + g + 1)
                    for k, b, at in group_heads(g):
                        ins = nc.vector.scalar_tensor_tensor(out=mt[:, system_at(k, b)], in0=bank(("KK", L, g), at, P),
                                                             scalar=area("beta", b * HG + k, 1),
                                                             in1=dec[:, system_at(k, b)], op0=ALU.mult, op1=ALU.mult)
                    ins.then_inc(s_free["v"], 1)
                for g in range(GS):
                    filled(dve, ("QK", L, g))
                    drained(dve, ("KK", L, g), "v")
                    d = dec[:, GW * g:GW * g + GW]
                    nc.vector.scalar_tensor_tensor(out=d, in0=bank(("QK", L, g), 0, GW), scalar=SCALE, in1=d, op0=ALU.mult,
                                                   op1=ALU.mult).then_inc(s_free["v"], 1)
                for k in range(HW):
                    filled(dve, ("D", L, k))
                    nc.vector.scalar_tensor_tensor(out=prob[:, k, :], in0=cc("dist"), scalar=SLOPES[k] / SCALE,
                                                   in1=bank(("D", L, k), 0, 384), op0=ALU.mult,
                                                   op1=ALU.add).then_inc(s_free["v"], 1)
                eye = ident.unsqueeze(1).broadcast_to([P, 3, P])

                def systems(ap):
                    return ap.rearrange("p (s i) -> p s i", s=3)

                for g in range(GS):
                    at = slice(GW * g, GW * g + GW)
                    dve.wait_ge(s_cm, GS * NLEV * L + g + 1)
                    nc.vector.scalar_tensor_tensor(out=systems(xt[:, at]), in0=systems(cm[:, at]), scalar=-1.0, in1=eye,
                                                   op0=ALU.mult, op1=ALU.add)
                    filled(dve, ("C0", L, g))
                    nc.vector.scalar_tensor_tensor(out=systems(xi[:, at]), in0=systems(bank(("C0", L, g), 0, GW)), scalar=-1.0,
                                                   in1=eye, op0=ALU.mult, op1=ALU.add).then_inc(s_free["v"], 1)

                def beside(kind, k):
                    if kind == "max":
                        some = slice(3 * k, 3 * k + 3)
                        nc.vector.reduce_max(area("rden", 3 * k, 3), prob[:, some, 0:P], AX_X).then_inc(st.sem, st.up())
                        nc.vector.reduce_max(area("rden", HW + 3 * k, 3), prob[:, some, P:384], AX_X).then_inc(
                            st.sem, st.up())
                        step()
                        nc.vector.tensor_scalar(area("nm").rearrange("p (b h) -> p b h", b=NB)[:, :, some],
                                                area("rden").rearrange("p (b h) -> p b h", b=NB)[:, :, some], -SCALE, None,
                                                ALU.mult).then_inc(s_nm, 1)
                    elif kind == "weigh":
                        dve.wait_ge(s_dex, HW * L + k + 1)
                        nc.vector.tensor_tensor(prob[:, k, :], prob[:, k, :], cc("mult"), ALU.mult).then_inc(s_dpr, 1)
                    elif kind == "F":
                        filled(dve, ("F", L, k))
                        f = bank(("F", L, k), 0, NB * (HD + 1)).rearrange("p (b e) -> p b e", b=NB)
                        nc.vector.reciprocal(area("rden", 2 * k, 2), f[:, :, HD]).then_inc(st.sem, st.up())
                        step()
                        nc.vector.tensor_tensor(o[:, :, DG + HD * k:DG + HD * k + HD], f[:, :, 0:HD],
                                                per_head(area("rden", 2 * k, 2), NB), ALU.mult).then_inc(s_free["v"], 1)
                    elif kind == "squares":
                        drained(dve, ("F", L, HW - 1), "v")
                        head_squares(L, 0)
                    elif kind == "scales":
                        head_scales(L, 0)
                    elif kind == "gate":
                        dve.wait_ge(s_zg, L + 1)
                        z = zt.rearrange("p b (h e) -> p b h e", h=HG)
                        nc.vector.tensor_tensor(z, z, head_weight(L, 0), ALU.mult).then_inc(st.sem, st.up())
                    elif kind == "softplus":
                        dve.wait_ge(s_zl, L + 1)
                        nc.vector.scalar_tensor_tensor(out=es[:, k, :], in0=zs[:, k, :], scalar=0.0, in1=es[:, k, :],
                                                       op0=ALU.max, op1=ALU.add).then_inc(st.sem, st.up())
                        step()
                        nc.vector.tensor_tensor(es[:, k, :], es[:, k, :], cc("earlier"), ALU.mult).then_inc(s_sps, 1)

                for lev in range(1, NLEV):
                    for g in range(GS):
                        at = slice(GW * g, GW * g + GW)
                        last = lev == NLEV - 1
                        key = ("Y" if last else "X", L, lev, g)
                        filled(dve, key)
                        v = joined((xt if last else xi)[:, at], lev, int(last))
                        nc.vector.tensor_tensor(v, v, packed(bank(key, 0, GW // 2), lev), ALU.subtract).then_inc(s_free["v"], 1)
                        for kind, k in aside(lev, g):
                            beside(kind, k)
                    if lev in (2, 3, 4, 5):
                        split.behind(("J", L, 1, 2), most=1)

                def kept(k):
                    filled(dve, ("CS", L, k))
                    nc.vector.tensor_tensor(zs[:, k, :], zs[:, k, :], bank(("CS", L, k), 0, 384),
                                            ALU.subtract).then_inc(s_free["v"], 1)

                def causal(k):
                    dve.wait_ge(s_ze, HS * L + k + 1)
                    nc.vector.scalar_tensor_tensor(out=zs[:, k, :], in0=zs[:, k, :], scalar=1.0, in1=cc("earlier"),
                                                   op0=ALU.min, op1=ALU.mult).then_inc(s_aT, 1)

                filled(dve, ("W0", L))
                nc.vector.tensor_tensor(heads(vn[:, 0, :]), heads(bank(("W0", L), 0, DG)), per_head(area("beta", 0, 6)),
                                        ALU.mult).then_inc(s_free["v"], 1)
                kept(0)
                kept(1)
                for parity in range(2):
                    key = (f"KS{parity}", L)
                    filled(dve, key)
                    nc.vector.tensor_tensor(rr.rearrange("p (q two e) -> p q two e", two=2, e=HD)[:, :, parity, :],
                                            heads(bank(key, 0, 3 * HD), 3), per_head(area("eg", 0, 6)[:, parity::2], 3),
                                            ALU.mult).then_inc(s_free["v"], 1)
                drained(dve, ("KS1", L), "v")
                nc.vector.tensor_tensor(rr, vt[:, 1, :], rr, ALU.subtract).then_inc(s_rr, 1)
                kept(2)
                kept(3)
                filled(dve, ("W1", L))
                nc.vector.tensor_tensor(heads(vn[:, 1, :]), heads(bank(("W1", L), 0, DG)), per_head(area("beta", 6, 6)),
                                        ALU.mult).then_inc(s_free["v"], 1)
                causal(0)
                causal(1)
                filled(dve, ("O1", L))
                drained(dve, ("QS1", L), "a")
                nc.vector.scalar_tensor_tensor(out=o[:, 1, 0:DG], in0=qs, scalar=SCALE, in1=bank(("O1", L), 0, DG),
                                               op0=ALU.mult, op1=ALU.add).then_inc(s_free["v"], 1)
                causal(2)
                causal(3)

            def output_heads(L):
                drained(dve, ("O0", L), "a")
                drained(dve, ("O1", L), "v")
                head_squares(L, 1)
                drained(dve, ("U", L), "a")
                head_squares(L, 2)
                turned_output(L, 0)
                head_scales(L, 1)
                turned_output(L, 1)
                turned_output(L, 2)
                head_scales(L, 2)
                turned_output(L, 3)

            def head_columns(n):
                first, count, _ = HEAD_PARTS[n]
                return o[:, :, first:first + count * HD], count

            def head_squares(L, n):
                v, count = head_columns(n)
                width = NB * count
                nc.vector.tensor_tensor(osq[n].rearrange("p (b c) -> p b c", b=NB), v, v, ALU.mult).then_inc(
                    st.sem, st.up())
                step()
                nc.vector.tensor_reduce(area("ss", HEAD_PARTS[n][2], width), osq[n].rearrange("p (h e) -> p h e", e=HD),
                                        AX_X, ALU.add).then_inc(s_oss, 1)

            def head_weight(L, n):
                w = rws[:, ROW_HN(L, n):ROW_HN(L, n) + HD]
                return w.unsqueeze(1).unsqueeze(1).broadcast_to([P, NB, HG if n < 2 else HS, HD])

            def head_scales(L, n):
                v, count = head_columns(n)
                start = HEAD_PARTS[n][2]
                dve.wait_ge(s_ors, 3 * L + n + 1)
                for b in range(NB):
                    vb = heads(v[:, b, :], count)
                    nc.vector.tensor_tensor(vb, vb, per_head(area("rs", start + b * count, count), count),
                                            ALU.mult).then_inc(st.sem, st.up())
                step()
                if n == 1:
                    nc.vector.tensor_tensor(v, v, zt[:, :, :], ALU.mult).then_inc(s_o, 1)
                else:
                    v = v.rearrange("p b (h e) -> p b h e", h=count)
                    nc.vector.tensor_tensor(v, v, head_weight(L, 1 if n == 0 else 2), ALU.mult).then_inc(s_o, 1)

            def turned_output(L, c):
                lower_part(("OT", L, c), xh[:, 512 * c:512 * c + 512], xl[:, 512 * c:512 * c + 512])

            def add_to_residual(key, b, m, it=None):
                filled(dve, key, it)
                v = h[:, b, 512 * m:512 * m + 512]
                nc.vector.tensor_tensor(v, v, bank(key), ALU.add).then_inc(s_free["v"], 1)

            def mixers(L):
                if L:
                    residual_ready(dve, 3 * L, 1, None)
                nc.vector.memset(xc[:, :, 0:3], 0.0).then_inc(st.sem, st.up())
                step()
                norm(3 * L)
                split.behind(("T", 3 * L, 3))
                split.behind(("J", L, 1, 0))
                gates(L)
                for t in range(5):
                    convolved(L, t)
                    split.behind(("I", L, t))
                decays(L)

                def channels(t):
                    filled(dve, ("I", L, t))
                    for c in (2 * t, 2 * t + 1):
                        if c < CQ + CA:
                            ins = nc.vector.tensor_copy(att[:, c - CQ, :], bank(("I", L, t), T * (c % 2), T))
                    ins.then_inc(s_free["v"], 1)
                    split.behind(("I", L, t))

                squares_of_qk(L)
                channels(5)
                split.behind(("I", L, 6))
                qk_normalised(L, 0)
                channels(7)
                qk_normalised(L, 1)
                split.behind(("I", L, 8))
                qk_normalised(L, 2)
                channels(9)
                delta(L)
                output_heads(L)
                for m in range(2):
                    for b in range(NB):
                        add_to_residual(("WO", L, b, m), b, m)
                    if m == 0:
                        split.behind(("WO", L, 1, m))

            def ple(L, items=None):
                split.behind(("PP", L, 1, 1), items)
                for m in range(2):
                    for b in range(NB):
                        drained(dve, ("PG", L, b, m), "a", items)
                        if m:
                            dve.wait_ge(s_ple, 4 * L + b + 1)
                        nc.vector.tensor_tensor(sgp[b], sig[b], bank(("PP", L, b, m)), ALU.mult).then_inc(s_free["v"], 1)
                        drained(dve, ("PP", L, b, m), "v", items)
                        v = h[:, b, 512 * m:512 * m + 512]
                        nc.vector.tensor_tensor(v, v, sgp[b], ALU.add).then_inc(s_ple, 1)
                    if m == 0:
                        split.behind(("PG", L, 1, m), items)

            dve.wait_ge(s_in, 16)
            dve.wait_ge(s_small, 48)
            nc.vector.memset(dva[:, :, :, HD], 1.0).then_inc(st.sem, st.up())
            mixers(0)
            norm(1)
            split.behind(("WO", 0, 1, 1))
            for f in range(NF):
                drained(dve, ("H", f), "a")
                if f >= 2:
                    dve.wait_ge(s_ffg, f - 1)
                nc.vector.tensor_tensor(ffp[f % 2], ffs[f % 2], bank(("H", f), T, T), ALU.mult).then_inc(s_free["v"], 1)
                drained(dve, ("H", f), "v")
                nc.vector.tensor_copy(gh[:, f % 2, :], ffp[f % 2]).then_inc(st.sem, st.up())
                step()
                nc.vector.tensor_tensor(gl[:, f % 2, :], ffp[f % 2], gh[:, f % 2, :].bitcast(F32),
                                        ALU.subtract).then_inc(s_ffg, 1)
                split.behind(("H", f))
            for m in range(2):
                for b in range(NB):
                    add_to_residual(("Y2", b, m), b, m)
            norm(2)
            dve.wait_ge(s_router, 1)
            nc.vector.tensor_tensor(rl, cols[:, COL_ROUTER:NCOL], rh.bitcast(F32), ALU.subtract).then_inc(s_router, 1)
            split.behind(("Y2", 1, 1))
            ple(0)
            mixers(1)
            norm(4)
            split.behind(("WO", 1, 1, 1))

            def selection(i):
                for b in range(NB):
                    p = posi[:, b, bass.ds(i, 1)] if not isinstance(i, int) else posi[:, b, i:i + 1]
                    g = gati[:, b, bass.ds(i, 1)] if not isinstance(i, int) else gati[:, b, i:i + 1]
                    nc.vector.tensor_scalar(pick[:, b, :], cc("slots"), p, None, ALU.is_equal)
                    ins = nc.vector.tensor_scalar(pickg[:, b, :], cc("slots"), p, g, ALU.is_equal, ALU.mult)
                ins.then_inc(s_pick, 1)

            filled(dve, ("LT",))
            nc.vector.tensor_copy(lg, bank(("LT",), 0, 16).rearrange("p (b e) -> p b e", b=NB)).then_inc(s_free["v"], 1)
            drained(dve, ("LT",), "v")
            nc.vector.tensor_reduce(top, lg, AX_X, ALU.max).then_inc(st.sem, st.up())
            other = [lg[:, b, :].unsqueeze(1).broadcast_to([P, NE, NE]) for b in range(NB)]
            own = [lg[:, b, :].unsqueeze(2).broadcast_to([P, NE, NE]) for b in range(NB)]
            lower8 = cc("lower8").rearrange("p (e f) -> p e f", e=NE)
            for b in range(NB):
                nc.vector.tensor_tensor(pairs[0][:, b], other[b], own[b], ALU.is_gt).then_inc(st.sem, st.up())
                nc.vector.tensor_tensor(pairs[1][:, b], other[b], own[b], ALU.is_ge).then_inc(st.sem, st.up())
            step()
            for b in range(NB):
                nc.vector.tensor_tensor(pairs[1][:, b], pairs[1][:, b], lower8, ALU.mult).then_inc(st.sem, st.up())
            nc.vector.tensor_tensor(exl, lg, top.unsqueeze(2).broadcast_to([P, NB, NE]), ALU.subtract).then_inc(s_lsub, 1)
            step()
            for b in range(NB):
                nc.vector.tensor_tensor(pairs[0][:, b], pairs[0][:, b], pairs[1][:, b], ALU.max).then_inc(st.sem, st.up())
            step()
            nc.vector.tensor_reduce(rank, pairs[0], AX_X, ALU.add).then_inc(st.sem, st.up())
            step()
            nc.vector.tensor_scalar(sel, rank, TOPK - 0.5, None, ALU.is_lt).then_inc(s_sel, 1)
            dve.wait_ge(s_sel, 1)
            dve.wait_ge(s_lex, 1)
            nc.vector.tensor_tensor(exl, exl, sel, ALU.mult).then_inc(st.sem, st.up())
            step()
            nc.vector.tensor_reduce(den, exl, AX_X, ALU.add).then_inc(st.sem, st.up())
            step()
            nc.vector.reciprocal(den, den).then_inc(st.sem, st.up())
            step()
            nc.vector.tensor_tensor(gate, exl, den.unsqueeze(2).broadcast_to([P, NB, NE]),
                                    ALU.mult).then_inc(st.sem, st.up())
            filled(dve, ("POS",))
            nc.vector.tensor_copy(cum, bank(("POS",), 0, 24)).then_inc(s_free["v"], 1)
            drained(dve, ("POS",), "v")
            nc.vector.tensor_tensor(pos1, cum[:, 0:16].rearrange("p (b e) -> p b e", b=NB), sel,
                                    ALU.mult).then_inc(st.sem, st.up())
            step()
            nc.vector.tensor_scalar(posi[:, :, 0:NE], pos1, -1.0, None, ALU.add).then_inc(st.sem, st.up())
            nc.vector.tensor_copy(gati[:, :, 0:NE], gate).then_inc(st.sem, st.up())
            step()
            selection(0)
            nc.vector.tensor_scalar(over, cum[:, 16:24], P + 0.5, None, ALU.is_gt).then_inc(st.sem, st.up())
            step()
            nc.vector.tensor_tensor(pairs[0][:, 0], over.unsqueeze(1).broadcast_to([P, NE, NE]), lower8,
                                    ALU.mult).then_inc(st.sem, st.up())
            step()
            nc.vector.tensor_reduce(oidx, pairs[0][:, 0], AX_X, ALU.add).then_inc(st.sem, st.up())
            step()
            shape = [P, MORE + 1, NE]
            nc.vector.tensor_tensor(osel, oidx.unsqueeze(1).broadcast_to(shape), cc("item").unsqueeze(2).broadcast_to(shape),
                                    ALU.is_equal).then_inc(st.sem, st.up())
            step()
            nc.vector.tensor_tensor(osel, osel, over.unsqueeze(1).broadcast_to(shape), ALU.mult).then_inc(st.sem, st.up())
            step()
            for b in range(NB):
                nc.vector.tensor_tensor(oprd[:, b], osel, pos1[:, b, :].unsqueeze(1).broadcast_to(shape),
                                        ALU.mult).then_inc(st.sem, st.up())
                nc.vector.tensor_tensor(oprd[:, 2 + b], osel, gate[:, b, :].unsqueeze(1).broadcast_to(shape),
                                        ALU.mult).then_inc(st.sem, st.up())
            nc.vector.tensor_tensor(oprd[:, 4], osel, cc("expert").unsqueeze(1).broadcast_to(shape),
                                    ALU.mult).then_inc(st.sem, st.up())
            nc.vector.tensor_reduce(tabf[:, MORE + 2:MORE + 3], over, AX_X, ALU.add).then_inc(st.sem, st.up())
            step()
            nc.vector.tensor_reduce(posi[:, :, NE:NI], oprd[:, 0:2], AX_X, ALU.add).then_inc(st.sem, st.up())
            nc.vector.tensor_reduce(gati[:, :, NE:NI], oprd[:, 2:4], AX_X, ALU.add).then_inc(st.sem, st.up())
            nc.vector.tensor_reduce(tabf[:, 1:MORE + 2], oprd[:, 4], AX_X, ALU.add).then_inc(st.sem, st.up())
            nc.vector.tensor_scalar(tabf[:, 0:1], tabf[:, MORE + 2:MORE + 3], 0.0, NE - 1.0, ALU.mult,
                                    ALU.add).then_inc(st.sem, st.up())
            nc.vector.tensor_scalar(tabf[:, MORE + 3:MORE + 4], tabf[:, MORE + 2:MORE + 3], NE - 1.0, None,
                                    ALU.add).then_inc(st.sem, st.up())
            step()
            nc.vector.tensor_scalar(posi[:, :, NE:NI], posi[:, :, NE:NI], -1.0 - P, None,
                                    ALU.add).then_inc(st.sem, st.up())
            nc.vector.tensor_copy(table[0:1, 0:MORE + 4], tabf[0:1, 0:MORE + 4]).then_inc(s_tab, 1)
            step()

            def gathered(when, it):
                for half in range(2):
                    drained(dve, ("GA", when, half), "a", it)
                    for q in range(4):
                        k = 4 * half + q
                        ins = nc.vector.scalar_tensor_tensor(out=xl[:, P * k:P * k + P], in0=bank(("GA", when, half), P * q, P),
                                                             scalar=col(COL_NORM(4) + k),
                                                             in1=xh[:, P * k:P * k + P].bitcast(F32), op0=ALU.mult,
                                                             op1=ALU.subtract)
                    ins.then_inc(s_free["v"], 1)

            def product(ph, j, it):
                drained(dve, ("A", ph, j), "a", it)
                filled(dve, ("B", ph, j), it)
                nc.vector.tensor_tensor(mg[j % 2], ms[j % 2], bank(("B", ph, j)), ALU.mult).then_inc(s_free["v"], 1)

            def turned(ph, j, it):
                lower_part(("TT", ph, j), mTh[j % 2], mTl[j % 2], it)

            def rest_of_item(ph, it):
                for j in range(1, NJ):
                    turned(ph, j - 1, it)
                    split.behind(("A", ph, j), it)
                    product(ph, j, it)
                    if j < NJ - 1:
                        split.behind(("B", ph, j), it)
                if ph == "each":
                    gathered(ph, it)
                    split.behind(("B", ph, NJ - 1), it, most=2)
                turned(ph, NJ - 1, it)
                if ph == "each":
                    split.behind(("B", ph, NJ - 1), it)
                    split.behind(("A", ph, 0), it)
                    split.behind(("YY", ph, 1), it)
                    product(ph, 0, it)
                else:
                    split.behind(("B", ph, NJ - 1), it)
                for m in range(2):
                    for b in range(NB):
                        add_to_residual(("SC", ph, b, m), b, m, it)
                if ph == "each":
                    split.behind(("B", ph, 0), it)

            gathered("first", None)
            split.behind(("LG",))
            split.behind(("A", "first", 0))
            product("first", 0, None)
            split.behind(("B", "first", 0))
            dve.wait_ge(s_tab, 1)
            items = dve.value_load(table[0:1, MORE + 3:MORE + 4], min_val=NE - 1, max_val=NE - 1 + MORE)
            split.in_round()
            with dve.Fori(0, items) as i:
                filled(dve, ("GT", "each"), i, 1)
                selection(i + 1)
                rest_of_item("each", i)
            split.after()
            rest_of_item("last", items)
            norm(5, items)
            ple(1, items)
            dve.wait_ge(s_rstd, 7)
            dve.wait_ge(s_fw, 16)
            for b in range(NB):
                nc.vector.scalar_tensor_tensor(out=res[:, b, :], in0=h[:, b, :], scalar=area("rstd", b, 1), in1=finw,
                                               op0=ALU.mult, op1=ALU.mult).then_inc(s_res, 1)

        @block.tensor
        def _(pe):
            def opened(key, it=None):
                before = tiles.at[key]["before"]
                if before is None:
                    return
                back = tiles.at[key]["back"]
                for who, count in before["drained"].items():
                    pe.wait_ge(s_free[who], through(count - back * per_drain[who], it, per_drain[who]))

            def norm(occ, items=None):
                for c in range(4):
                    opened(("T", occ, c), items)
                    if c == 0:
                        pe.wait_ge(s_hn["a"], occ + 1)
                        pe.wait_ge(s_hn["v"], occ + 1)
                    for q in range(4):
                        k, b = 2 * c + q // 2, q % 2
                        ins = pe.transpose(bank(("T", occ, c), P * q, P), hn[:, b, P * k:P * k + P], ident)
                    ins.then_inc(s_fill, 1)

            def chunk_ready(turned, k, items=None):
                if turned is not None and k % 2 == 0:
                    drained(pe, turned + (k // 2,), "v", items)

            def product(out, a, b, start, stop):
                (ah, al), (bh, bl) = a, b
                pe.matmul(out, ah, bh, start=start, stop=False)
                pe.matmul(out, ah, bl, start=False, stop=False)
                return pe.matmul(out, al, bh, start=False, stop=stop)

            def x_part(start, width):
                return xh[:, start:start + width], xl[:, start:start + width]

            def both_blocks(keys, name, width, items=None, turned=None):
                for half in range(2):
                    ready(pe, name + (half,), items)
                    for b, key in enumerate(keys):
                        if half == 0:
                            opened(key, items)
                        for q in range(4):
                            k = 4 * half + q
                            if b == 0:
                                chunk_ready(turned, k, items)
                            ins = product(bank(key, 0, width), x_part(T * k + P * b, P),
                                          weights(name + (half,), width * q, width), k == 0, k == KC - 1)
                        if half:
                            ins.then_inc(s_fill, 1)
                    if half == 0:
                        ins.then_inc(s_used, 1)

            def projections(L):
                def token_major(g, width, turned=None):
                    both_blocks([("J", L, b, g) for b in range(NB)], ("J", L, g), width, None, turned)

                token_major(0, DG + 2 * HG, ("T", 3 * L))

                def channels(t):
                    ready(pe, ("I", L, t))
                    opened(("I", L, t))
                    for c in (2 * t, 2 * t + 1):
                        if c < CQ + CA:
                            for k in range(KC):
                                ins = product(bank(("I", L, t), T * (c % 2), T),
                                              weights(("I", L, t), P * (KC * (c % 2) + k), P), x_part(T * k, T), k == 0,
                                              k == KC - 1)
                    ins.then_inc(s_fill, 1)

                for t in range(5):
                    channels(t)
                opened(("G", L))
                if L == 0:
                    pe.wait_ge(s_cst, 16)
                pe.wait_ge(s_g, L + 1)
                g12 = area("g")
                for b in range(NB):
                    pe.matmul(bank(("G", L), HG * b, HG), cc("upto"), g12[:, HG * b:HG * b + HG], start=True, stop=True)
                pe.matmul(bank(("G", L), 2 * HG, HG), ones, g12[:, 0:HG], start=True, stop=True).then_inc(s_fill, 1)
                for g in range(GS):
                    opened(("R", L, g))
                    for k, b, at in group_heads(g):
                        ins = pe.matmul(bank(("R", L, g), at, P), area("g", b * HG + k, 1).broadcast_to([P, P]),
                                        cc("upto"), start=True, stop=True)
                    ins.then_inc(s_fill, 1)
                channels(5)
                channels(6)
                for c in range(3):
                    opened(("N2", L, c))
                    pe.wait_ge(s_sq, L + 1)
                    pe.matmul(bank(("N2", L, c)), cc("headsum"), squares[:, 512 * c:512 * c + 512], start=True,
                              stop=True).then_inc(s_fill, 1)
                channels(7)
                turned_qkv(L, 0)
                turned_qkv(L, 1)
                channels(8)
                channels(9)
                token_major(1, DW)
                token_major(2, DS)
                turned_qkv(L, 2)

            def turned_qkv(L, c):
                opened(("V", L, c))
                if c == 0:
                    pe.wait_ge(s_silu, 3 * L + 3)
                if c == 2:
                    pe.wait_ge(s_qk, 3 * L + 3)
                for k in range(3):
                    src = qkv[:, 6 + k, P * c:P * c + P] if c < 2 else qkv[:, 3 + k, 0:P]
                    ins = pe.transpose(bank(("V", L, c), P * k, P), src, ident)
                ins.then_inc(s_fill, 1)

            def lanes(k):
                return slice(HD * (k % 2), HD * (k % 2) + HD)

            def delta(L):
                for kind, first in (("KK", 3), ("QK", 0)):
                    for g in range(GS):
                        opened((kind, L, g))
                        for k, b, at in group_heads(g):
                            tok = slice(P * b, P * b + P)
                            ins = pe.matmul(bank((kind, L, g), at, P), qkv[lanes(k), 3 + k // 2, tok],
                                            qkv[lanes(k), first + k // 2, tok], start=True, stop=True)
                        ins.then_inc(s_fill, 1)

                for k in range(HW):
                    opened(("D", L, k))
                    q, kk = att[lanes(k), k // 2, :], att[lanes(k), 3 + k // 2, :]
                    pe.matmul(bank(("D", L, k), 0, P), q[:, 0:P], kk[:, 0:P], start=True, stop=True)
                    pe.matmul(bank(("D", L, k), P, T), q[:, P:T], kk, start=True, stop=True).then_inc(s_fill, 1)

                def group(kind, lev, g, lhs, rhs):
                    key = (kind, L, g) if lev is None else (kind, L, lev, g)
                    opened(key)
                    for s in range(3):
                        at = slice(GW * g + P * s, GW * g + P * s + P)
                        if rhs is None:
                            ins = pe.transpose(bank(key, P * s, P), lhs[:, at], ident)
                        else:
                            ins = pe.matmul(bank(key, P * s, P), lhs[:, at], rhs[:, at], start=True, stop=True)
                    ins.then_inc(s_fill, 1)

                def update(kind, lev, g, lhs, rhs, odd):
                    key = (kind, L, lev, g)
                    opened(key)
                    for s in range(3):
                        at = slice(GW * g + P * s, GW * g + P * s + P)
                        ins = pe.matmul(packed(bank(key, P // 2 * s, P // 2), lev), lhs[:, at], joined(rhs[:, at], lev, odd),
                                        start=True, stop=True)
                    ins.then_inc(s_fill, 1)

                def beside(kind, k):
                    if kind in WHO_ASIDE:
                        opened((kind, L, k))
                    if kind == "E":
                        pe.wait_ge(s_dpr, HW * L + k + 1)
                        for s in range(3):
                            ins = pe.transpose(bank(("E", L, k), P * s, P), prob[:, k, P * s:P * s + P], ident)
                        ins.then_inc(s_fill, 1)
                    elif kind == "F":
                        drained(pe, ("E", L, k), "a")
                        w = HD + 1
                        pe.matmul(bank(("F", L, k), 0, w), prob[:, k, 0:P], dva[:, 0, k, :], start=True, stop=True)
                        pe.matmul(bank(("F", L, k), w, w), prob[:, k, P:T], dva[:, 0, k, :], start=True, stop=False)
                        pe.matmul(bank(("F", L, k), w, w), prob[:, k, T:384], dva[:, 1, k, :], start=False,
                                  stop=True).then_inc(s_fill, 1)
                    elif kind == "Z":
                        q, kk = att[lanes(k), 6 + k // 2, :], att[lanes(k), 8 + k // 2, :]
                        pe.matmul(bank(("Z", L, k), 0, T), kk[:, 0:P], q, start=True, stop=True)
                        pe.matmul(bank(("Z", L, k), T, P), kk[:, P:T], q[:, P:T], start=True, stop=True).then_inc(s_fill, 1)

                def suffix_sums(k):
                    opened(("CS", L, k))
                    pe.wait_ge(s_sps, HS * L + k + 1)
                    pe.matmul(bank(("CS", L, k), 0, 384), cc("from"), es[:, k, :], start=True, stop=False)
                    pe.matmul(bank(("CS", L, k), P, P), ones, es[:, k, T:384], start=False, stop=True).then_inc(s_fill, 1)

                for g in range(GS):
                    pe.wait_ge(s_cm, GS * NLEV * L + g + 1)
                    group("C0", None, g, cm, None)
                for lev in range(1, NLEV):
                    for g in range(GS):
                        pe.wait_ge(s_cm, GS * NLEV * L + GS * lev + g + 1)
                        drained(pe, ("C0", L, g) if lev == 1 else ("X", L, lev - 1, g), "v")
                        group("P", lev, g, cm, xi)
                        if lev > 1:
                            group("Y", lev - 1, g, xi, None)
                    for g in range(GS):
                        drained(pe, ("P", L, lev, g), "a")
                        if lev > 1:
                            drained(pe, ("Y", L, lev - 1, g), "a")
                        if lev < NLEV - 1:
                            update("X", lev, g, xt, pbuf, 0)
                        else:
                            update("Y", lev, g, pbuf, xt, 1)
                        for kind, k in aside(lev, g):
                            beside(kind, k)

                def heads_of(key, wait, lhs, rhs, out=None, which=range(HG)):
                    opened(key)
                    wait()
                    for n, k in enumerate(which):
                        dst = bank(key, HD * n, HD) if out is None else out(k)
                        ins = pe.matmul(dst, lhs(k), rhs(k), start=True, stop=True)
                    ins.then_inc(s_fill, 1)

                def system(ap, b):
                    return lambda k: ap[:, system_at(k, b)]

                def state(k):
                    return s1[lanes(k), HD * (k // 2):HD * (k // 2) + HD]

                drained_y = lambda: [drained(pe, ("Y", L, NLEV - 1, g), "v") for g in range(GS)]
                heads_of(("W0", L), lambda: (drained_y(), drained(pe, ("V", L, 0), "a")), system(xt, 0),
                         lambda k: vt[:, 0, HD * k:HD * k + HD])
                suffix_sums(0)
                heads_of(("S", L), lambda: drained(pe, ("W0", L), "v"), lambda k: kd[:, HD * k:HD * k + HD],
                         lambda k: vn[:, 0, HD * k:HD * k + HD],
                         lambda k: ps[lanes(k), tiles.at[("S", L)]["bank"], HD * (k // 2):HD * (k // 2) + HD])
                suffix_sums(1)
                for name, first in (("KS", 3), ("QS", 0)):
                    for parity in range(2):
                        heads_of((f"{name}{parity}", L), lambda: drained(pe, ("S", L), "a"),
                                 lambda k: qkv[lanes(k), first + k // 2, P:T], state, which=range(parity, HG, 2))
                    suffix_sums(2 if name == "KS" else 3)
                heads_of(("W1", L), lambda: pe.wait_ge(s_rr, L + 1), system(xt, 1), lambda k: rr[:, HD * k:HD * k + HD])
                heads_of(("O0", L), lambda: None, system(dec, 0), lambda k: vn[:, 0, HD * k:HD * k + HD])
                heads_of(("O1", L), lambda: drained(pe, ("W1", L), "v"), system(dec, 1),
                         lambda k: vn[:, 1, HD * k:HD * k + HD])
                opened(("U", L))
                for k in range(HS):
                    pe.wait_ge(s_aT, HS * L + k + 1)
                    v = sva[:, :, HD * k:HD * k + HD]
                    pe.matmul(bank(("U", L), HD * k, HD), zs[:, k, 0:P], v[:, 0, :], start=True, stop=True)
                    pe.matmul(bank(("U", L), DS + HD * k, HD), zs[:, k, P:T], v[:, 0, :], start=True, stop=False)
                    ins = pe.matmul(bank(("U", L), DS + HD * k, HD), zs[:, k, T:384], v[:, 1, :], start=False, stop=True)
                ins.then_inc(s_fill, 1)

            def mixers(L):
                norm(3 * L)
                projections(L)
                delta(L)

                def turned_output(c):
                    opened(("OT", L, c))
                    pe.wait_ge(s_o, 3 * L + (1, 2, 2, 3)[c])
                    for q in range(4):
                        k, b = OUT_CHUNKS[2 * c + q // 2], q % 2
                        ins = pe.transpose(bank(("OT", L, c), P * q, P), o[:, b, P * k:P * k + P], ident)
                    ins.then_inc(s_fill, 1)

                turned_output(0)
                for half in range(2):
                    ready(pe, ("WO", L, 0, half))
                    for q in range(4):
                        k = 4 * half + q
                        if k == 2:
                            turned_output(1)
                            turned_output(2)
                        elif k == 4:
                            turned_output(3)
                        chunk_ready(("OT", L), k)
                        for b in range(NB):
                            if k == 0:
                                opened(("WO", L, b, 0))
                            ins = product(bank(("WO", L, b, 0)), x_part(T * k + P * b, P),
                                          weights(("WO", L, 0, half), 512 * q, 512), k == 0, k == KC - 1)
                            if k == KC - 1:
                                ins.then_inc(s_fill, 1)
                    if half == 0:
                        ins.then_inc(s_used, 1)
                both_blocks([("WO", L, b, 1) for b in range(NB)], ("WO", L, 1), 512)

            def ple(L, items=None):
                ready(pe, ("PP", L), items)
                for m in range(2):
                    for b in range(NB):
                        key = ("PP", L, b, m)
                        opened(key, items)
                        for k in range(PLE // P):
                            ins = product(bank(key), weights(("PT", L), T * k + P * b, P),
                                          weights(("PP", L), D * k + 512 * m, 512), k == 0, k == 1)
                        ins.then_inc(s_fill, 1)
                norm(3 * L + 2, items)
                for m in range(2):
                    both_blocks([("PG", L, b, m) for b in range(NB)], ("PG", L, m), 512, items,
                                None if m else ("T", 3 * L + 2))

            pe.wait_ge(s_small, 48)
            mixers(0)
            norm(1)

            def dense_down(f):
                pe.wait_ge(s_ffg, f + 1)
                ready(pe, ("w2", f // 2))
                for m in range(2):
                    for b in range(NB):
                        if f == 0:
                            opened(("Y2", b, m))
                        ins = product(bank(("Y2", b, m)), (gh[:, f % 2, P * b:P * b + P], gl[:, f % 2, P * b:P * b + P]),
                                      weights(("w2", f // 2), D * (f % 2) + 512 * m, 512), f == 0, f == NF - 1)
                        if f == NF - 1:
                            ins.then_inc(s_fill, 1)
                if f % 2 and f < NF - 1:
                    ins.then_inc(s_used, 1)

            for f in range(NF):
                opened(("H", f))
                ready(pe, ("w13", f))
                for side in range(2):
                    for k in range(KC):
                        chunk_ready(None if f or side else ("T", 1), k)
                        ins = product(bank(("H", f), T * side, T), weights(("w13", f), P * (KC * side + k), P),
                                      x_part(T * k, T), k == 0, k == KC - 1)
                ins.then_inc(s_fill, 1)
                if f >= 1:
                    dense_down(f - 1)
            dense_down(NF - 1)
            ple(0)
            mixers(1)
            norm(4)
            drained(pe, ("T", 4, 3), "v")
            opened(("LG",))
            pe.wait_ge(s_router, 2)
            for k in range(KC):
                at = slice(NE * k, NE * k + NE)
                ins = product(bank(("LG",), 0, T)[0:NE], (rh[:, at], rl[:, at]), x_part(T * k, T), k == 0, k == KC - 1)
            ins.then_inc(s_fill, 1)
            opened(("LT",))
            drained(pe, ("LG",), "a")
            for b in range(NB):
                ins = pe.transpose(bank(("LT",), NE * b, NE), logits[:, P * b:P * b + P], ident[0:NE, 0:NE])
            ins.then_inc(s_fill, 1)
            opened(("POS",))
            pe.wait_ge(s_sel, 1)
            pe.matmul(bank(("POS",), 0, NE), cc("upto"), sel[:, 0, :], start=True, stop=True)
            for start in (NE, 2 * NE):
                pe.matmul(bank(("POS",), start, NE), ones, sel[:, 0, :], start=True, stop=False)
                ins = pe.matmul(bank(("POS",), start, NE), cc("upto") if start == NE else ones, sel[:, 1, :], start=False,
                                stop=True)
            ins.then_inc(s_fill, 1)

            def gather(when, it, number):
                pe.wait_ge(s_pick, number)
                for half in range(2):
                    key = ("GA", when, half)
                    opened(key, it)
                    for q in range(4):
                        k = 4 * half + q
                        for b in range(NB):
                            ins = pe.matmul(bank(key, P * q, P), hn[:, b, P * k:P * k + P], pick[:, b, :], start=(b == 0),
                                            stop=(b == NB - 1))
                    ins.then_inc(s_fill, 1)

            def scatter_matrix(when, it):
                opened(("GT", when), it)
                for b in range(NB):
                    ins = pe.transpose(bank(("GT", when), P * b, P), pickg[:, b, :], ident)
                ins.then_inc(s_fill, 1)

            def up(kind, ph, j, it):
                key = (kind, ph, j)
                opened(key, it)
                for half in range(2):
                    ready(pe, key + (half,), it)
                    for q in range(4):
                        k = 4 * half + q
                        ins = product(bank(key), x_part(P * k, P), weights(key + (half,), 512 * q, 512), k == 0, k == KC - 1)
                    ins.then_inc(s_fill if half else s_used, 1)

            def turn(ph, j, it):
                opened(("TT", ph, j), it)
                for q in range(4):
                    ins = pe.transpose(bank(("TT", ph, j), P * q, P), mg[j % 2][:, P * q:P * q + P], ident)
                ins.then_inc(s_fill, 1)

            def down(ph, j, it):
                drained(pe, ("TT", ph, j), "v", it)
                if j == 0:
                    opened(("YY", ph, 0), it)
                    opened(("YY", ph, 1), it)
                for half in range(2):
                    ready(pe, ("C", ph, j, half), it)
                    for m in range(2):
                        for q in range(2):
                            c = 2 * half + q
                            ins = product(bank(("YY", ph, m)), (mTh[j % 2][:, P * c:P * c + P], mTl[j % 2][:, P * c:P * c + P]),
                                          weights(("C", ph, j, half), D * q + 512 * m, 512), j == 0 and c == 0,
                                          j == NJ - 1 and c == 3)
                        if j == NJ - 1 and half:
                            ins.then_inc(s_fill, 1)
                    if j < NJ - 1 or half == 0:
                        ins.then_inc(s_used, 1)

            def rest_of_item(ph, it):
                for j in range(1, NJ):
                    up("A", ph, j, it)
                    if j == 1:
                        drained(pe, ("B", "each", 0), "v", it, 1)
                    else:
                        drained(pe, ("B", ph, j - 1), "v", it)
                    turn(ph, j - 1, it)
                    if j == NJ - 1 and ph == "each":
                        gather(ph, it, it + 2)
                    up("B", ph, j, it)
                    down(ph, j - 1, it)
                drained(pe, ("B", ph, NJ - 1), "v", it)
                turn(ph, NJ - 1, it)
                if ph == "each":
                    drained(pe, ("GA", ph, 1), "v", it)
                    up("A", ph, 0, it)
                down(ph, NJ - 1, it)
                if ph == "each":
                    up("B", ph, 0, it)
                drained(pe, ("GT", "each"), "a", it, 1)
                for m in range(2):
                    drained(pe, ("YY", ph, m), "a", it)
                    for b in range(NB):
                        opened(("SC", ph, b, m), it)
                        pe.matmul(bank(("SC", ph, b, m)), back[:, P * b:P * b + P], ysb[:, 512 * m:512 * m + 512], start=True,
                                  stop=True).then_inc(s_fill, 1)
                if ph == "each":
                    scatter_matrix(ph, it)

            gather("first", None, 1)
            drained(pe, ("GA", "first", 1), "v")
            up("A", "first", 0, None)
            scatter_matrix("first", None)
            up("B", "first", 0, None)
            for who in "va":
                pe.wait_ge(s_free[who], tiles.base[who])
            pe.wait_ge(s_tab, 1)
            items = pe.value_load(table[0:1, MORE + 3:MORE + 4], min_val=NE - 1, max_val=NE - 1 + MORE)
            with pe.Fori(0, items) as i:
                rest_of_item("each", i)
            rest_of_item("last", items)
            ple(1, items)


def chunks_of(w):
    k, c = w.shape
    return w.reshape(k // P, P, c // P, P).transpose(1, 2, 0, 3)


def slot(*parts):
    flat = np.concatenate([a.reshape(P, -1) for a in parts], 1)
    out = np.zeros((P, SLOT), np.float32)
    out[:, :flat.shape[1]] = flat
    return out


def k_major(w):
    return w.reshape(-1, P, w.shape[1]).transpose(1, 0, 2)


def kernel(**inputs):
    import concourse.bacc as bacc
    from concourse.bass_utils import run_bass_kernel_spmd

    a = {k: np.asarray(v) for k, v in inputs.items()}
    plan = plan_loads(plan_tiles()[0])
    per_load = len(plan["each"])
    w_in = a["w_in"]
    q0, z0, dq0 = 0, 3 * DG, 4 * DG + 2 * HG
    dv0 = dq0 + 2 * DW
    sq0 = dv0 + DW
    sv0 = sq0 + 2 * DS

    def load(key):
        kind = key[0]
        if kind == "J":
            L, g, half = key[1:]
            lo, hi = ((z0, dq0), (dv0, sq0), (sv0, sv0 + DS))[g]
            return slot(k_major(w_in[L][:, lo:hi])[:, 4 * half:4 * half + 4])
        if kind == "I":
            L, c = key[1:]
            every = np.concatenate([w_in[L][:, q0:z0], w_in[L][:, dq0:dv0], w_in[L][:, sq0:sv0]], 1)
            return slot(chunks_of(every[:, 2 * P * c:2 * P * c + 2 * P]))
        if kind in ("WO", "PG"):
            L, m, half = key[1:]
            w = k_major(a["w_out" if kind == "WO" else "ple_gate"][L][:, 512 * m:512 * m + 512])
            if kind == "WO":
                w = w[:, list(OUT_CHUNKS)]
            return slot(w[:, 4 * half:4 * half + 4])
        if kind == "w13":
            at = slice(P * key[1], P * key[1] + P)
            return slot(chunks_of(a["ffn_w1"][0][:, at]), chunks_of(a["ffn_w3"][0][:, at]))
        if kind == "w2":
            return slot(k_major(a["ffn_w2"][0][2 * P * key[1]:2 * P * key[1] + 2 * P]))
        if kind == "PP":
            return slot(k_major(a["ple_proj"][key[1]]))
        return slot(k_major(np.ascontiguousarray(a["p"][key[1], 0].T)))

    stream = np.stack([load(key) for key in plan["before"][:-FIRST] + plan["after"][plan["last"]:]])
    experts = np.empty((NE, per_load, P, SLOT), np.float32)
    for key in plan["each"]:
        n, (kind, _, j, half) = expert_place(key), key
        if kind == "C":
            w = a["moe_w2"][0][:, 512 * j + T * half:512 * j + T * half + T]
            experts[:, n] = w.reshape(NE, 2, P, D).transpose(0, 2, 1, 3).reshape(NE, P, SLOT)
        else:
            w = a["moe_w1" if kind == "A" else "moe_w3"][0][:, 512 * half:512 * half + 512, 512 * j:512 * j + 512]
            experts[:, n] = w.reshape(NE, 4, P, 512).transpose(0, 2, 1, 3).reshape(NE, P, SLOT)
    norms = np.stack([a["attn_norm_w"], a["ffn_norm_w"], a["ple_norm_w"]], 1)
    columns = np.concatenate([
        norms.reshape(-1, P).T,
        a["conv_w"].reshape(DEPTH, CONV, CQ, P).transpose(3, 0, 2, 1).reshape(P, -1),
        k_major(a["router_w"][0]).reshape(P, -1)], 1)
    heads = np.stack([a["gdn_norm_w"], a["dsw_norm_w"], a["sb_norm_w"]], 1)
    rows = np.concatenate([a["a_log"].ravel(), a["dt_bias"].ravel(), heads.ravel()])

    given = dict(x=a["x"][0], stream=stream, experts=experts.reshape(NE * per_load, P, SLOT), columns=columns,
                 rows=np.broadcast_to(rows, (P, NROW)), final_w=np.broadcast_to(a["final_norm_w"], (P, D)),
                 consts=shape_constants())
    nc = bacc.Bacc("TRN2", target_bir_lowering=False, num_devices=1)
    arrays, args = {}, {}
    for name, v in given.items():
        v = np.ascontiguousarray(v)
        arrays[f"in_{name}"] = v
        args[name] = nc.dram_tensor(f"in_{name}", v.shape, mybir.dt.from_np(v.dtype), kind="ExternalInput").ap()
    out = nc.dram_tensor("out", (T, D), F32, kind="ExternalOutput").ap()
    build(nc, out=out, **args)
    r = run_bass_kernel_spmd(nc, [arrays], core_ids=[0])
    return r.results[0]["out"].reshape(1, T, D)
```
